# Optimizing a Trainium2 kernel written in Bass

```python
import math
import jax, jax.numpy as jnp
from jax import lax
import numpy as np

D_MODEL = 2048
BATCH = 1
SEQ = 512
DEPTH = 1
DEC_BATCH = 8
DEC_SEQ = 8
PAST_LEN = 4096
PAGE_SIZE = 128

HEAD_DIM = 128
N_Q_HEADS = 8
N_KV_HEADS = 2
ATTN_W = N_Q_HEADS * HEAD_DIM
KV_W = N_KV_HEADS * HEAD_DIM
LRU_W = D_MODEL // 2
N_LRU_BLOCKS = 8
LRU_BLOCK = LRU_W // N_LRU_BLOCKS
CONV_W = 4
LRU_C = 8.0
MIX_W = ATTN_W + LRU_W
IN_W = ATTN_W + 2 * KV_W + 2 * LRU_W
D_FF = 4 * D_MODEL
WINDOW = 128
ATTN_BLOCK = WINDOW
N_BUCKETS = 32
MAX_DISTANCE = 128
N_META = 16
EPS = 1e-6

kernel_name = "hymba_griffin_swa_sink_hybrid_step"

def rmsnorm(x, g):
    xf = x.astype(jnp.float32)
    y = xf * lax.rsqrt(jnp.mean(xf * xf, axis=-1, keepdims=True) + EPS)
    return (y * g.astype(jnp.float32)).astype(x.dtype)

def rel_bucket(dist):
    n = jnp.maximum(dist, 0)
    max_exact = N_BUCKETS // 2
    nf = jnp.maximum(n, 1).astype(jnp.float32)
    large = max_exact + (jnp.log(nf / max_exact) / math.log(MAX_DISTANCE / max_exact)
                         * (N_BUCKETS - max_exact)).astype(jnp.int32)
    large = jnp.minimum(large, N_BUCKETS - 1)
    return jnp.where(n < max_exact, n, large)

def sink_attention(q, k, v, q_pos, k_pos, k_valid, sinks, rel_bias):
    B, N, Q, H, D = q.shape
    S = k.shape[2]
    G = H // N_KV_HEADS
    qf = q.astype(jnp.float32).reshape(B, N, Q, N_KV_HEADS, G, D)
    s = jnp.einsum('bnqkgd,bnskd->bnkgqs', qf, k.astype(jnp.float32)) * (D ** -0.5)
    dist = q_pos[:, :, None] - k_pos[:, None, :]
    mask = k_valid[:, None, :] & (dist >= 0) & (dist < WINDOW)
    bias = rel_bias.astype(jnp.float32)[rel_bucket(dist)]
    bias = jnp.transpose(bias, (0, 3, 1, 2)).reshape(N, N_KV_HEADS, G, Q, S)
    s = jnp.where(mask[:, None, None], s + bias[None], -jnp.inf)
    sink = sinks.astype(jnp.float32).reshape(1, 1, N_KV_HEADS, G, 1, 1)
    m = jnp.maximum(jnp.max(s, axis=-1, keepdims=True), sink)
    p = jnp.exp(s - m)
    denom = jnp.sum(p, axis=-1, keepdims=True) + jnp.exp(sink - m)
    o = jnp.einsum('bnkgqs,bnskd->bnqkgd', p / denom, v.astype(jnp.float32))
    return o.reshape(B, N, Q, H, D).astype(q.dtype)

def prompt_window_attention(q, k, v, sinks, rel_bias):
    B, T = q.shape[:2]
    p0 = (-N_META) % ATTN_BLOCK
    nb = -(-(p0 + T) // ATTN_BLOCK)
    p1 = nb * ATTN_BLOCK - p0 - T
    qb = jnp.pad(q, ((0, 0), (p0, p1), (0, 0), (0, 0))).reshape(B, nb, ATTN_BLOCK, N_Q_HEADS, HEAD_DIM)

    def key_blocks(t):
        tp = jnp.pad(t, ((0, 0), (p0 + ATTN_BLOCK, p1), (0, 0), (0, 0)))
        prev = tp[:, :nb * ATTN_BLOCK].reshape(B, nb, ATTN_BLOCK, N_KV_HEADS, HEAD_DIM)
        cur = tp[:, ATTN_BLOCK:].reshape(B, nb, ATTN_BLOCK, N_KV_HEADS, HEAD_DIM)
        return jnp.concatenate([prev, cur], axis=2)

    start = jnp.arange(nb, dtype=jnp.int32)[:, None] * ATTN_BLOCK - p0
    q_pos = start + jnp.arange(ATTN_BLOCK, dtype=jnp.int32)[None]
    k_pos = start - ATTN_BLOCK + jnp.arange(2 * ATTN_BLOCK, dtype=jnp.int32)[None]
    k_valid = (k_pos >= 0) & (k_pos < T)
    o = sink_attention(qb, key_blocks(k), key_blocks(v), q_pos, k_pos, k_valid, sinks, rel_bias)
    return o.reshape(B, nb * ATTN_BLOCK, N_Q_HEADS, HEAD_DIM)[:, p0:p0 + T]

def causal_conv(x, prev, w, b):
    T = x.shape[1]
    xp = jnp.concatenate([prev.astype(x.dtype), x], axis=1)
    out = b.astype(x.dtype) + xp[:, 0:T] * w[0].astype(x.dtype)
    for j in range(1, CONV_W):
        out = out + xp[:, j:j + T] * w[j].astype(x.dtype)
    return out, xp[:, -(CONV_W - 1):]

def rg_lru(x, pos, h0, w_a, b_a, w_x, b_x, lam):
    B, T, _ = x.shape
    xf = x.astype(jnp.float32)
    xb = xf.reshape(B, T, N_LRU_BLOCKS, LRU_BLOCK)
    gate_a = jax.nn.sigmoid(jnp.einsum('btnc,ncd->btnd', xb, w_a.astype(jnp.float32)).reshape(B, T, LRU_W)
                            + b_a.astype(jnp.float32))
    gate_x = jax.nn.sigmoid(jnp.einsum('btnc,ncd->btnd', xb, w_x.astype(jnp.float32)).reshape(B, T, LRU_W)
                            + b_x.astype(jnp.float32))
    log_a = -LRU_C * gate_a * jax.nn.softplus(-lam.astype(jnp.float32))
    a = jnp.exp(log_a)
    mult = jnp.sqrt(-jnp.expm1(2.0 * log_a))
    mult = jnp.where((pos == 0)[None, :, None], 1.0, mult)
    bterm = xf * gate_x * mult
    bterm = bterm.at[:, 0].add(a[:, 0] * h0.astype(jnp.float32))

    def combine(l, r):
        return (l[0] * r[0], r[0] * l[1] + r[1])

    _, h = lax.associative_scan(combine, (a, bterm), axis=1)
    return h, h[:, -1]

def setup_inputs(seed: int = 0) -> dict:
    key = jax.random.key(seed)
    ks = jax.random.split(key, 32)
    f32 = jnp.float32

    def nrm(k, shape, scale):
        return jax.random.normal(k, shape, f32) * scale

    kv_buf = min(WINDOW, PAST_LEN)
    u = jax.random.uniform(ks[15], (DEPTH, LRU_W), f32, 0.9, 0.999)
    a0 = u ** (1.0 / LRU_C)
    lru_lambda = jnp.log(a0) - jnp.log1p(-a0)
    return {
        "x_prompt": nrm(ks[0], (BATCH, SEQ, D_MODEL), 1.0),
        "x_sample": nrm(ks[1], (DEC_BATCH, DEC_SEQ, D_MODEL), 1.0),
        "cache_k_win": nrm(ks[2], (DEPTH, DEC_BATCH, kv_buf, N_KV_HEADS, HEAD_DIM), 1.0),
        "cache_v_win": nrm(ks[3], (DEPTH, DEC_BATCH, kv_buf, N_KV_HEADS, HEAD_DIM), 1.0),
        "state_conv": nrm(ks[4], (DEPTH, DEC_BATCH, CONV_W - 1, LRU_W), 1.0),
        "state_lru": nrm(ks[5], (DEPTH, DEC_BATCH, LRU_W), 0.5),
        "meta_tokens": nrm(ks[6], (N_META, D_MODEL), 1.0),
        "norm_mix_g": 1.0 + nrm(ks[7], (DEPTH, D_MODEL), 0.02),
        "w_in": nrm(ks[8], (DEPTH, D_MODEL, IN_W), D_MODEL ** -0.5),
        "conv_w": nrm(ks[9], (DEPTH, CONV_W, LRU_W), CONV_W ** -0.5),
        "conv_b": nrm(ks[10], (DEPTH, LRU_W), 0.01),
        "w_gate_a": nrm(ks[11], (DEPTH, N_LRU_BLOCKS, LRU_BLOCK, LRU_BLOCK), LRU_BLOCK ** -0.5),
        "b_gate_a": nrm(ks[12], (DEPTH, LRU_W), 0.01),
        "w_gate_x": nrm(ks[13], (DEPTH, N_LRU_BLOCKS, LRU_BLOCK, LRU_BLOCK), LRU_BLOCK ** -0.5),
        "b_gate_x": nrm(ks[14], (DEPTH, LRU_W), 0.01),
        "lru_lambda": lru_lambda,
        "attn_sinks": nrm(ks[16], (DEPTH, N_Q_HEADS), 1.0),
        "rel_bias": nrm(ks[17], (N_BUCKETS, N_Q_HEADS), 0.5),
        "attn_out_g": 1.0 + nrm(ks[18], (DEPTH, ATTN_W), 0.02),
        "rec_out_g": 1.0 + nrm(ks[19], (DEPTH, LRU_W), 0.02),
        "w_out": nrm(ks[20], (DEPTH, MIX_W, D_MODEL), MIX_W ** -0.5),
        "norm_mlp_g": 1.0 + nrm(ks[21], (DEPTH, D_MODEL), 0.02),
        "w_up": nrm(ks[22], (DEPTH, D_MODEL, D_FF), D_MODEL ** -0.5),
        "w_down": nrm(ks[23], (DEPTH, D_FF, D_MODEL), D_FF ** -0.5),
        "final_norm_g": 1.0 + nrm(ks[24], (D_MODEL,), 0.02),
    }

def reference(x_prompt, x_sample, cache_k_win, cache_v_win, state_conv, state_lru,
              meta_tokens, norm_mix_g, w_in, conv_w, conv_b, w_gate_a, b_gate_a, w_gate_x, b_gate_x,
              lru_lambda, attn_sinks, rel_bias, attn_out_g, rec_out_g, w_out, norm_mlp_g, w_up, w_down,
              final_norm_g):
    split_at = [ATTN_W, ATTN_W + KV_W, ATTN_W + 2 * KV_W, ATTN_W + 2 * KV_W + LRU_W]

    def layer(h, l, pos, attend, conv_prev, lru_prev):
        B, T = h.shape[:2]
        u = rmsnorm(h, norm_mix_g[l])
        z = u @ w_in[l]
        q, k, v, xr, gr = jnp.split(z, split_at, axis=-1)
        q = q.reshape(B, T, N_Q_HEADS, HEAD_DIM)
        k = k.reshape(B, T, N_KV_HEADS, HEAD_DIM)
        v = v.reshape(B, T, N_KV_HEADS, HEAD_DIM)
        attn, k_buf, v_buf = attend(q, k, v, l)
        xc, conv_new = causal_conv(xr, conv_prev, conv_w[l], conv_b[l])
        hr, lru_new = rg_lru(xc, pos, lru_prev, w_gate_a[l], b_gate_a[l], w_gate_x[l], b_gate_x[l],
                             lru_lambda[l])
        rec = (hr * jax.nn.gelu(gr.astype(jnp.float32))).astype(h.dtype)
        mixed = jnp.concatenate([rmsnorm(attn.reshape(B, T, ATTN_W), attn_out_g[l]),
                                 rmsnorm(rec, rec_out_g[l])], axis=-1)
        h = h + mixed @ w_out[l]
        hid = jnp.square(jax.nn.relu(rmsnorm(h, norm_mlp_g[l]) @ w_up[l]))
        h = h + hid @ w_down[l]
        return h, k_buf, v_buf, conv_new, lru_new.astype(h.dtype)

    def attend_prompt(q, k, v, l):
        o = prompt_window_attention(q, k, v, attn_sinks[l], rel_bias)
        return o, k[:, -WINDOW:], v[:, -WINDOW:]

    def attend_sample(q, k, v, l):
        kk = jnp.concatenate([cache_k_win[l].astype(k.dtype), k], axis=1)
        vv = jnp.concatenate([cache_v_win[l].astype(v.dtype), v], axis=1)
        buf = cache_k_win.shape[2]
        T = q.shape[1]
        q_pos = (PAST_LEN + jnp.arange(T, dtype=jnp.int32))[None]
        k_pos = (PAST_LEN - buf + jnp.arange(buf + T, dtype=jnp.int32))[None]
        o = sink_attention(q[:, None], kk[:, None], vv[:, None], q_pos, k_pos, k_pos >= 0,
                           attn_sinks[l], rel_bias)
        return o[:, 0], kk[:, -buf:], vv[:, -buf:]

    meta = jnp.broadcast_to(meta_tokens.astype(x_prompt.dtype)[None], (x_prompt.shape[0], N_META, D_MODEL))
    hp = jnp.concatenate([meta, x_prompt], axis=1)
    Bp, Tp = hp.shape[:2]
    pos_p = jnp.arange(Tp, dtype=jnp.int32)
    conv0 = jnp.zeros((Bp, CONV_W - 1, LRU_W), hp.dtype)
    lru0 = jnp.zeros((Bp, LRU_W), jnp.float32)

    hs = x_sample
    pos_s = PAST_LEN + jnp.arange(x_sample.shape[1], dtype=jnp.int32)

    kp_l, vp_l, cp_l, lp_l = [], [], [], []
    ks_l, vs_l, cs_l, ls_l = [], [], [], []
    for l in range(DEPTH):
        hp, kb, vb, cb, lb = layer(hp, l, pos_p, attend_prompt, conv0, lru0)
        kp_l.append(kb); vp_l.append(vb); cp_l.append(cb); lp_l.append(lb)
        hs, kb, vb, cb, lb = layer(hs, l, pos_s, attend_sample, state_conv[l], state_lru[l])
        ks_l.append(kb); vs_l.append(vb); cs_l.append(cb); ls_l.append(lb)

    y_prompt = rmsnorm(hp, final_norm_g)[:, N_META:]
    y_sample = rmsnorm(hs, final_norm_g)
    return (y_prompt, y_sample,
            jnp.stack(kp_l), jnp.stack(vp_l), jnp.stack(cp_l), jnp.stack(lp_l),
            jnp.stack(ks_l), jnp.stack(vs_l), jnp.stack(cs_l), jnp.stack(ls_l))


_drawn_inputs = setup_inputs


def setup_inputs(seed=0):
    import zlib

    import numpy as np

    out = dict(_drawn_inputs(seed))
    spreads = {}
    factors = {'b_gate_a': 24.069,
     'b_gate_x': 8.0,
     'attn_sinks': 8.0,
     'attn_out_g': 72.186,
     'rec_out_g': 68.452,
     'norm_mlp_g': 13.315,
     'final_norm_g': 22.616}
    for name, (base, spread) in spreads.items():
        noise = np.random.default_rng([zlib.crc32(name.encode()), seed]).standard_normal(out[name].shape)
        drawn = base * np.exp(spread * noise) if base else spread * noise
        out[name] = __import__('jax').numpy.asarray(drawn.astype(out[name].dtype))
    for name, factor in factors.items():
        out[name] = (out[name] * factor).astype(out[name].dtype)
    return out
```

```python
from contextlib import ExitStack

import numpy as np

import concourse.bass as bass
from concourse import mybir

F32 = mybir.dt.float32
F32R = mybir.dt.float32r
ALU = mybir.AluOpType
ACT = mybir.ActivationFunctionType
AX = mybir.AxisListType

P = 128
D_MODEL = 2048
SEQ = 512
META = 16
DEC_B = 8
DEC_T = 8
HEADS = 8
KV = 2
GQ = HEADS // KV
WINDOW = 128
LRU_W = 1024
NB = LRU_W // P
CONV_W = 4
HIST = CONV_W - 1
D_FF = 4 * D_MODEL
BUCKETS = 32
EPS = 1e-6

TP = META + SEQ
TS = DEC_B * DEC_T
T = TP + TS
HALF = T // 2
KT = D_MODEL // P
BANK = 512

SEQ_S = HIST + DEC_T
CONV_IN = HIST + TP + DEC_B * SEQ_S
LT = CONV_IN - HIST
LH = LT // 2
S0 = TP + HIST

SLAB_K = 8
SLAB = SLAB_K * P
RING = 4
RAW = 2
SLABS_REC = 2 * NB * 2
SLABS_QKV = (HEADS + 2 * KV) * 2
SLABS_IN = SLABS_REC + SLABS_QKV
SLABS_OUT = KT * 2
FC = 8
CHUNKS = D_FF // P // FC
SLABS_CHUNK = FC * 2 + KT
S_OUT = SLABS_IN
S_MLP = SLABS_IN + SLABS_OUT
SLABS = S_MLP + CHUNKS * SLABS_CHUNK
G_OUT = 2 * NB + HEADS + 2 * KV
G_MLP = G_OUT + KT
G_CHUNK = FC + KT

SCALE = 128 ** -0.5
MASKED = -1e30
GY = 384
GELU_C = float(np.sqrt(2.0 / np.pi))
GELU_K = 0.044715 ** 0.5

_COLS = [("g_mix", KT), ("conv_w", CONV_W * NB), ("conv_b", NB), ("b_a", NB), ("b_x", NB), ("lam", NB),
         ("g_att", HEADS), ("g_rec", NB), ("g_mlp", KT), ("g_fin", KT), ("sink_p", HEADS), ("sink_s", KV),
         ("h0", NB * DEC_B * HIST), ("hist", (NB + 1) * DEC_B * HIST)]
COL = {}
_at = 0
for _n, _w in _COLS:
    COL[_n] = (_at, _w)
    _at += _w
NPAR = _at

UNITS = [("prompt", i, g) for i in range(5) for g in range(KV)] + [("sample", i, g) for i in range(2) for g in range(KV)]
NU = len(UNITS)


class Steps:

    def __init__(self, eng, sem):
        self.eng, self.sem, self.base, self.k = eng, sem, 0, 0

    def loop(self, base):
        self.base, self.k = base, 0

    def __call__(self, ins):
        self.k += 1
        ins.then_inc(self.sem, 1)
        self.eng.wait_ge(self.sem, self.base + self.k)


def hymba_layer(nc, weights, x_t, params, consts, rel_bias, onehot, gy_mask, w_gates, cache_kt, cache_v,
                cache_k_rows, cache_v_rows, y_t, kv_t, conv_o, lru_o, keep_k, keep_v):
    ctx = ExitStack()
    gy_dram = nc.dram_tensor("gy_dram", [HEADS, P, GY], F32, kind="Internal")

    base = (nc.sbuf_base + 31) // 32 * 32
    TILE = T * 4
    top = [base]

    def region(size):
        at = top[0]
        top[0] = at + (size + 31) // 32 * 32
        return at

    def sb(name, shape, dt, offset):
        return nc.alloc_sbuf_tensor_at(name, [P] + shape, dt, offset=offset)

    def small(name, shape, dt=F32):
        return sb(name, shape, dt, region(4 * int(np.prod(shape))))

    reg_a = region(2 * KT * TILE)
    reg_x = region(KT * TILE)
    reg_h = region(KT * TILE)
    act_hi = sb("act_hi", [KT, T], F32R, reg_a)
    act_lo = sb("act_lo", [KT, T], F32R, reg_a + KT * TILE)
    w_raw = small("w_raw", [RAW, SLAB])
    w_hi = small("w_hi", [RING, SLAB_K, P], F32R)
    w_lo = small("w_lo", [RING, SLAB_K, P], F32R)
    par = small("par", [NPAR])
    con = small("con", [2, P])
    gate_w = small("gate_w", [2, P])
    rb = small("rb", [T])
    acc = small("acc", [T])
    sq = small("sq", [2, T])
    conv_out = small("conv_out", [NB, 9, HIST])
    lru_out = small("lru_out", [NB, 1 + DEC_B])
    sp2 = small("sp2", [NB])
    spt = small("spt", [4, NB])
    half_b = small("half_b", [2, NB])
    eps_t = small("eps_t", [1])
    mlp_a = small("mlp_a", [T])
    mlp_b = small("mlp_b", [T])
    rn = mlp_a
    stat = small("stat", [2, 6, GQ])
    assert top[0] <= nc.sbuf_usable_end, top[0] - nc.sbuf_usable_end
    ident, ones = con[:, 0, :], con[:, 1, :]

    x_raw = sb("x_raw", [KT, T], F32, reg_x)
    h_res = sb("h_res", [KT, T], F32, reg_x)
    xp = sb("xp", [CONV_IN], F32, reg_x)
    LB = (CONV_IN * 4 + 31) // 32 * 32
    xc = sb("xc", [LT], F32, reg_x + LB)
    t_a = sb("t_a", [LT], F32, reg_x + 2 * LB)
    t_x = sb("t_x", [LT], F32, reg_x + 3 * LB)
    t_r = sb("t_r", [LT], F32, reg_x + 4 * LB)
    t_s = sb("t_s", [LT], F32, reg_x + 5 * LB)
    gel = sb("gel", [T], F32, reg_x + 6 * LB)
    gel_t = sb("gel_t", [T], F32, reg_x + 7 * LB)
    hs = sb("hs", [LT], F32, reg_x + 8 * LB)
    kv = sb("kv", [2 * KV, T], F32, reg_x + 9 * LB)
    at = reg_x
    v_tok = sb("v_tok", [6, KV, P], F32, at)
    bias_s = sb("bias_s", [2, KV, P + TS], F32, at + 6144)
    q_s = sb("q_s", [KV, 2 * P], F32, at + 6144 + 3072)
    bias_p = sb("bias_p", [HEADS, 2 * P], F32, at + 6144 + 3072 + 2048)
    assert 6144 + 3072 + 2048 + 8192 <= 9 * LB and 9 * LB + 4 * TILE <= KT * TILE
    rec = sb("rec", [NB, T], F32, reg_h)
    q = sb("q", [HEADS, T], F32, reg_h + NB * TILE)
    ck = sb("ck", [DEC_B, KV, P], F32, reg_a)
    cv = sb("cv", [DEC_B, KV, P], F32, reg_a + 8192)
    probs = sb("probs", [2, GQ, 2 * P], F32, reg_a + KT * TILE)
    probs_t = sb("probs_t", [2, 2, GQ, P], F32, reg_a + KT * TILE + 8192)
    assert 16384 <= 8 * TILE
    hid_hi = sb("hid_hi", [FC, T], F32R, reg_h)
    hid_lo = sb("hid_lo", [FC, T], F32R, reg_h + FC * TILE)
    oneh = sb("oneh", [GY], F32, reg_h + NB * TILE)
    relb = sb("relb", [HEADS], F32, reg_h + NB * TILE + 4 * GY)
    gym = sb("gym", [GY], F32, reg_h + NB * TILE + 4 * GY + 32)
    gy = sb("gy", [GY], F32, reg_h + NB * TILE + 8 * GY + 32)

    ps = ctx.enter_context(nc.psum_tensor("ps", [P, 8, BANK], F32))

    def sem(name):
        return ctx.enter_context(nc.semaphore(name))

    raw_landed = [sem(f"raw_landed{i}") for i in range(RAW)]
    x_landed = [sem(f"x_landed{i}") for i in range(8)]
    h_landed = [sem(f"h_landed{i}") for i in range(4)]
    par_landed = sem("par_landed")
    con_landed = sem("con_landed")
    rel_landed = sem("rel_landed")
    gate_landed = sem("gate_landed")
    cache_landed = sem("cache_landed")
    gy_stored = sem("gy_stored")
    bias_landed = sem("bias_landed")
    hi_ready = sem("hi_ready")
    lo_ready = sem("lo_ready")
    slab_used = sem("slab_used")
    group_out = sem("group_out")
    xhi_ready = sem("xhi_ready")
    xlo_ready = sem("xlo_ready")
    x_squared = sem("x_squared")
    x_added = sem("x_added")
    sums_ready = sem("sums_ready")
    root_ready = sem("root_ready")
    rb_ready = sem("rb_ready")
    gy_ps_ready = sem("gy_ps_ready")
    gy_ready = sem("gy_ready")
    sp_exp = sem("sp_exp")
    sp_ready = sem("sp_ready")
    hist_ready = sem("hist_ready")
    pads_ready = sem("pads_ready")
    tap0_ready = sem("tap0_ready")
    conv_ready = sem("conv_ready")
    xr_kept = sem("xr_kept")
    gates_ready = sem("gates_ready")
    g_squared = sem("g_squared")
    g_poly = sem("g_poly")
    g_tanh = sem("g_tanh")
    tanh_a = sem("tanh_a")
    tanh_x = sem("tanh_x")
    tau_ready = sem("tau_ready")
    sqrt_ready = sem("sqrt_ready")
    rec_ready = sem("rec_ready")
    rec_squared = sem("rec_squared")
    rec_added = sem("rec_added")
    rec_scaled = sem("rec_scaled")
    vt_ready = sem("vt_ready")
    v_copied = sem("v_copied")
    qs_ready = sem("qs_ready")
    s_ready = sem("s_ready")
    negmax_ready = sem("negmax_ready")
    exp_ready = sem("exp_ready")
    probs_ready = sem("probs_ready")
    pt_ready = sem("pt_ready")
    pt_copied = sem("pt_copied")
    o_ready = sem("o_ready")
    o_copied = sem("o_copied")
    o_added = sem("o_added")
    att_scaled = sem("att_scaled")
    h_squared = sem("h_squared")
    h_added = sem("h_added")
    square_ready = sem("square_ready")
    hid_split = sem("hid_split")
    hid_ready = sem("hid_ready")
    y_ready = sem("y_ready")
    stored = sem("stored")
    dve_step = sem("dve_step")
    act_step = sem("act_step")
    pool_step = sem("pool_step")

    def col(name, i=0, n=1):
        a = COL[name][0]
        return par[:, a + i:a + i + n]

    def dcol(name, i):
        return par[:, bass.ds(i + COL[name][0], 1)]

    def acc_pair(b):
        return ps[:, 2 * b:2 * b + 2, 0:HALF]

    def sample(buf, at):
        return buf[:, at:at + DEC_B * SEQ_S].rearrange("p (b t) -> p b t", b=DEC_B)

    rec_f = rec[:, :, :].rearrange("p k t -> p (k t)")
    kv_f = kv[:, :, :].rearrange("p k t -> p (k t)")
    q_f = q[:, :, :].rearrange("p k t -> p (k t)")
    h_f = h_res[:, :, :].rearrange("p k t -> p (k t)")
    hid_hi_f = hid_hi[:, :, :].rearrange("p k t -> p (k t)")
    hid_lo_f = hid_lo[:, :, :].rearrange("p k t -> p (k t)")
    conv_f = conv_out[:, :, :, :].rearrange("p n s t -> p (n s t)")
    lru_f = lru_out[:, :, :].rearrange("p n s -> p (n s)")

    def halves(ap):
        return ap.rearrange("p (h n) -> p h n", h=2)

    block = ctx.enter_context(nc.Block())

    @block.sync
    def _(sp):
        def raw_load(i, slot, wait):
            if wait:
                sp.wait_ge(hi_ready, i * RAW + (slot - 1))
                sp.wait_ge(lo_ready, i * RAW + (slot - 1))
            sp.dma_start(w_raw[:, slot, :], weights_v[i, slot]).then_inc(raw_landed[slot], 16)

        weights_v = weights.rearrange("(i j) p n -> i j p n", j=RAW)

        x_v = x_t.rearrange("(k p) t -> p k t", p=P)
        sp.dma_start(x_raw[:, 0:2, :], x_v[:, 0:2, :]).then_inc(x_landed[0], 16)
        raw_load(0, 0, False)
        sp.dma_start(par[:, :], params).then_inc(par_landed, 16)
        sp.dma_start(con[:, :, :], consts).then_inc(con_landed, 16)
        for i in range(1, 8):
            sp.dma_start(x_raw[:, 2 * i:2 * i + 2, :], x_v[:, 2 * i:2 * i + 2, :]).then_inc(x_landed[i], 16)
            if i == 1:
                raw_load(0, 1, False)
        sp.dma_start(gate_w[:, :, :], w_gates[0]).then_inc(gate_landed, 16)
        sp.dma_start(oneh[0:BUCKETS, :], onehot).then_inc(rel_landed, 16)
        sp.dma_start(relb[0:BUCKETS, :], rel_bias).then_inc(rel_landed, 16)
        sp.dma_start(gym[0:HEADS, :], gy_mask).then_inc(rel_landed, 16)
        sp.dma_start(keep_k, cache_k_rows).then_inc(stored, 16)
        sp.dma_start(keep_v, cache_v_rows).then_inc(stored, 16)
        with sp.Fori(1, SLABS // RAW) as i:
            for j in range(RAW):
                raw_load(i, j, True)

        for m in range(KT):
            sp.wait_ge(y_ready, m + 1)
            sp.dma_start(y_t[m], h_res[:, m, :]).then_inc(stored, 16)
        sp.wait_ge(stored, 16 * (2 + KT + 3))

    @block.tensor
    def _(pe):
        def slab(s, slot, buf, hi, lo, k0, first, last, ready=None):
            pe.wait_ge(hi_ready, s + 1)
            pe.wait_ge(lo_ready, s + 1)
            for k in range(SLAB_K):
                if ready is not None:
                    ready(k)
                wh, wl = w_hi[:, slot, k, :], w_lo[:, slot, k, :]
                for part, (w, act) in enumerate(((wh, hi), (wh, lo), (wl, hi))):
                    for half in range(2):
                        st = first and k == 0 and part == 0
                        en = last and k == SLAB_K - 1 and part == 2
                        ins = nc.tensor.matmul(ps[:, 2 * buf + half, 0:HALF], w,
                                               act[:, k0 + k, half * HALF:(half + 1) * HALF],
                                               start=st, stop=en)
                if k == SLAB_K - 1:
                    ins.then_inc(slab_used, 1)

        def group(g, s, slot, buf, hi, lo, ready=None, wait=True):
            if wait:
                pe.wait_ge(group_out, g - 1)
            slab(s, slot, buf, hi, lo, 0, True, False, ready)
            slab(s + 1, slot + 1, buf, hi, lo, 8, False, True, None if ready is None else (lambda k: ready(8 + k)))

        def token_sums(src, n, ready, bank=4):
            ready()
            for half in range(2):
                ins = nc.tensor.matmul(ps[:, bank + half, 0:HALF], ones, src[:, half * HALF:(half + 1) * HALF],
                                       start=True, stop=True)
            ins.then_inc(sums_ready, 1)

        def xready(k):
            pe.wait_ge(xhi_ready, k + 1)
            pe.wait_ge(xlo_ready, k + 1)

        def gates(n):
            pe.wait_ge(conv_ready, n + 1)
            pe.wait_ge(gate_landed, (n + 1) * 16)
            for gi in range(2):
                for half in range(2):
                    ins = nc.tensor.matmul(ps[:, 4 + 2 * gi + half, 0:LH], gate_w[:, gi, :],
                                           xc[:, half * LH:(half + 1) * LH], start=True, stop=True)
            ins.then_inc(gates_ready, 1)

        group(0, 0, 0, 0, act_hi, act_lo, ready=xready, wait=False)
        group(1, 2, 2, 1, act_hi, act_lo, wait=False)
        pe.wait_ge(con_landed, 16)
        token_sums(acc, 0, lambda: pe.wait_ge(x_added, KT))
        pe.wait_ge(rel_landed, 48)
        nc.tensor.matmul(ps[0:HEADS, 6, 0:GY], relb[0:BUCKETS, :], oneh[0:BUCKETS, :],
                         start=True, stop=True).then_inc(gy_ps_ready, 1)
        pe.wait_ge(rb_ready, 1)
        pe.wait_ge(gy_ready, 1)
        gates(0)
        with pe.Fori(1, NB) as n:
            group(n * 2, n * 4, 0, 0, act_hi, act_lo)
            group(n * 2 + 1, n * 4 + 2, 2, 1, act_hi, act_lo)
            gates(n)
        with pe.Fori(0, KV) as j:
            group(j * 2 + 2 * NB, j * 4 + SLABS_REC, 0, 0, act_hi, act_lo)
            group(j * 2 + 2 * NB + 1, j * 4 + SLABS_REC + 2, 2, 1, act_hi, act_lo)
        token_sums(acc, 1, lambda: pe.wait_ge(rec_added, NB))
        pe.wait_ge(group_out, 2 * NB + 2 * KV)
        pe.wait_ge(root_ready, 2)
        for b in range(4):
            for g in range(KV):
                i = b * KV + g
                nc.tensor.transpose(ps[:, 4 + i // 4, (i % 4) * P:(i % 4 + 1) * P],
                                    kv[:, KV + g, b * P:(b + 1) * P], ident)
        for g in range(KV):
            nc.tensor.transpose(ps[0:TP - 4 * P, 6, g * P:(g + 1) * P], kv[:, KV + g, 4 * P:TP], ident)
        for g in range(KV):
            ins = nc.tensor.transpose(ps[0:TS, 7, g * P:(g + 1) * P], kv[:, KV + g, TP:T], ident)
        ins.then_inc(vt_ready, 1)
        with pe.Fori(KV, KV + HEADS // 2) as j:
            group(j * 2 + 2 * NB, j * 4 + SLABS_REC, 0, 0, act_hi, act_lo)
            group(j * 2 + 2 * NB + 1, j * 4 + SLABS_REC + 2, 2, 1, act_hi, act_lo)

        def scores(u):
            kind, i, g = UNITS[u]
            b0 = 4 + 2 * (u % 2)
            if u >= 2:
                pe.wait_ge(exp_ready, u - 1)
            if kind == "prompt":
                Q = min(P, TP - i * P)
                k0 = max(i - 1, 0) * P
                nk = i * P + Q - k0
                for h in range(GQ):
                    ins = nc.tensor.matmul(ps[0:Q, b0 + h // 2, (h % 2) * 2 * P:(h % 2) * 2 * P + nk],
                                           q[:, g * GQ + h, i * P:i * P + Q], kv[:, g, k0:k0 + nk],
                                           start=True, stop=True)
            else:
                nc.tensor.matmul(ps[:, b0, P:P + TS], q_s[:, g, i * P:(i + 1) * P], kv[:, g, TP:T],
                                 start=True, stop=True)
                for b in range(4):
                    ins = nc.tensor.matmul(ps[32 * b:32 * b + 32, b0, 0:P],
                                           q_s[:, g, i * P + 32 * b:i * P + 32 * b + 32],
                                           ck[:, 4 * i + b, g, :], start=True, stop=True)
            ins.then_inc(s_ready, 1)

        def turned(u):
            kind, i, g = UNITS[u]
            pe.wait_ge(probs_ready, u + 1)
            if u >= 1:
                pe.wait_ge(pt_copied, u)
            if kind == "prompt":
                Q = min(P, TP - i * P)
                k0 = max(i - 1, 0) * P
                nk = i * P + Q - k0
                for kb in range((nk + P - 1) // P):
                    kn = min(P, nk - kb * P)
                    for h in range(GQ):
                        ins = nc.tensor.transpose(ps[0:kn, kb, h * P:h * P + Q],
                                                  probs[0:Q, u % 2, h, kb * P:kb * P + kn], ident[0:Q, 0:Q])
            else:
                nc.tensor.transpose(ps[:, 0, 0:P], probs[:, u % 2, 0, 0:P], ident)
                ins = nc.tensor.transpose(ps[0:TS, 1, 0:P], probs[:, u % 2, 0, P:P + TS], ident)
            ins.then_inc(pt_ready, 1)

        def weighted(u):
            kind, i, g = UNITS[u]
            ob = 2 + u % 2
            pe.wait_ge(pt_copied, u + 1)
            if u >= 2:
                pe.wait_ge(o_copied, u - 1)
            if kind == "prompt":
                Q = min(P, TP - i * P)
                k0 = max(i - 1, 0) * P
                nk = i * P + Q - k0
                nkb = (nk + P - 1) // P
                for kb in range(nkb):
                    kn = min(P, nk - kb * P)
                    ins = nc.tensor.matmul(ps[:, ob, 0:GQ * Q], v_tok[0:kn, k0 // P + kb, g, :],
                                           probs_t[0:kn, u % 2, kb, :, 0:Q], start=kb == 0, stop=kb == nkb - 1)
            else:
                nc.tensor.matmul(ps[:, ob, 0:P], v_tok[0:TS, 5, g, :], probs_t[0:TS, u % 2, 1, 0, :],
                                 start=True, stop=False, skip_group_check=True)
                for b in range(4):
                    ins = nc.tensor.matmul(ps[:, ob, 32 * b:32 * b + 32], cv[:, 4 * i + b, g, :],
                                           probs_t[:, u % 2, 0, 0, 32 * b:32 * b + 32],
                                           start=False, stop=b == 3, skip_group_check=True)
            ins.then_inc(o_ready, 1)

        pe.wait_ge(group_out, G_OUT)
        pe.wait_ge(v_copied, 3)
        scores(0)
        scores(1)
        for u in range(NU):
            if u + 2 == 10:
                pe.wait_ge(qs_ready, KV)
                pe.wait_ge(cache_landed, 32)
            turned(u)
            if u + 2 < NU:
                scores(u + 2)
            weighted(u)

        def rec_ready_k(k):
            pe.wait_ge(xhi_ready, KT + k + 1)
            pe.wait_ge(xlo_ready, KT + k + 1)

        def att_ready_k(k):
            pe.wait_ge(xhi_ready, KT + 8 + k + 1)
            pe.wait_ge(xlo_ready, KT + 8 + k + 1)

        pe.wait_ge(pt_copied, NU)
        slab(S_OUT, 0, 0, act_hi, act_lo, 8, True, False, rec_ready_k)
        token_sums(acc, 2, lambda: pe.wait_ge(o_added, NU))
        pe.wait_ge(o_copied, NU)
        slab(S_OUT + 1, 1, 1, act_hi, act_lo, 8, True, False)
        slab(S_OUT + 2, 2, 0, act_hi, act_lo, 0, False, True, att_ready_k)
        slab(S_OUT + 3, 3, 1, act_hi, act_lo, 0, False, True)
        with pe.Fori(1, KT // 2) as j:
            for b in range(2):
                pe.wait_ge(group_out, j * 2 + G_OUT + b - 1)
                slab(j * 4 + S_OUT + 2 * b, 2 * b, b, act_hi, act_lo, 8, True, False)
                slab(j * 4 + S_OUT + 2 * b + 1, 2 * b + 1, b, act_hi, act_lo, 0, False, True)

        def hready(k):
            pe.wait_ge(xhi_ready, 2 * KT + k + 1)
            pe.wait_ge(xlo_ready, 2 * KT + k + 1)

        def up_pair(g, s, first=False):
            group(g, s, 0, 0, act_hi, act_lo, ready=hready if first else None)
            if first:
                token_sums(acc, 3, lambda: pe.wait_ge(h_added, KT))
            group(g + 1, s + 2, 2, 1, act_hi, act_lo)

        def down_four(g, s, ready=None):
            for b in range(4):
                pe.wait_ge(group_out, g + b - 1)
                slab(s + b, b, b % 2, hid_hi, hid_lo, 0, True, True, ready if b == 0 else None)

        def chunk(c, first):
            if first:
                up_pair(G_MLP, S_MLP, True)
            with pe.Fori(1 if first else 0, FC // 2) as f:
                up_pair(c * G_CHUNK + f * 2 + G_MLP, c * SLABS_CHUNK + f * 4 + S_MLP)
            g1, s1 = c * G_CHUNK + (G_MLP + FC), c * SLABS_CHUNK + (S_MLP + 2 * FC)
            down_four(g1, s1, lambda k: pe.wait_ge(hid_ready, c * FC + k + 1))
            with pe.Fori(1, KT // 4) as m:
                down_four(g1 + m * 4, s1 + m * 4)

        chunk(0, True)
        with pe.Fori(1, CHUNKS) as c:
            chunk(c, False)
        token_sums(acc, 4, lambda: pe.wait_ge(h_added, 2 * KT))

    @block.scalar
    def _(act):
        step = Steps(act, act_step)

        def w_high(s, slot, free=True):
            act.wait_ge(raw_landed[slot % RAW], s * 8 + (16 - 8 * (slot % RAW)))
            if free:
                act.wait_ge(slab_used, s - (RING - 1))
            nc.scalar.activation(w_hi[:, slot, :, :], w_raw[:, slot % RAW, :].rearrange("p (k n) -> p k n", k=SLAB_K),
                                 ACT.Copy).then_inc(hi_ready, 1)

        def root(n, width, dst):
            act.wait_ge(sums_ready, n + 1)
            nc.scalar.activation(halves(dst[:, :]), ps[:, 4:6, 0:HALF], ACT.Sqrt, bias=eps_t[:, :],
                                 scale=1.0 / width).then_inc(root_ready, 1)

        act.wait_ge(par_landed, 16)
        for k in range(KT):
            if k % 2 == 0:
                act.wait_ge(x_landed[k // 2], 16)
            nc.scalar.activation(act_hi[:, k, :], x_raw[:, k, :], ACT.Copy, scale=col("g_mix", k))\
                .then_inc(xhi_ready, 1)
            if k == 0:
                w_high(0, 0, False)
            if k == 4:
                w_high(1, 1, False)
            if k == 12:
                w_high(2, 2, False)
        for k in range(KT):
            if k >= 2:
                act.wait_ge(x_added, k - 1)
            nc.scalar.activation(sq[:, k % 2, :], x_raw[:, k, :], ACT.Square).then_inc(x_squared, 1)
        act.wait_ge(sp_exp, 1)
        nc.scalar.activation(spt[:, 1, :], spt[:, 0, :], ACT.Exp).then_inc(sp_exp, 1)
        w_high(3, 3, False)
        act.wait_ge(pads_ready, 1)
        root(0, D_MODEL, rb)
        act.wait_ge(gy_ready, 1)
        act.dma_start(gy_dram.ap(), gy[0:HEADS, :].rearrange("h (o y) -> h o y", o=1).to_broadcast([HEADS, P, GY])).then_inc(gy_stored, 16)

        def tap0(n):
            act.wait_ge(group_out, n * 2 + 1)
            act.wait_ge(hist_ready, n + 1)
            nc.scalar.activation(xc[:, :], xp[:, 0:LT], ACT.Identity, bias=dcol("conv_b", n),
                                 scale=dcol("conv_w", n)).then_inc(tap0_ready, 1)

        def square_rec(n):
            act.wait_ge(rec_ready, n + 1)
            act.wait_ge(rec_added, n)
            nc.scalar.activation(sq[:, 0, :], rec_f[:, bass.ds(n * T, T)], ACT.Square).then_inc(rec_squared, 1)

        def gelu_and_gates(n):
            act.wait_ge(group_out, n * 2 + 2)
            nc.scalar.activation(gel_t[:, :], gel[:, :], ACT.Square, scale=GELU_K).then_inc(g_squared, 1)
            act.wait_ge(g_poly, n + 1)
            nc.scalar.activation(gel_t[:, :], gel_t[:, :], ACT.Tanh, scale=GELU_C).then_inc(g_tanh, 1)

        def gates(n):
            act.wait_ge(gates_ready, n + 1)
            nc.scalar.activation(t_a[:, :].rearrange("p (h n) -> p h n", h=2), ps[:, 4:6, 0:LH], ACT.Tanh,
                                 bias=half_b[:, 0, bass.ds(n, 1)], scale=0.5).then_inc(tanh_a, 1)
            nc.scalar.activation(t_x[:, :].rearrange("p (h n) -> p h n", h=2), ps[:, 6:8, 0:LH], ACT.Tanh,
                                 bias=half_b[:, 1, bass.ds(n, 1)], scale=0.5).then_inc(tanh_x, 1)
            act.wait_ge(tanh_a, n + 1)
            nc.scalar.activation(t_a[:, :], t_a[:, :], ACT.Tanh, bias=sp2[:, bass.ds(n, 1)],
                                 scale=sp2[:, bass.ds(n, 1)]).then_inc(tau_ready, 1)
            act.wait_ge(tau_ready, n + 1)
            nc.scalar.activation(t_s[:, :], t_a[:, :], ACT.Sqrt).then_inc(sqrt_ready, 1)

        with act.Fori(0, NB) as n:
            s = n * 4
            act.wait_ge(sp_ready, 1)

            def high(i):
                w_high(s + i, i % RING)
            high(4)
            high(5)
            tap0(n)
            high(6)
            gelu_and_gates(n)
            high(7)
            gates(n)
            act.dma_start(gate_w[:, :, :], w_gates[n + 1]).then_inc(gate_landed, 16)
            square_rec(n)

        with act.Fori(SLABS_REC // 4, SLABS_REC // 4 + KV) as j:
            for i in range(4):
                w_high(j * 4 + 4 + i, i)
        act.wait_ge(rec_added, NB)
        root(1, LRU_W, rn)
        act.wait_ge(vt_ready, 1)
        nc.scalar.activation(v_tok[:, 0:4, :, :].rearrange("p b g d -> p (b g d)").rearrange("p (c n) -> p c n", c=2),
                             ps[:, 4:6, :], ACT.Copy).then_inc(v_copied, 1)
        nc.scalar.activation(v_tok[0:TP - 4 * P, 4, :, :], ps[0:TP - 4 * P, 6, 0:KV * P].rearrange("p (g d) -> p g d", g=KV),
                             ACT.Copy).then_inc(v_copied, 1)
        nc.scalar.activation(v_tok[0:TS, 5, :, :], ps[0:TS, 7, 0:KV * P].rearrange("p (g d) -> p g d", g=KV),
                             ACT.Copy).then_inc(v_copied, 1)
        act.wait_ge(xr_kept, NB)
        act.dma_start(conv_o, conv_out[:, :, :, :]).then_inc(stored, 16)
        act.wait_ge(rec_ready, NB)
        act.dma_start(lru_o, lru_out[:, :, :]).then_inc(stored, 16)
        act.dma_start(kv_t, kv[:, :, TP - WINDOW:T]).then_inc(stored, 16)
        act.wait_ge(gy_stored, 16)
        act.dma_start(bias_p[:, :, :], bass.AP(gy_dram, P - 1, [[GY - 1, P], [P * GY, HEADS], [1, 2 * P]]))\
            .then_inc(bias_landed, 16)
        act.wait_ge(pads_ready, 2)
        for g in range(KV):
            for b in range(4):
                for i in range(2):
                    act.dma_start(bias_s[32 * b:32 * b + 32, i, g, 0:P],
                                  bass.AP(gy_dram, g * GQ * P * GY + P - 1, [[P * GY, GQ], [GY - 1, DEC_T], [1, P]]))\
                        .then_inc(bias_landed, 16)
                    act.dma_start(bias_s[32 * b:32 * b + 32, i, g, P + DEC_T * (4 * i + b):P + DEC_T * (4 * i + b + 1)],
                                  bass.AP(gy_dram, g * GQ * P * GY + 2 * P - 1, [[P * GY, GQ], [GY - 1, DEC_T], [1, DEC_T]]))\
                        .then_inc(bias_landed, 16)
        with act.Fori(SLABS_REC // 4 + KV, SLABS_IN // 4) as j:
            for i in range(3):
                w_high(j * 4 + 4 + i, i)
            w_high(j * 4 + 7, 3)
        act.wait_ge(slab_used, SLABS_IN)
        act.dma_start(ck[:, :, :, :], cache_kt).then_inc(cache_landed, 16)
        act.dma_start(cv[:, :, :, :], cache_v).then_inc(cache_landed, 16)

        def exps(u):
            kind, i, g = UNITS[u]
            act.wait_ge(negmax_ready, u + 1)
            if kind == "prompt":
                Q = min(P, TP - i * P)
                nk = i * P + Q - max(i - 1, 0) * P
                nc.scalar.activation(stat[0:Q, u % 2, 4, :], stat[0:Q, u % 2, 2, :], ACT.Exp).then_inc(act_step, 1)
                for h in range(GQ):
                    ins = nc.scalar.activation(probs[0:Q, u % 2, h, 0:nk], probs[0:Q, u % 2, h, 0:nk], ACT.Exp,
                                               bias=stat[0:Q, u % 2, 1, h:h + 1], accum_out=stat[0:Q, u % 2, 3, h:h + 1])
                    if h < GQ - 1:
                        ins.then_inc(act_step, 1)
            else:
                nc.scalar.activation(stat[:, u % 2, 4, 0:1], stat[:, u % 2, 2, 0:1], ACT.Exp).then_inc(act_step, 1)
                ins = nc.scalar.activation(probs[:, u % 2, 0, 0:P + TS], probs[:, u % 2, 0, 0:P + TS], ACT.Exp,
                                           bias=stat[:, u % 2, 1, 0:1], accum_out=stat[:, u % 2, 3, 0:1])
            ins.then_inc(exp_ready, 1)

        def pt_copy(u):
            kind, i, g = UNITS[u]
            act.wait_ge(pt_ready, u + 1)
            if u >= 2:
                act.wait_ge(o_ready, u - 1)
            if kind == "prompt" and 0 < i < 4:
                nc.scalar.activation(probs_t[:, u % 2, :, :, :], ps[:, 0:2, :].rearrange("p c (h n) -> p c h n", h=GQ),
                                     ACT.Copy).then_inc(pt_copied, 1)
            elif kind == "prompt" and i == 0:
                nc.scalar.activation(probs_t[:, u % 2, 0, :, :], ps[:, 0, :].rearrange("p (h n) -> p h n", h=GQ),
                                     ACT.Copy).then_inc(pt_copied, 1)
            elif kind == "prompt":
                Q = TP - 4 * P
                nc.scalar.activation(probs_t[:, u % 2, 0, :, 0:Q], ps[:, 0, :].rearrange("p (h n) -> p h n", h=GQ)[:, :, 0:Q],
                                     ACT.Copy).then_inc(act_step, 1)
                nc.scalar.activation(probs_t[0:Q, u % 2, 1, :, 0:Q],
                                     ps[0:Q, 1, :].rearrange("p (h n) -> p h n", h=GQ)[:, :, 0:Q],
                                     ACT.Copy).then_inc(pt_copied, 1)
            else:
                nc.scalar.activation(probs_t[:, u % 2, 0, 0, :], ps[:, 0, 0:P], ACT.Copy).then_inc(act_step, 1)
                nc.scalar.activation(probs_t[0:TS, u % 2, 1, 0, :], ps[0:TS, 1, 0:P], ACT.Copy).then_inc(pt_copied, 1)

        act.wait_ge(rec_scaled, NB)
        for u in range(NU + 1):
            if u < NU:
                exps(u)
            if u < NB:
                nc.scalar.activation(act_hi[:, 8 + u, :], rec[:, u, :], ACT.Copy).then_inc(xhi_ready, 1)
            if u >= 1:
                pt_copy(u - 1)
        act.wait_ge(s_ready, NU)
        act.wait_ge(o_ready, NU)
        act.wait_ge(negmax_ready, NU)
        act.wait_ge(stored, 16 * 5)
        x_v = x_t.rearrange("(k p) t -> p k t", p=P)
        for i in range(4):
            act.dma_start(h_res[:, 4 * i:4 * i + 4, :], x_v[:, 4 * i:4 * i + 4, :]).then_inc(h_landed[i], 16)
        root(2, LRU_W, rn)
        for k in range(HEADS):
            act.wait_ge(att_scaled, k + 1)
            nc.scalar.activation(act_hi[:, k, :], q[:, k, :], ACT.Copy).then_inc(xhi_ready, 1)

        def high_and_square(j):
            for b in range(2):
                w_high(j * 4 + S_OUT + 4 + 2 * b, 2 * b)
                w_high(j * 4 + S_OUT + 4 + 2 * b + 1, 2 * b + 1)
                act.wait_ge(group_out, j * 2 + G_OUT + b + 1)
                if isinstance(j, int) and j == 0:
                    nc.scalar.activation(sq[:, b, :], h_res[:, b, :], ACT.Square).then_inc(h_squared, 1)
                else:
                    act.wait_ge(h_added, j * 2 + b - 1)
                    nc.scalar.activation(sq[:, b, :], h_f[:, bass.ds((j * 2 + b) * T, T)], ACT.Square)\
                        .then_inc(h_squared, 1)

        high_and_square(0)
        with act.Fori(1, KT // 2) as j:
            high_and_square(j)
        for k in range(KT):
            nc.scalar.activation(act_hi[:, k, :], h_res[:, k, :], ACT.Copy, scale=col("g_mlp", k)).then_inc(xhi_ready, 1)
        root(3, D_MODEL, rb)

        def square_hid(g):
            act.wait_ge(group_out, g + 1)
            nc.scalar.activation(mlp_b[:, :], mlp_a[:, :], ACT.Square).then_inc(square_ready, 1)

        def chunk(c, last):
            s = c * SLABS_CHUNK + S_MLP
            with act.Fori(0, FC // 2) as f:
                for b in range(2):
                    w_high(s + f * 4 + 4 + 2 * b, 2 * b)
                    w_high(s + f * 4 + 4 + 2 * b + 1, 2 * b + 1)
                    square_hid(c * G_CHUNK + f * 2 + (G_MLP + b))
            if not last:
                with act.Fori(0, KT // 4) as m:
                    for b in range(4):
                        w_high(s + m * 4 + 2 * FC + 4 + b, b)
            else:
                for m in range(KT):
                    if m + 4 < KT:
                        w_high(SLABS - KT + m + 4, m % 4)
                    act.wait_ge(group_out, G_MLP + CHUNKS * G_CHUNK - KT + m + 1)
                    act.wait_ge(h_added, KT + m - 1)
                    nc.scalar.activation(sq[:, m % 2, :], h_res[:, m, :], ACT.Square).then_inc(h_squared, 1)

        with act.Fori(0, CHUNKS - 1) as c:
            chunk(c, False)
        chunk(CHUNKS - 1, True)
        root(4, D_MODEL, rb)

    @block.gpsimd
    def _(pool):
        step = Steps(pool, pool_step)

        def w_low(s, slot, free=True):
            pool.wait_ge(raw_landed[slot % RAW], s * 8 + (16 - 8 * (slot % RAW)))
            pool.wait_ge(hi_ready, s + 1)
            if free:
                pool.wait_ge(slab_used, s - (RING - 1))
            nc.gpsimd.tensor_tensor(w_lo[:, slot, :, :], w_raw[:, slot % RAW, :].rearrange("p (k n) -> p k n", k=SLAB_K),
                                    w_hi[:, slot, :, :].bitcast(F32), ALU.subtract).then_inc(lo_ready, 1)

        pool.memset(eps_t[:, :], EPS).then_inc(pads_ready, 1)
        for s in range(4):
            w_low(s, s, False)

        def history(n):
            a = COL["hist"][0]
            nc.gpsimd.tensor_copy(sample(xp, S0)[:, :, 0:HIST],
                                  par[:, bass.ds(n * (DEC_B * HIST) + a, DEC_B * HIST)].rearrange(
                                      "p (b t) -> p b t", b=DEC_B)).then_inc(hist_ready, 1)

        pool.wait_ge(par_landed, 16)
        pool.wait_ge(x_squared, KT)
        pool.wait_ge(xlo_ready, KT)
        step(nc.gpsimd.memset(xp[:, 0:HIST], 0.0))
        a = COL["hist"][0]
        nc.gpsimd.tensor_copy(sample(xp, S0)[:, :, 0:HIST],
                              par[:, a:a + DEC_B * HIST].rearrange("p (b t) -> p b t", b=DEC_B)).then_inc(hist_ready, 1)

        def kept(n):
            pool.wait_ge(conv_ready, n + 1)
            nc.gpsimd.tensor_copy(conv_f[:, bass.ds(n * 9 * HIST, HIST)], xp[:, TP:TP + HIST]).then_inc(pool_step, 1)
            nc.gpsimd.tensor_copy(conv_f[:, bass.ds(n * 9 * HIST + HIST, DEC_B * HIST)].rearrange("p (b t) -> p b t", b=DEC_B),
                                  sample(xp, S0)[:, :, DEC_T:SEQ_S]).then_inc(xr_kept, 1)
            pool.wait_ge(xr_kept, n + 1)

        def add_rec(n, first):
            pool.wait_ge(rec_squared, n + 1)
            if first:
                pool.wait_ge(sums_ready, 1)
                nc.gpsimd.tensor_copy(acc[:, :], sq[:, 0, :]).then_inc(rec_added, 1)
            else:
                pool.wait_ge(rec_added, n)
                nc.gpsimd.tensor_tensor(acc[:, :], acc[:, :], sq[:, 0, :], ALU.add).then_inc(rec_added, 1)

        def rec_block(n, first):
            for i in (4, 5):
                w_low(n * 4 + i, i % RING)
            kept(n)
            history(n + 1)
            for i in (6, 7):
                w_low(n * 4 + i, i % RING)
            add_rec(n, first)

        rec_block(0, True)
        with pool.Fori(1, NB) as n:
            rec_block(n, False)

        with pool.Fori(SLABS_REC // 4, SLABS_REC // 4 + KV) as j:
            for i in range(4):
                w_low(j * 4 + 4 + i, i)
        pool.wait_ge(rec_ready, NB)
        pool.memset(bias_s[:, :, :, :], MASKED).then_inc(pads_ready, 1)
        with pool.Fori(SLABS_REC // 4 + KV, SLABS_IN // 4) as j:
            for i in range(4):
                w_low(j * 4 + 4 + i, i)

        pool.wait_ge(group_out, G_OUT)
        for g in range(KV):
            nc.gpsimd.tensor_copy(
                q_s[:, g, :].rearrange("p (b h t) -> p b h t", b=DEC_B, h=GQ),
                q[:, g * GQ:(g + 1) * GQ, TP:T].rearrange("p h (b t) -> p b h t", b=DEC_B)).then_inc(qs_ready, 1)
        step.loop(step.k + NB)
        pool.wait_ge(sums_ready, 2)
        for u in range(NU):
            if u < NB:
                pool.wait_ge(xhi_ready, KT + u + 1)
                nc.gpsimd.tensor_tensor(act_lo[:, 8 + u, :], rec[:, u, :], act_hi[:, 8 + u, :].bitcast(F32),
                                        ALU.subtract).then_inc(xlo_ready, 1)
            kind, i, g = UNITS[u]
            pool.wait_ge(o_copied, u + 1)
            if kind == "prompt":
                c0, n = i * P, min(P, TP - i * P)
            else:
                c0, n = TP + 32 * i, 32
            o = q[:, g * GQ:(g + 1) * GQ, c0:c0 + n]
            s = sq[:, 0, 0:GQ * n].rearrange("p (h n) -> p h n", h=GQ)
            step(nc.gpsimd.tensor_tensor(s, o, o, ALU.mult))
            step(nc.gpsimd.tensor_tensor(s[:, 0:2, :], s[:, 0:2, :], s[:, 2:4, :], ALU.add))
            if g == 0:
                nc.gpsimd.tensor_tensor(acc[:, c0:c0 + n], s[:, 0, :], s[:, 1, :], ALU.add).then_inc(o_added, 1)
            else:
                step(nc.gpsimd.tensor_tensor(s[:, 0, :], s[:, 0, :], s[:, 1, :], ALU.add))
                nc.gpsimd.tensor_tensor(acc[:, c0:c0 + n], acc[:, c0:c0 + n], s[:, 0, :], ALU.add).then_inc(o_added, 1)
            pool.wait_ge(o_added, u + 1)

        def low_and_add(j):
            for b in range(2):
                w_low(j * 4 + S_OUT + 4 + 2 * b, 2 * b)
                w_low(j * 4 + S_OUT + 4 + 2 * b + 1, 2 * b + 1)
                pool.wait_ge(h_squared, j * 2 + b + 1)
                if isinstance(j, int) and b == 0:
                    pool.wait_ge(sums_ready, 3)
                    nc.gpsimd.tensor_copy(acc[:, :], sq[:, 0, :]).then_inc(h_added, 1)
                else:
                    pool.wait_ge(h_added, j * 2 + b)
                    nc.gpsimd.tensor_tensor(acc[:, :], acc[:, :], sq[:, b, :], ALU.add).then_inc(h_added, 1)

        low_and_add(0)
        with pool.Fori(1, KT // 2) as j:
            low_and_add(j)

        with pool.Fori(S_MLP // 4, (SLABS - KT) // 4) as j:
            for i in range(4):
                w_low(j * 4 + 4 + i, i)
        for m in range(KT):
            if m + 4 < KT:
                w_low(SLABS - KT + m + 4, m % 4)
            pool.wait_ge(h_squared, KT + m + 1)
            if m == 0:
                pool.wait_ge(sums_ready, 4)
                nc.gpsimd.tensor_copy(acc[:, :], sq[:, 0, :]).then_inc(h_added, 1)
            else:
                pool.wait_ge(h_added, KT + m)
                nc.gpsimd.tensor_tensor(acc[:, :], acc[:, :], sq[:, m % 2, :], ALU.add).then_inc(h_added, 1)

    @block.vector
    def _(dve):
        step = Steps(dve, dve_step)
        v = nc.vector

        def rsqrt(n, dst):
            dve.wait_ge(root_ready, n + 1)
            v.reciprocal(dst[:, :], dst[:, :]).then_inc(rb_ready, 1)
            dve.wait_ge(rb_ready, n + 1)

        dve.wait_ge(par_landed, 16)
        for k in range(KT):
            dve.wait_ge(xhi_ready, k + 1)
            v.scalar_tensor_tensor(act_lo[:, k, :], x_raw[:, k, :], col("g_mix", k), act_hi[:, k, :].bitcast(F32),
                                   ALU.mult, ALU.subtract).then_inc(xlo_ready, 1)
        for k in range(KT):
            dve.wait_ge(x_squared, k + 1)
            if k == 0:
                v.tensor_copy(acc[:, :], sq[:, 0, :]).then_inc(x_added, 1)
            else:
                dve.wait_ge(x_added, k)
                v.tensor_tensor(acc[:, :], acc[:, :], sq[:, k % 2, :], ALU.add).then_inc(x_added, 1)
        step(v.tensor_scalar(spt[:, 2, :], col("lam", 0, NB), -1.0, None, ALU.mult))
        v.tensor_tensor(spt[:, 0, :], col("lam", 0, NB), spt[:, 2, :], ALU.min).then_inc(sp_exp, 1)
        dve.wait_ge(sp_exp, 2)
        step(v.tensor_scalar(spt[:, 3, :], spt[:, 1, :], 2.0, None, ALU.add))
        step(v.reciprocal(spt[:, 3, :], spt[:, 3, :]))
        step(v.tensor_tensor(spt[:, 1, :], spt[:, 1, :], spt[:, 3, :], ALU.mult))
        step(v.tensor_tensor(spt[:, 3, :], spt[:, 1, :], spt[:, 1, :], ALU.mult))
        step(v.memset(spt[:, 0, :], 1.0 / 17.0))
        for d in (15, 13, 11, 9, 7, 5, 3, 1):
            step(v.tensor_tensor(spt[:, 0, :], spt[:, 0, :], spt[:, 3, :], ALU.mult))
            step(v.tensor_scalar(spt[:, 0, :], spt[:, 0, :], 1.0 / d, None, ALU.add))
        step(v.tensor_tensor(spt[:, 0, :], spt[:, 0, :], spt[:, 1, :], ALU.mult))
        step(v.tensor_scalar(spt[:, 2, :], spt[:, 2, :], 0.0, 2.0, ALU.max, ALU.mult))
        step(v.scalar_tensor_tensor(sp2[:, :], spt[:, 0, :], 4.0, spt[:, 2, :], ALU.mult, ALU.add))
        step(v.tensor_scalar(half_b[:, 0, :], col("b_a", 0, NB), 0.5, None, ALU.mult))
        v.tensor_scalar(half_b[:, 1, :], col("b_x", 0, NB), 0.5, None, ALU.mult).then_inc(sp_ready, 1)
        rsqrt(0, rb)
        dve.wait_ge(gy_ps_ready, 1)
        v.tensor_tensor(gy[0:HEADS, :], ps[0:HEADS, 6, 0:GY], gym[0:HEADS, :], ALU.add).then_inc(gy_ready, 1)

        STEPS_REC = 18
        first_base = step.k

        def rec_block(n):
            step.loop(n * STEPS_REC + first_base)
            dve.wait_ge(slab_used, n * 4 + 2)
            dve.wait_ge(hist_ready, n + 1)
            v.tensor_tensor(xp[:, HIST:HIST + HALF], ps[:, 0, 0:HALF], rb[:, 0:HALF], ALU.mult).then_inc(dve_step, 1)
            v.tensor_tensor(xp[:, HIST + HALF:HIST + TP], ps[:, 1, 0:TP - HALF], rb[:, HALF:TP], ALU.mult)\
                .then_inc(dve_step, 1)
            step.k += 2
            v.tensor_tensor(sample(xp, S0)[:, :, HIST:SEQ_S],
                            ps[:, 1, TP - HALF:HALF].rearrange("p (b t) -> p b t", b=DEC_B),
                            rb[:, TP:T].rearrange("p (b t) -> p b t", b=DEC_B), ALU.mult).then_inc(group_out, 1)
            dve.wait_ge(group_out, n * 2 + 1)
            dve.wait_ge(tap0_ready, n + 1)
            for j in range(1, CONV_W):
                ins = v.scalar_tensor_tensor(xc[:, :], xp[:, j:j + LT], dcol("conv_w", n + j * NB), xc[:, :],
                                             ALU.mult, ALU.add)
                if j < CONV_W - 1:
                    step(ins)
            ins.then_inc(conv_ready, 1)
            dve.wait_ge(slab_used, n * 4 + 4)
            v.tensor_tensor(halves(gel[:, :]), acc_pair(1), halves(rb[:, :]), ALU.mult).then_inc(group_out, 1)
            dve.wait_ge(g_squared, n + 1)
            v.scalar_tensor_tensor(gel_t[:, :], gel_t[:, :], 1.0, gel[:, :], ALU.add, ALU.mult).then_inc(g_poly, 1)
            dve.wait_ge(g_tanh, n + 1)
            step(v.scalar_tensor_tensor(gel[:, :], gel_t[:, :], 1.0, gel[:, :], ALU.add, ALU.mult))
            dve.wait_ge(tanh_x, n + 1)
            step(v.scalar_tensor_tensor(t_x[:, :], t_x[:, :], 1.0, xc[:, :], ALU.add, ALU.mult))
            dve.wait_ge(tau_ready, n + 1)
            step(v.tensor_scalar(t_r[:, :], t_a[:, :], 1.0, None, ALU.add))
            step(v.reciprocal(t_r[:, :], t_r[:, :]))
            dve.wait_ge(sqrt_ready, n + 1)
            step(v.tensor_scalar(t_a[:, :], t_r[:, :], 2.0, -1.0, ALU.mult, ALU.add))
            step(v.tensor_tensor(t_s[:, :], t_s[:, :], t_r[:, :], ALU.mult))
            step(v.memset(t_s[:, 0:1], 0.5))
            step(v.tensor_tensor(t_s[:, :], t_s[:, :], t_x[:, :], ALU.mult))
            pads = [sample(t, TP)[:, :, 0:HIST] for t in (t_a, t_s)]
            step(v.memset(pads[0], 0.0))
            step(v.tensor_copy(pads[1], par[:, bass.ds(n * (DEC_B * HIST) + COL["h0"][0], DEC_B * HIST)].rearrange(
                "p (b t) -> p b t", b=DEC_B)))
            step(v.tensor_tensor_scan(hs[:, :], t_a[:, :], t_s[:, :], 0.0, ALU.mult, ALU.add))
            v.tensor_copy(lru_f[:, bass.ds(n * 9, 1)], hs[:, TP - 1:TP]).then_inc(dve_step, 1)
            v.tensor_copy(lru_f[:, bass.ds(n * 9 + 1, DEC_B)], sample(hs, TP)[:, :, SEQ_S - 1]).then_inc(dve_step, 1)
            v.scalar_tensor_tensor(rec_f[:, bass.ds(n * T, TP)], gel[:, 0:TP], 0.5, hs[:, 0:TP],
                                   ALU.mult, ALU.mult).then_inc(dve_step, 1)
            v.scalar_tensor_tensor(
                rec_f[:, bass.ds(n * T + TP, TS)].rearrange("p (b t) -> p b t", b=DEC_B),
                gel[:, TP:T].rearrange("p (b t) -> p b t", b=DEC_B), 0.5,
                sample(hs, TP)[:, :, HIST:SEQ_S], ALU.mult, ALU.mult).then_inc(rec_ready, 1)
            step.k += 3
            dve.wait_ge(rec_ready, n + 1)
            assert step.k == STEPS_REC, step.k

        with dve.Fori(0, NB) as n:
            rec_block(n)
        step.base, step.k = first_base + NB * STEPS_REC, 0

        with dve.Fori(0, KV) as j:
            for b in range(2):
                dve.wait_ge(slab_used, j * 4 + SLABS_REC + 2 * b + 2)
                v.tensor_tensor(halves(kv_f[:, bass.ds((j * 2 + b) * T, T)]), acc_pair(b),
                                halves(rb[:, :]), ALU.mult).then_inc(group_out, 1)
        rsqrt(1, rn)
        with dve.Fori(0, NB) as n:
            tile = rec_f[:, bass.ds(n * T, T)]
            v.scalar_tensor_tensor(tile, tile, dcol("g_rec", n), rn[:, :], ALU.mult, ALU.mult).then_inc(rec_scaled, 1)
        with dve.Fori(0, HEADS // 2) as j:
            for b in range(2):
                dve.wait_ge(slab_used, j * 4 + SLABS_REC + 4 * KV + 2 * b + 2)
                v.tensor_tensor(halves(q_f[:, bass.ds((j * 2 + b) * T, T)]), acc_pair(b),
                                halves(rb[:, :]), ALU.mult).then_inc(group_out, 1)

        def unit_rows(u):
            kind, i, g = UNITS[u]
            if kind == "prompt":
                Q = min(P, TP - i * P)
                return Q, i * P + Q - max(i - 1, 0) * P, slice(0, GQ)
            return P, P + TS, slice(0, 1)

        def front(u):
            kind, i, g = UNITS[u]
            Q, nk, hs_ = unit_rows(u)
            b0 = 4 + 2 * (u % 2)
            dve.wait_ge(s_ready, u + 1)
            if u >= 2:
                dve.wait_ge(pt_ready, u - 1)
            st = stat[0:Q, u % 2]
            if kind == "prompt":
                off = P if i == 0 else 0
                s_in = ps[0:Q, b0:b0 + 2, :].rearrange("p c (h n) -> p (c h) n", h=2)[:, :, 0:nk]
                bias, sink = bias_p[0:Q, g * GQ:(g + 1) * GQ, off:off + nk], col("sink_p", g * GQ, GQ)[0:Q]
                dst = probs[0:Q, u % 2, :, 0:nk]
            else:
                s_in, bias, sink = ps[:, b0, 0:nk], bias_s[:, i, g, :], col("sink_s", g)
                dst = probs[:, u % 2, 0, 0:nk]
            step(v.scalar_tensor_tensor(dst, s_in, SCALE, bias, ALU.mult, ALU.add))
            step(v.tensor_reduce(st[:, 0, hs_], dst, AX.X, ALU.max))
            step(v.tensor_tensor(st[:, 0, hs_], st[:, 0, hs_], sink, ALU.max))
            v.tensor_scalar(st[:, 1, hs_], st[:, 0, hs_], -1.0, None, ALU.mult).then_inc(dve_step, 1)
            step.k += 1
            v.tensor_tensor(st[:, 2, hs_], sink, st[:, 0, hs_], ALU.subtract).then_inc(negmax_ready, 1)

        def norm(u):
            kind, i, g = UNITS[u]
            Q, nk, hs_ = unit_rows(u)
            st = stat[0:Q, u % 2]
            dve.wait_ge(exp_ready, u + 1)
            step(v.tensor_tensor(st[:, 5, hs_], st[:, 3, hs_], st[:, 4, hs_], ALU.add))
            step(v.reciprocal(st[:, 5, hs_], st[:, 5, hs_]))
            if kind == "prompt":
                p = probs[0:Q, u % 2, :, 0:nk]
                r = st[:, 5, :].rearrange("p (h o) -> p h o", o=1).to_broadcast([Q, GQ, nk])
                v.tensor_tensor(p, p, r, ALU.mult).then_inc(probs_ready, 1)
            else:
                p = probs[:, u % 2, 0, 0:nk]
                v.tensor_scalar(p, p, st[:, 5, 0:1], None, ALU.mult).then_inc(probs_ready, 1)

        def out(u):
            kind, i, g = UNITS[u]
            dve.wait_ge(o_ready, u + 1)
            if kind == "prompt":
                Q = min(P, TP - i * P)
                v.tensor_copy(q[:, g * GQ:(g + 1) * GQ, i * P:i * P + Q],
                              ps[:, 2 + u % 2, 0:GQ * Q].rearrange("p (h n) -> p h n", h=GQ)).then_inc(o_copied, 1)
            else:
                c0 = TP + 32 * i
                v.tensor_copy(q[:, g * GQ:(g + 1) * GQ, c0:c0 + 32].rearrange("p h (b t) -> p b h t", b=4),
                              ps[:, 2 + u % 2, 0:P].rearrange("p (b h t) -> p b h t", b=4, h=GQ)).then_inc(o_copied, 1)

        dve.wait_ge(bias_landed, 16 * (1 + 4 * 2 * 2 * KV))
        for u in range(NU + 2):
            if u < NU:
                front(u)
            if 1 <= u <= NU:
                norm(u - 1)
            if u >= 2:
                if u == 2 + 10:
                    dve.wait_ge(qs_ready, KV)
                out(u - 2)

        rsqrt(2, rn)
        v.scalar_tensor_tensor(q[:, 0, :], q[:, 0, :], col("g_att", 0), rn[:, :], ALU.mult, ALU.mult).then_inc(att_scaled, 1)
        for k in range(HEADS):
            if k + 1 < HEADS:
                v.scalar_tensor_tensor(q[:, k + 1, :], q[:, k + 1, :], col("g_att", k + 1), rn[:, :], ALU.mult, ALU.mult)\
                    .then_inc(att_scaled, 1)
            dve.wait_ge(att_scaled, k + 1)
            dve.wait_ge(xhi_ready, KT + NB + k + 1)
            v.tensor_tensor(act_lo[:, k, :], q[:, k, :], act_hi[:, k, :].bitcast(F32), ALU.subtract).then_inc(xlo_ready, 1)

        for i in range(4):
            dve.wait_ge(h_landed[i], 16)
        for b in range(2):
            dve.wait_ge(slab_used, S_OUT + 3 + b)
            v.tensor_tensor(halves(h_res[:, b, :]), acc_pair(b), halves(h_res[:, b, :]), ALU.add).then_inc(group_out, 1)
        with dve.Fori(1, KT // 2) as j:
            for b in range(2):
                dve.wait_ge(slab_used, j * 4 + S_OUT + 2 * b + 2)
                tile = halves(h_f[:, bass.ds((j * 2 + b) * T, T)])
                v.tensor_tensor(tile, acc_pair(b), tile, ALU.add).then_inc(group_out, 1)
        for k in range(KT):
            dve.wait_ge(xhi_ready, 2 * KT + k + 1)
            v.scalar_tensor_tensor(act_lo[:, k, :], h_res[:, k, :], col("g_mlp", k), act_hi[:, k, :].bitcast(F32),
                                   ALU.mult, ALU.subtract).then_inc(xlo_ready, 1)
        rsqrt(3, rb)

        def chunk(c):
            with dve.Fori(0, FC // 2) as f:
                for b in range(2):
                    dve.wait_ge(slab_used, c * SLABS_CHUNK + f * 4 + (S_MLP + 2 * b + 2))
                    v.scalar_tensor_tensor(halves(mlp_a[:, :]), acc_pair(b), 0.0, halves(rb[:, :]), ALU.max, ALU.mult)\
                        .then_inc(group_out, 1)
                    dve.wait_ge(square_ready, c * FC + f * 2 + b + 1)
                    at = (f * 2 + b) * T
                    v.tensor_copy(hid_hi_f[:, bass.ds(at, T)], mlp_b[:, :]).then_inc(hid_split, 1)
                    dve.wait_ge(hid_split, c * FC + f * 2 + b + 1)
                    v.tensor_tensor(hid_lo_f[:, bass.ds(at, T)], mlp_b[:, :], hid_hi_f[:, bass.ds(at, T)].bitcast(F32),
                                    ALU.subtract).then_inc(hid_ready, 1)
            with dve.Fori(0, KT // 2) as m:
                for b in range(2):
                    dve.wait_ge(slab_used, c * SLABS_CHUNK + m * 2 + (S_MLP + 2 * FC + b + 1))
                    tile = halves(h_f[:, bass.ds((m * 2 + b) * T, T)])
                    v.tensor_tensor(tile, acc_pair(b), tile, ALU.add).then_inc(group_out, 1)

        with dve.Fori(0, CHUNKS) as c:
            chunk(c)
        rsqrt(4, rb)
        for k in range(KT):
            v.scalar_tensor_tensor(h_res[:, k, :], h_res[:, k, :], col("g_fin", k), rb[:, :], ALU.mult, ALU.mult)\
                .then_inc(y_ready, 1)

    return ctx


def _rel_bucket(n):
    exact = BUCKETS // 2
    if n < exact:
        return n
    large = exact + int(np.float32(np.log(np.float32(n) / exact)) / np.float32(np.log(WINDOW / exact)) * (BUCKETS - exact))
    return min(large, BUCKETS - 1)


_IN = ["weights", "x_t", "params", "consts", "rel_bias", "onehot", "gy_mask", "w_gates", "cache_kt", "cache_v",
       "cache_k_rows", "cache_v_rows"]
_OUT = [("y_t", (KT, P, T)), ("kv_t", (P, 2 * KV, WINDOW + TS)), ("conv_o", (P, NB, 9, HIST)), ("lru_o", (P, NB, 9)),
        ("keep_k", (DEC_B, WINDOW - DEC_T, KV * P)), ("keep_v", (DEC_B, WINDOW - DEC_T, KV * P))]


def kernel(x_prompt, x_sample, cache_k_win, cache_v_win, state_conv, state_lru, meta_tokens, norm_mix_g, w_in, conv_w,
           conv_b, w_gate_a, b_gate_a, w_gate_x, b_gate_x, lru_lambda, attn_sinks, rel_bias, attn_out_g, rec_out_g,
           w_out, norm_mlp_g, w_up, w_down, final_norm_g):
    import concourse.bacc as bacc
    from concourse.bass_utils import run_bass_kernel_spmd

    A = np.asarray
    c = np.ascontiguousarray

    def tiles(w):
        k, m = w.shape
        return w.reshape(k // P, P, m // P, P).transpose(0, 2, 1, 3)

    def slab_rows(t, ks, m):
        return t[ks, m].transpose(1, 0, 2).reshape(1, P, SLAB)

    w_i, w_o, w_u, w_d = (tiles(A(w)[0]) for w in (w_in, w_out, w_up, w_down))
    n_att = HEADS + 2 * KV
    lo8, hi8 = list(range(8)), list(range(8, 16))
    slabs = []
    order = [m for n in range(NB) for m in (n_att + n, n_att + NB + n)]
    order += list(range(HEADS, n_att)) + list(range(HEADS))
    for m in order:
        slabs += [slab_rows(w_i, lo8, m), slab_rows(w_i, hi8, m)]
    slabs += [slab_rows(w_o, hi8, 0), slab_rows(w_o, hi8, 1), slab_rows(w_o, lo8, 0), slab_rows(w_o, lo8, 1)]
    for m in range(2, KT):
        slabs += [slab_rows(w_o, hi8, m), slab_rows(w_o, lo8, m)]
    for ch in range(CHUNKS):
        for f in range(FC):
            slabs += [slab_rows(w_u, lo8, ch * FC + f), slab_rows(w_u, hi8, ch * FC + f)]
        for m in range(KT):
            slabs.append(slab_rows(w_d, list(range(ch * FC, ch * FC + FC)), m))
    weights = c(np.concatenate(slabs))
    assert weights.shape[0] == SLABS

    xs = A(x_sample).reshape(TS, D_MODEL)
    x_t = c(np.concatenate([A(meta_tokens), A(x_prompt)[0], xs]).T)

    def per_channel(a):
        a = A(a)
        a = a.reshape(-1, a.shape[-1] // P, P)
        return a.transpose(2, 0, 1).reshape(P, -1)

    h0 = np.zeros((P, NB, DEC_B, HIST), np.float32)
    h0[..., HIST - 1] = A(state_lru)[0].reshape(DEC_B, NB, P).transpose(2, 1, 0)
    hist = np.zeros((P, NB + 1, DEC_B, HIST), np.float32)
    hist[:, :NB] = A(state_conv)[0].reshape(DEC_B, HIST, NB, P).transpose(3, 2, 0, 1)
    sinks = A(attn_sinks)[0]
    sink_s = np.broadcast_to(sinks.reshape(1, KV, GQ, 1), (4, KV, GQ, DEC_T)).transpose(0, 2, 3, 1).reshape(P, KV)
    parts = {"g_mix": per_channel(norm_mix_g), "conv_w": per_channel(A(conv_w)[0]), "conv_b": per_channel(conv_b),
             "b_a": per_channel(b_gate_a), "b_x": per_channel(b_gate_x), "lam": per_channel(lru_lambda),
             "g_att": per_channel(attn_out_g), "g_rec": per_channel(rec_out_g), "g_mlp": per_channel(norm_mlp_g),
             "g_fin": per_channel(A(final_norm_g)[None]), "sink_p": np.broadcast_to(sinks, (P, HEADS)),
             "sink_s": sink_s, "h0": h0.reshape(P, -1), "hist": hist.reshape(P, -1)}
    params = c(np.concatenate([parts[n] for n, _ in _COLS], axis=1))

    onehot = np.zeros((BUCKETS, GY), np.float32)
    gy_mask = np.full((HEADS, GY), MASKED, np.float32)
    for y in range(GY):
        d = 2 * P - 1 - y
        if 0 <= d < WINDOW:
            onehot[_rel_bucket(d), y] = 1.0
            gy_mask[:, y] = 0.0
    consts = c(np.stack([np.eye(P, dtype=np.float32), np.ones((P, P), np.float32)], axis=1))
    gw = np.stack([A(w_gate_a)[0], A(w_gate_x)[0]], axis=2)
    w_gates = c(np.concatenate([gw, gw[:1]]))

    kc, vc = A(cache_k_win)[0], A(cache_v_win)[0]
    arrays = {
        "weights": weights, "x_t": x_t, "params": params, "consts": consts, "rel_bias": c(A(rel_bias)),
        "onehot": onehot, "gy_mask": gy_mask, "w_gates": w_gates,
        "cache_kt": c(kc.transpose(3, 0, 2, 1)), "cache_v": c(vc.transpose(1, 0, 2, 3)),
        "cache_k_rows": c(kc.reshape(DEC_B, WINDOW, KV * P)[:, DEC_T:]),
        "cache_v_rows": c(vc.reshape(DEC_B, WINDOW, KV * P)[:, DEC_T:]),
    }
    nc = bacc.Bacc("TRN2", target_bir_lowering=False, num_devices=1)
    args = [nc.dram_tensor(n, arrays[n].shape, F32, kind="ExternalInput").ap() for n in _IN]
    args += [nc.dram_tensor(n, s, F32, kind="ExternalOutput").ap() for n, s in _OUT]
    hymba_layer(nc, *args).close()
    r = run_bass_kernel_spmd(nc, [arrays], core_ids=[0]).results[0]

    y = r["y_t"].reshape(D_MODEL, T).T
    y_prompt = c(y[META:TP]).reshape(1, SEQ, D_MODEL)
    y_sample = c(y[TP:]).reshape(DEC_B, DEC_T, D_MODEL)
    kvw = r["kv_t"]

    def windows(t):
        return c(t[:, :, :WINDOW].transpose(2, 1, 0)).reshape(1, 1, WINDOW, KV, P),             t[:, :, WINDOW:].transpose(2, 1, 0).reshape(DEC_B, DEC_T, KV, P)

    kp, ks = windows(kvw[:, :KV])
    vp, vs = windows(kvw[:, KV:])
    new_k = np.concatenate([r["keep_k"].reshape(DEC_B, WINDOW - DEC_T, KV, P), ks], axis=1)[None]
    new_v = np.concatenate([r["keep_v"].reshape(DEC_B, WINDOW - DEC_T, KV, P), vs], axis=1)[None]
    conv = r["conv_o"].transpose(2, 3, 1, 0).reshape(9, HIST, LRU_W)
    lru = r["lru_o"].transpose(2, 1, 0).reshape(9, LRU_W)
    return (y_prompt, y_sample, kp, vp, c(conv[:1])[None], c(lru[:1])[None], c(new_k), c(new_v),
            c(conv[1:])[None], c(lru[1:])[None])
```

```python
from contextlib import ExitStack

import numpy as np

import concourse.bass as bass
from concourse import mybir

F32 = mybir.dt.float32
F32R = mybir.dt.float32r
ALU = mybir.AluOpType
ACT = mybir.ActivationFunctionType
AX = mybir.AxisListType

P = 128
D_MODEL = 2048
SEQ = 512
META = 16
DEC_B = 8
DEC_T = 8
HEADS = 8
KV = 2
GQ = HEADS // KV
WINDOW = 128
LRU_W = 1024
NB = LRU_W // P
CONV_W = 4
HIST = CONV_W - 1
D_FF = 4 * D_MODEL
BUCKETS = 32
EPS = 1e-6

TP = META + SEQ
TS = DEC_B * DEC_T
T = TP + TS
HALF = T // 2
TA = T - META
HA = TA // 2
KT = D_MODEL // P
BANK = 512

SEQ_S = HIST + DEC_T
CONV_IN = HIST + TP + DEC_B * SEQ_S
LT = CONV_IN - HIST
LH = LT // 2
S0 = TP + HIST

SLAB_K = 8
SLAB = SLAB_K * P
RING = 4
RAW = 2
SLABS_REC = 2 * NB * 2
SLABS_QKV = (HEADS + 2 * KV) * 2
SLABS_IN = SLABS_REC + SLABS_QKV
SLABS_OUT = KT * 2
FC = 8
CHUNKS = D_FF // P // FC
SLABS_CHUNK = FC * 2 + KT
S_OUT = SLABS_IN
S_MLP = SLABS_IN + SLABS_OUT
SLABS = S_MLP + CHUNKS * SLABS_CHUNK
G_OUT = 2 * NB + HEADS + 2 * KV
G_MLP = G_OUT + KT
G_CHUNK = FC + KT

SCALE = 128 ** -0.5
MASKED = -1e30
GY = 384
GELU_C = float(np.sqrt(2.0 / np.pi))
GELU_K = 0.044715 ** 0.5

_COLS = [("g_mix", KT), ("conv_w", CONV_W * NB), ("conv_b", NB), ("b_a", NB), ("b_x", NB), ("lam", NB),
         ("g_att", HEADS), ("g_rec", NB), ("g_mlp", KT), ("g_fin", KT), ("sink_p", HEADS), ("sink_s", KV),
         ("h0", NB * DEC_B * HIST), ("hist", (NB + 1) * DEC_B * HIST)]
COL = {}
_at = 0
for _n, _w in _COLS:
    COL[_n] = (_at, _w)
    _at += _w
NPAR = _at

UNITS = [("prompt", i, g) for i in range(SEQ // P) for g in range(KV)] + [("sample", i, g) for i in range(2) for g in range(KV)]
NU = len(UNITS)
NU_PROMPT = SEQ // P * KV


def keys_of(i):
    if i == 0:
        return 0, META + P, [(0, META, 0), (1, P, META)]
    return META + (i - 1) * P, 2 * P, [(i, P, 0), (i + 1, P, P)]


class Steps:

    def __init__(self, eng, sem):
        self.eng, self.sem, self.base, self.k = eng, sem, 0, 0

    def loop(self, base):
        self.base, self.k = base, 0

    def __call__(self, ins):
        self.k += 1
        ins.then_inc(self.sem, 1)
        self.eng.wait_ge(self.sem, self.base + self.k)


def hymba_layer(nc, weights, x_t, params, consts, rel_bias, onehot, gy_mask, w_gates, cache_kt, cache_v,
                cache_k_rows, cache_v_rows, y_t, kv_t, conv_o, lru_o, keep_k, keep_v):
    ctx = ExitStack()
    gy_dram = nc.dram_tensor("gy_dram", [HEADS, P, GY], F32, kind="Internal")

    base = (nc.sbuf_base + 31) // 32 * 32
    TILE = T * 4
    top = [base]

    def region(size):
        at = top[0]
        top[0] = at + (size + 31) // 32 * 32
        return at

    def sb(name, shape, dt, offset):
        return nc.alloc_sbuf_tensor_at(name, [P] + shape, dt, offset=offset)

    def small(name, shape, dt=F32):
        return sb(name, shape, dt, region(4 * int(np.prod(shape))))

    reg_a = region(2 * KT * TILE)
    reg_x = region(KT * TILE)
    reg_h = region(KT * TILE)
    act_hi = sb("act_hi", [KT, T], F32R, reg_a)
    act_lo = sb("act_lo", [KT, T], F32R, reg_a + KT * TILE)
    w_raw = small("w_raw", [RAW, SLAB])
    w_hi = small("w_hi", [RING, SLAB_K, P], F32R)
    w_lo = small("w_lo", [RING, SLAB_K, P], F32R)
    par = small("par", [NPAR])
    con = small("con", [2, P])
    gate_w = small("gate_w", [2, P])
    rb = small("rb", [T])
    acc = small("acc", [T])
    sq = small("sq", [2, T])
    conv_out = small("conv_out", [NB, 9, HIST])
    lru_out = small("lru_out", [NB, 1 + DEC_B])
    sp2 = small("sp2", [NB])
    spt = small("spt", [4, NB])
    half_b = small("half_b", [2, NB])
    eps_t = small("eps_t", [1])
    mlp_a = small("mlp_a", [T])
    mlp_b = small("mlp_b", [T])
    rn = mlp_a
    stat = small("stat", [2, 6, GQ])
    assert top[0] <= nc.sbuf_usable_end, top[0] - nc.sbuf_usable_end
    ident, ones = con[:, 0, :], con[:, 1, :]

    x_raw = sb("x_raw", [KT, T], F32, reg_x)
    h_res = sb("h_res", [KT, T], F32, reg_x)
    xp = sb("xp", [CONV_IN], F32, reg_x)
    LB = (CONV_IN * 4 + 31) // 32 * 32
    xc = sb("xc", [LT], F32, reg_x + LB)
    t_a = sb("t_a", [LT], F32, reg_x + 2 * LB)
    t_x = sb("t_x", [LT], F32, reg_x + 3 * LB)
    t_r = sb("t_r", [LT], F32, reg_x + 4 * LB)
    t_s = sb("t_s", [LT], F32, reg_x + 5 * LB)
    gel = sb("gel", [TA], F32, reg_x + 6 * LB)
    gel_t = sb("gel_t", [TA], F32, reg_x + 7 * LB)
    hs = sb("hs", [LT], F32, reg_x + 8 * LB)
    kv = sb("kv", [2 * KV, T], F32, reg_x + 9 * LB)
    at = reg_x
    v_tok = sb("v_tok", [6, KV, P], F32, at)
    bias_s = sb("bias_s", [2, KV, P + TS], F32, at + 6144)
    q_s = sb("q_s", [KV, 2 * P], F32, at + 6144 + 3072)
    bias_p = sb("bias_p", [HEADS, 2 * P], F32, at + 6144 + 3072 + 2048)
    assert 6144 + 3072 + 2048 + 8192 <= 9 * LB and 9 * LB + 4 * TILE <= KT * TILE
    rec = sb("rec", [NB, T], F32, reg_h)
    q = sb("q", [HEADS, T], F32, reg_h + NB * TILE)
    ck = sb("ck", [DEC_B, KV, P], F32, reg_a)
    cv = sb("cv", [DEC_B, KV, P], F32, reg_a + 8192)
    probs = sb("probs", [2, GQ, 2 * P], F32, reg_a + KT * TILE)
    probs_t = sb("probs_t", [2, 2, GQ, P], F32, reg_a + KT * TILE + 8192)
    assert 16384 <= 8 * TILE
    hid_hi = sb("hid_hi", [FC, T], F32R, reg_h)
    hid_lo = sb("hid_lo", [FC, T], F32R, reg_h + FC * TILE)
    oneh = sb("oneh", [GY], F32, reg_h + NB * TILE)
    relb = sb("relb", [HEADS], F32, reg_h + NB * TILE + 4 * GY)
    gym = sb("gym", [GY], F32, reg_h + NB * TILE + 4 * GY + 32)
    gy = sb("gy", [GY], F32, reg_h + NB * TILE + 8 * GY + 32)

    ps = ctx.enter_context(nc.psum_tensor("ps", [P, 8, BANK], F32))

    def sem(name):
        return ctx.enter_context(nc.semaphore(name))

    raw_landed = [sem(f"raw_landed{i}") for i in range(RAW)]
    x_landed = [sem(f"x_landed{i}") for i in range(8)]
    h_landed = [sem(f"h_landed{i}") for i in range(4)]
    par_landed = sem("par_landed")
    con_landed = sem("con_landed")
    rel_landed = sem("rel_landed")
    gate_landed = sem("gate_landed")
    cache_landed = sem("cache_landed")
    gy_stored = sem("gy_stored")
    bias_landed = sem("bias_landed")
    hi_ready = sem("hi_ready")
    lo_ready = sem("lo_ready")
    slab_used = sem("slab_used")
    group_out = sem("group_out")
    xhi_ready = sem("xhi_ready")
    xlo_ready = sem("xlo_ready")
    x_squared = sem("x_squared")
    x_added = sem("x_added")
    sums_ready = sem("sums_ready")
    root_ready = sem("root_ready")
    rb_ready = sem("rb_ready")
    gy_ps_ready = sem("gy_ps_ready")
    gy_ready = sem("gy_ready")
    sp_exp = sem("sp_exp")
    sp_ready = sem("sp_ready")
    hist_ready = sem("hist_ready")
    pads_ready = sem("pads_ready")
    tap0_ready = sem("tap0_ready")
    conv_ready = sem("conv_ready")
    xr_kept = sem("xr_kept")
    gates_ready = sem("gates_ready")
    g_squared = sem("g_squared")
    g_poly = sem("g_poly")
    g_tanh = sem("g_tanh")
    tanh_a = sem("tanh_a")
    tanh_x = sem("tanh_x")
    tau_ready = sem("tau_ready")
    sqrt_ready = sem("sqrt_ready")
    rec_ready = sem("rec_ready")
    rec_squared = sem("rec_squared")
    rec_added = sem("rec_added")
    rec_scaled = sem("rec_scaled")
    vt_ready = sem("vt_ready")
    v_copied = sem("v_copied")
    qs_ready = sem("qs_ready")
    s_ready = sem("s_ready")
    negmax_ready = sem("negmax_ready")
    exp_ready = sem("exp_ready")
    probs_ready = sem("probs_ready")
    pt_ready = sem("pt_ready")
    pt_copied = sem("pt_copied")
    o_ready = sem("o_ready")
    o_copied = sem("o_copied")
    o_added = sem("o_added")
    att_scaled = sem("att_scaled")
    h_squared = sem("h_squared")
    h_added = sem("h_added")
    square_ready = sem("square_ready")
    hid_split = sem("hid_split")
    hid_ready = sem("hid_ready")
    y_ready = sem("y_ready")
    stored = sem("stored")
    dve_step = sem("dve_step")
    act_step = sem("act_step")
    pool_step = sem("pool_step")

    def col(name, i=0, n=1):
        a = COL[name][0]
        return par[:, a + i:a + i + n]

    def dcol(name, i):
        return par[:, bass.ds(i + COL[name][0], 1)]

    def acc_pair(b, width=HA):
        return ps[:, 2 * b:2 * b + 2, 0:width]

    def live(buf, k=None):
        return halves(buf[:, META:T] if k is None else buf[:, k, META:T])

    def live_at(flat, k):
        return flat[:, bass.ds(k * T + META, TA)]

    def sample(buf, at):
        return buf[:, at:at + DEC_B * SEQ_S].rearrange("p (b t) -> p b t", b=DEC_B)

    rec_f = rec[:, :, :].rearrange("p k t -> p (k t)")
    kv_f = kv[:, :, :].rearrange("p k t -> p (k t)")
    q_f = q[:, :, :].rearrange("p k t -> p (k t)")
    h_f = h_res[:, :, :].rearrange("p k t -> p (k t)")
    hid_hi_f = hid_hi[:, :, :].rearrange("p k t -> p (k t)")
    hid_lo_f = hid_lo[:, :, :].rearrange("p k t -> p (k t)")
    conv_f = conv_out[:, :, :, :].rearrange("p n s t -> p (n s t)")
    lru_f = lru_out[:, :, :].rearrange("p n s -> p (n s)")

    def halves(ap):
        return ap.rearrange("p (h n) -> p h n", h=2)

    block = ctx.enter_context(nc.Block())

    @block.sync
    def _(sp):
        def raw_load(i, slot, wait):
            if wait:
                sp.wait_ge(hi_ready, i * RAW + (slot - 1))
                sp.wait_ge(lo_ready, i * RAW + (slot - 1))
            sp.dma_start(w_raw[:, slot, :], weights_v[i, slot]).then_inc(raw_landed[slot], 16)

        weights_v = weights.rearrange("(i j) p n -> i j p n", j=RAW)

        x_v = x_t.rearrange("(k p) t -> p k t", p=P)
        sp.dma_start(x_raw[:, 0:2, :], x_v[:, 0:2, :]).then_inc(x_landed[0], 16)
        raw_load(0, 0, False)
        sp.dma_start(par[:, :], params).then_inc(par_landed, 16)
        sp.dma_start(con[:, :, :], consts).then_inc(con_landed, 16)
        for i in range(1, 8):
            sp.dma_start(x_raw[:, 2 * i:2 * i + 2, :], x_v[:, 2 * i:2 * i + 2, :]).then_inc(x_landed[i], 16)
            if i == 1:
                raw_load(0, 1, False)
        sp.dma_start(gate_w[:, :, :], w_gates[0]).then_inc(gate_landed, 16)
        sp.dma_start(oneh[0:BUCKETS, :], onehot).then_inc(rel_landed, 16)
        sp.dma_start(relb[0:BUCKETS, :], rel_bias).then_inc(rel_landed, 16)
        sp.dma_start(gym[0:HEADS, :], gy_mask).then_inc(rel_landed, 16)
        sp.dma_start(keep_k, cache_k_rows).then_inc(stored, 16)
        sp.dma_start(keep_v, cache_v_rows).then_inc(stored, 16)
        with sp.Fori(1, SLABS // RAW) as i:
            for j in range(RAW):
                raw_load(i, j, True)

        for m in range(KT):
            sp.wait_ge(y_ready, m + 1)
            sp.dma_start(y_t[m], h_res[:, m, META:T]).then_inc(stored, 16)
        sp.wait_ge(stored, 16 * (2 + KT + 3))

    @block.tensor
    def _(pe):
        def slab(s, slot, buf, hi, lo, k0, first, last, ready=None, meta=False):
            c0, width = (0, HALF) if meta else (META, HA)
            pe.wait_ge(hi_ready, s + 1)
            pe.wait_ge(lo_ready, s + 1)
            for k in range(SLAB_K):
                if ready is not None:
                    ready(k)
                wh, wl = w_hi[:, slot, k, :], w_lo[:, slot, k, :]
                for part, (w, act) in enumerate(((wh, hi), (wh, lo), (wl, hi))):
                    for half in range(2):
                        st = first and k == 0 and part == 0
                        en = last and k == SLAB_K - 1 and part == 2
                        ins = nc.tensor.matmul(ps[:, 2 * buf + half, 0:width], w,
                                               act[:, k0 + k, c0 + half * width:c0 + (half + 1) * width],
                                               start=st, stop=en)
                if k == SLAB_K - 1:
                    ins.then_inc(slab_used, 1)

        def group(g, s, slot, buf, hi, lo, ready=None, wait=True, meta=False):
            if wait:
                pe.wait_ge(group_out, g - 1)
            slab(s, slot, buf, hi, lo, 0, True, False, ready, meta)
            slab(s + 1, slot + 1, buf, hi, lo, 8, False, True, None if ready is None else (lambda k: ready(8 + k)), meta)

        def token_sums(src, meta=False, bank=4):
            c0, width = (0, HALF) if meta else (META, HA)
            for half in range(2):
                ins = nc.tensor.matmul(ps[:, bank + half, 0:width], ones,
                                       src[:, c0 + half * width:c0 + (half + 1) * width],
                                       start=True, stop=True)
            ins.then_inc(sums_ready, 1)

        def xready(k):
            pe.wait_ge(xhi_ready, k + 1)
            pe.wait_ge(xlo_ready, k + 1)

        def gates(n):
            pe.wait_ge(conv_ready, n + 1)
            pe.wait_ge(gate_landed, (n + 1) * 16)
            for gi in range(2):
                for half in range(2):
                    ins = nc.tensor.matmul(ps[:, 4 + 2 * gi + half, 0:LH], gate_w[:, gi, :],
                                           xc[:, half * LH:(half + 1) * LH], start=True, stop=True)
            ins.then_inc(gates_ready, 1)

        group(0, 0, 0, 0, act_hi, act_lo, ready=xready, wait=False, meta=True)
        group(1, 2, 2, 1, act_hi, act_lo, wait=False)
        pe.wait_ge(con_landed, 16)
        pe.wait_ge(x_added, KT)
        token_sums(acc, meta=True)
        pe.wait_ge(rel_landed, 48)
        nc.tensor.matmul(ps[0:HEADS, 6, 0:GY], relb[0:BUCKETS, :], oneh[0:BUCKETS, :],
                         start=True, stop=True).then_inc(gy_ps_ready, 1)
        pe.wait_ge(rb_ready, 1)
        pe.wait_ge(gy_ready, 1)
        gates(0)
        with pe.Fori(1, NB) as n:
            group(n * 2, n * 4, 0, 0, act_hi, act_lo, meta=True)
            group(n * 2 + 1, n * 4 + 2, 2, 1, act_hi, act_lo)
            gates(n)
        with pe.Fori(0, KV) as j:
            group(j * 2 + 2 * NB, j * 4 + SLABS_REC, 0, 0, act_hi, act_lo, meta=True)
            group(j * 2 + 2 * NB + 1, j * 4 + SLABS_REC + 2, 2, 1, act_hi, act_lo, meta=True)
        pe.wait_ge(rec_added, NB)
        token_sums(acc)
        pe.wait_ge(group_out, 2 * NB + 2 * KV)
        pe.wait_ge(root_ready, 2)
        for b in range(SEQ // P):
            for g in range(KV):
                i = b * KV + g
                nc.tensor.transpose(ps[:, 4 + i // 4, (i % 4) * P:(i % 4 + 1) * P],
                                    kv[:, KV + g, META + b * P:META + (b + 1) * P], ident)
        for g in range(KV):
            nc.tensor.transpose(ps[0:META, 6, g * P:(g + 1) * P], kv[:, KV + g, 0:META], ident)
        for g in range(KV):
            ins = nc.tensor.transpose(ps[0:TS, 7, g * P:(g + 1) * P], kv[:, KV + g, TP:T], ident)
        ins.then_inc(vt_ready, 1)
        with pe.Fori(KV, KV + HEADS // 2) as j:
            group(j * 2 + 2 * NB, j * 4 + SLABS_REC, 0, 0, act_hi, act_lo)
            group(j * 2 + 2 * NB + 1, j * 4 + SLABS_REC + 2, 2, 1, act_hi, act_lo)

        def scores(u):
            kind, i, g = UNITS[u]
            b0 = 4 + 2 * (u % 2)
            if u >= 2:
                pe.wait_ge(exp_ready, u - 1)
            if kind == "prompt":
                k0, nk, _ = keys_of(i)
                for h in range(GQ):
                    ins = nc.tensor.matmul(ps[:, b0 + h // 2, (h % 2) * 2 * P:(h % 2) * 2 * P + nk],
                                           q[:, g * GQ + h, META + i * P:META + (i + 1) * P], kv[:, g, k0:k0 + nk],
                                           start=True, stop=True)
            else:
                nc.tensor.matmul(ps[:, b0, P:P + TS], q_s[:, g, i * P:(i + 1) * P], kv[:, g, TP:T],
                                 start=True, stop=True)
                for b in range(4):
                    ins = nc.tensor.matmul(ps[32 * b:32 * b + 32, b0, 0:P],
                                           q_s[:, g, i * P + 32 * b:i * P + 32 * b + 32],
                                           ck[:, 4 * i + b, g, :], start=True, stop=True)
            ins.then_inc(s_ready, 1)

        def turned(u):
            kind, i, g = UNITS[u]
            pe.wait_ge(probs_ready, u + 1)
            if u >= 1:
                pe.wait_ge(pt_copied, u)
            if kind == "prompt":
                for kb, (_, rows, c) in enumerate(keys_of(i)[2]):
                    for h in range(GQ):
                        ins = nc.tensor.transpose(ps[0:rows, kb, h * P:(h + 1) * P],
                                                  probs[:, u % 2, h, c:c + rows], ident)
            else:
                nc.tensor.transpose(ps[:, 0, 0:P], probs[:, u % 2, 0, 0:P], ident)
                ins = nc.tensor.transpose(ps[0:TS, 1, 0:P], probs[:, u % 2, 0, P:P + TS], ident)
            ins.then_inc(pt_ready, 1)

        def weighted(u):
            kind, i, g = UNITS[u]
            ob = 2 + u % 2
            pe.wait_ge(pt_copied, u + 1)
            if u >= 2:
                pe.wait_ge(o_copied, u - 1)
            if kind == "prompt":
                for kb, (vb, rows, _) in enumerate(keys_of(i)[2]):
                    ins = nc.tensor.matmul(ps[:, ob, 0:GQ * P], v_tok[0:rows, vb, g, :],
                                           probs_t[0:rows, u % 2, kb, :, :], start=kb == 0, stop=kb == 1)
            else:
                nc.tensor.matmul(ps[:, ob, 0:P], v_tok[0:TS, 5, g, :], probs_t[0:TS, u % 2, 1, 0, :],
                                 start=True, stop=False, skip_group_check=True)
                for b in range(4):
                    ins = nc.tensor.matmul(ps[:, ob, 32 * b:32 * b + 32], cv[:, 4 * i + b, g, :],
                                           probs_t[:, u % 2, 0, 0, 32 * b:32 * b + 32],
                                           start=False, stop=b == 3, skip_group_check=True)
            ins.then_inc(o_ready, 1)

        pe.wait_ge(group_out, G_OUT)
        pe.wait_ge(v_copied, 3)
        scores(0)
        scores(1)
        for u in range(NU):
            if u + 2 == NU_PROMPT:
                pe.wait_ge(qs_ready, KV)
                pe.wait_ge(cache_landed, 32)
            turned(u)
            if u + 2 < NU:
                scores(u + 2)
            weighted(u)

        def rec_ready_k(k):
            pe.wait_ge(xhi_ready, KT + k + 1)
            pe.wait_ge(xlo_ready, KT + k + 1)

        def att_ready_k(k):
            pe.wait_ge(xhi_ready, KT + 8 + k + 1)
            pe.wait_ge(xlo_ready, KT + 8 + k + 1)

        pe.wait_ge(pt_copied, NU)
        slab(S_OUT, 0, 0, act_hi, act_lo, 8, True, False, rec_ready_k)
        pe.wait_ge(o_added, NU)
        token_sums(acc)
        pe.wait_ge(o_copied, NU)
        slab(S_OUT + 1, 1, 1, act_hi, act_lo, 8, True, False)
        slab(S_OUT + 2, 2, 0, act_hi, act_lo, 0, False, True, att_ready_k)
        slab(S_OUT + 3, 3, 1, act_hi, act_lo, 0, False, True)
        with pe.Fori(1, KT // 2) as j:
            for b in range(2):
                pe.wait_ge(group_out, j * 2 + G_OUT + b - 1)
                slab(j * 4 + S_OUT + 2 * b, 2 * b, b, act_hi, act_lo, 8, True, False)
                slab(j * 4 + S_OUT + 2 * b + 1, 2 * b + 1, b, act_hi, act_lo, 0, False, True)

        def hready(k):
            pe.wait_ge(xhi_ready, 2 * KT + k + 1)
            pe.wait_ge(xlo_ready, 2 * KT + k + 1)

        def up_pair(g, s, first=False):
            group(g, s, 0, 0, act_hi, act_lo, ready=hready if first else None)
            if first:
                pe.wait_ge(h_added, KT)
                token_sums(acc)
            group(g + 1, s + 2, 2, 1, act_hi, act_lo)

        def down_four(g, s, ready=None):
            for b in range(4):
                pe.wait_ge(group_out, g + b - 1)
                slab(s + b, b, b % 2, hid_hi, hid_lo, 0, True, True, ready if b == 0 else None)

        def chunk(c, first):
            if first:
                up_pair(G_MLP, S_MLP, True)
            with pe.Fori(1 if first else 0, FC // 2) as f:
                up_pair(c * G_CHUNK + f * 2 + G_MLP, c * SLABS_CHUNK + f * 4 + S_MLP)
            g1, s1 = c * G_CHUNK + (G_MLP + FC), c * SLABS_CHUNK + (S_MLP + 2 * FC)
            down_four(g1, s1, lambda k: pe.wait_ge(hid_ready, c * FC + k + 1))
            with pe.Fori(1, KT // 4) as m:
                down_four(g1 + m * 4, s1 + m * 4)

        chunk(0, True)
        with pe.Fori(1, CHUNKS) as c:
            chunk(c, False)
        pe.wait_ge(h_added, 2 * KT)
        token_sums(acc)

    @block.scalar
    def _(act):
        step = Steps(act, act_step)

        def w_high(s, slot, free=True):
            act.wait_ge(raw_landed[slot % RAW], s * 8 + (16 - 8 * (slot % RAW)))
            if free:
                act.wait_ge(slab_used, s - (RING - 1))
            nc.scalar.activation(w_hi[:, slot, :, :], w_raw[:, slot % RAW, :].rearrange("p (k n) -> p k n", k=SLAB_K),
                                 ACT.Copy).then_inc(hi_ready, 1)

        def root(n, width, dst, meta=False):
            act.wait_ge(sums_ready, n + 1)
            nc.scalar.activation(halves(dst[:, :]) if meta else live(dst), ps[:, 4:6, 0:HALF if meta else HA], ACT.Sqrt, bias=eps_t[:, :],
                                 scale=1.0 / width).then_inc(root_ready, 1)

        act.wait_ge(par_landed, 16)
        for k in range(KT):
            if k % 2 == 0:
                act.wait_ge(x_landed[k // 2], 16)
            nc.scalar.activation(act_hi[:, k, :], x_raw[:, k, :], ACT.Copy, scale=col("g_mix", k))\
                .then_inc(xhi_ready, 1)
            if k == 0:
                w_high(0, 0, False)
            if k == 4:
                w_high(1, 1, False)
            if k == 12:
                w_high(2, 2, False)
        for k in range(KT):
            if k >= 2:
                act.wait_ge(x_added, k - 1)
            nc.scalar.activation(sq[:, k % 2, :], x_raw[:, k, :], ACT.Square).then_inc(x_squared, 1)
        act.wait_ge(sp_exp, 1)
        nc.scalar.activation(spt[:, 1, :], spt[:, 0, :], ACT.Exp).then_inc(sp_exp, 1)
        w_high(3, 3, False)
        act.wait_ge(pads_ready, 1)
        root(0, D_MODEL, rb, True)
        act.wait_ge(gy_ready, 1)
        act.dma_start(gy_dram.ap(), gy[0:HEADS, :].rearrange("h (o y) -> h o y", o=1).to_broadcast([HEADS, P, GY])).then_inc(gy_stored, 16)

        def tap0(n):
            act.wait_ge(group_out, n * 2 + 1)
            act.wait_ge(hist_ready, n + 1)
            nc.scalar.activation(xc[:, :], xp[:, 0:LT], ACT.Identity, bias=dcol("conv_b", n),
                                 scale=dcol("conv_w", n)).then_inc(tap0_ready, 1)

        def square_rec(n):
            act.wait_ge(rec_ready, n + 1)
            act.wait_ge(rec_added, n)
            nc.scalar.activation(sq[:, 0, META:T], live_at(rec_f, n), ACT.Square).then_inc(rec_squared, 1)

        def gelu_and_gates(n):
            act.wait_ge(group_out, n * 2 + 2)
            nc.scalar.activation(gel_t[:, :], gel[:, :], ACT.Square, scale=GELU_K).then_inc(g_squared, 1)
            act.wait_ge(g_poly, n + 1)
            nc.scalar.activation(gel_t[:, :], gel_t[:, :], ACT.Tanh, scale=GELU_C).then_inc(g_tanh, 1)

        def gates(n):
            act.wait_ge(gates_ready, n + 1)
            nc.scalar.activation(t_a[:, :].rearrange("p (h n) -> p h n", h=2), ps[:, 4:6, 0:LH], ACT.Tanh,
                                 bias=half_b[:, 0, bass.ds(n, 1)], scale=0.5).then_inc(tanh_a, 1)
            nc.scalar.activation(t_x[:, :].rearrange("p (h n) -> p h n", h=2), ps[:, 6:8, 0:LH], ACT.Tanh,
                                 bias=half_b[:, 1, bass.ds(n, 1)], scale=0.5).then_inc(tanh_x, 1)
            act.wait_ge(tanh_a, n + 1)
            nc.scalar.activation(t_a[:, :], t_a[:, :], ACT.Tanh, bias=sp2[:, bass.ds(n, 1)],
                                 scale=sp2[:, bass.ds(n, 1)]).then_inc(tau_ready, 1)
            act.wait_ge(tau_ready, n + 1)
            nc.scalar.activation(t_s[:, :], t_a[:, :], ACT.Sqrt).then_inc(sqrt_ready, 1)

        with act.Fori(0, NB) as n:
            s = n * 4
            act.wait_ge(sp_ready, 1)

            def high(i):
                w_high(s + i, i % RING)
            high(4)
            high(5)
            tap0(n)
            high(6)
            gelu_and_gates(n)
            high(7)
            gates(n)
            act.dma_start(gate_w[:, :, :], w_gates[n + 1]).then_inc(gate_landed, 16)
            square_rec(n)

        with act.Fori(SLABS_REC // 4, SLABS_REC // 4 + KV) as j:
            for i in range(4):
                w_high(j * 4 + 4 + i, i)
        act.wait_ge(rec_added, NB)
        root(1, LRU_W, rn)
        act.wait_ge(vt_ready, 1)
        nc.scalar.activation(v_tok[:, 1:5, :, :].rearrange("p b g d -> p (b g d)").rearrange("p (c n) -> p c n", c=2),
                             ps[:, 4:6, :], ACT.Copy).then_inc(v_copied, 1)
        nc.scalar.activation(v_tok[0:META, 0, :, :], ps[0:META, 6, 0:KV * P].rearrange("p (g d) -> p g d", g=KV),
                             ACT.Copy).then_inc(v_copied, 1)
        nc.scalar.activation(v_tok[0:TS, 5, :, :], ps[0:TS, 7, 0:KV * P].rearrange("p (g d) -> p g d", g=KV),
                             ACT.Copy).then_inc(v_copied, 1)
        act.wait_ge(xr_kept, NB)
        act.dma_start(conv_o, conv_out[:, :, :, :]).then_inc(stored, 16)
        act.wait_ge(rec_ready, NB)
        act.dma_start(lru_o, lru_out[:, :, :]).then_inc(stored, 16)
        act.dma_start(kv_t, kv[:, :, TP - WINDOW:T]).then_inc(stored, 16)
        act.wait_ge(gy_stored, 16)
        act.dma_start(bias_p[:, :, :], bass.AP(gy_dram, P - 1, [[GY - 1, P], [P * GY, HEADS], [1, 2 * P]]))\
            .then_inc(bias_landed, 16)
        act.wait_ge(pads_ready, 2)
        for g in range(KV):
            for b in range(4):
                for i in range(2):
                    act.dma_start(bias_s[32 * b:32 * b + 32, i, g, 0:P],
                                  bass.AP(gy_dram, g * GQ * P * GY + P - 1, [[P * GY, GQ], [GY - 1, DEC_T], [1, P]]))\
                        .then_inc(bias_landed, 16)
                    act.dma_start(bias_s[32 * b:32 * b + 32, i, g, P + DEC_T * (4 * i + b):P + DEC_T * (4 * i + b + 1)],
                                  bass.AP(gy_dram, g * GQ * P * GY + 2 * P - 1, [[P * GY, GQ], [GY - 1, DEC_T], [1, DEC_T]]))\
                        .then_inc(bias_landed, 16)
        with act.Fori(SLABS_REC // 4 + KV, SLABS_IN // 4) as j:
            for i in range(3):
                w_high(j * 4 + 4 + i, i)
            w_high(j * 4 + 7, 3)
        act.wait_ge(slab_used, SLABS_IN)
        act.dma_start(ck[:, :, :, :], cache_kt).then_inc(cache_landed, 16)
        act.dma_start(cv[:, :, :, :], cache_v).then_inc(cache_landed, 16)

        def exps(u):
            kind, i, g = UNITS[u]
            act.wait_ge(negmax_ready, u + 1)
            if kind == "prompt":
                nk = keys_of(i)[1]
                nc.scalar.activation(stat[:, u % 2, 4, :], stat[:, u % 2, 2, :], ACT.Exp).then_inc(act_step, 1)
                for h in range(GQ):
                    ins = nc.scalar.activation(probs[:, u % 2, h, 0:nk], probs[:, u % 2, h, 0:nk], ACT.Exp,
                                               bias=stat[:, u % 2, 1, h:h + 1], accum_out=stat[:, u % 2, 3, h:h + 1])
                    if h < GQ - 1:
                        ins.then_inc(act_step, 1)
            else:
                nc.scalar.activation(stat[:, u % 2, 4, 0:1], stat[:, u % 2, 2, 0:1], ACT.Exp).then_inc(act_step, 1)
                ins = nc.scalar.activation(probs[:, u % 2, 0, 0:P + TS], probs[:, u % 2, 0, 0:P + TS], ACT.Exp,
                                           bias=stat[:, u % 2, 1, 0:1], accum_out=stat[:, u % 2, 3, 0:1])
            ins.then_inc(exp_ready, 1)

        def pt_copy(u):
            kind, i, g = UNITS[u]
            act.wait_ge(pt_ready, u + 1)
            if u >= 2:
                act.wait_ge(o_ready, u - 1)
            if kind == "prompt" and i > 0:
                nc.scalar.activation(probs_t[:, u % 2, :, :, :], ps[:, 0:2, :].rearrange("p c (h n) -> p c h n", h=GQ),
                                     ACT.Copy).then_inc(pt_copied, 1)
            elif kind == "prompt":
                nc.scalar.activation(probs_t[0:META, u % 2, 0, :, :], ps[0:META, 0, :].rearrange("p (h n) -> p h n", h=GQ),
                                     ACT.Copy).then_inc(act_step, 1)
                nc.scalar.activation(probs_t[:, u % 2, 1, :, :], ps[:, 1, :].rearrange("p (h n) -> p h n", h=GQ),
                                     ACT.Copy).then_inc(pt_copied, 1)
            else:
                nc.scalar.activation(probs_t[:, u % 2, 0, 0, :], ps[:, 0, 0:P], ACT.Copy).then_inc(act_step, 1)
                nc.scalar.activation(probs_t[0:TS, u % 2, 1, 0, :], ps[0:TS, 1, 0:P], ACT.Copy).then_inc(pt_copied, 1)

        act.wait_ge(rec_scaled, NB)
        for u in range(NU + 1):
            if u < NU:
                exps(u)
            if u < NB:
                nc.scalar.activation(act_hi[:, 8 + u, META:T], rec[:, u, META:T], ACT.Copy).then_inc(xhi_ready, 1)
            if u >= 1:
                pt_copy(u - 1)
        act.wait_ge(s_ready, NU)
        act.wait_ge(o_ready, NU)
        act.wait_ge(negmax_ready, NU)
        act.wait_ge(stored, 16 * 5)
        x_v = x_t.rearrange("(k p) t -> p k t", p=P)
        for i in range(4):
            act.dma_start(h_res[:, 4 * i:4 * i + 4, META:T], x_v[:, 4 * i:4 * i + 4, META:T]).then_inc(h_landed[i], 16)
        root(2, LRU_W, rn)
        for k in range(HEADS):
            act.wait_ge(att_scaled, k + 1)
            nc.scalar.activation(act_hi[:, k, META:T], q[:, k, META:T], ACT.Copy).then_inc(xhi_ready, 1)

        def high_and_square(j):
            for b in range(2):
                w_high(j * 4 + S_OUT + 4 + 2 * b, 2 * b)
                w_high(j * 4 + S_OUT + 4 + 2 * b + 1, 2 * b + 1)
                act.wait_ge(group_out, j * 2 + G_OUT + b + 1)
                if isinstance(j, int) and j == 0:
                    nc.scalar.activation(sq[:, b, META:T], h_res[:, b, META:T], ACT.Square).then_inc(h_squared, 1)
                else:
                    act.wait_ge(h_added, j * 2 + b - 1)
                    nc.scalar.activation(sq[:, b, META:T], live_at(h_f, j * 2 + b), ACT.Square)\
                        .then_inc(h_squared, 1)

        high_and_square(0)
        with act.Fori(1, KT // 2) as j:
            high_and_square(j)
        for k in range(KT):
            nc.scalar.activation(act_hi[:, k, META:T], h_res[:, k, META:T], ACT.Copy, scale=col("g_mlp", k)).then_inc(xhi_ready, 1)
        root(3, D_MODEL, rb)

        def square_hid(g):
            act.wait_ge(group_out, g + 1)
            nc.scalar.activation(mlp_b[:, META:T], mlp_a[:, META:T], ACT.Square).then_inc(square_ready, 1)

        def chunk(c, last):
            s = c * SLABS_CHUNK + S_MLP
            with act.Fori(0, FC // 2) as f:
                for b in range(2):
                    w_high(s + f * 4 + 4 + 2 * b, 2 * b)
                    w_high(s + f * 4 + 4 + 2 * b + 1, 2 * b + 1)
                    square_hid(c * G_CHUNK + f * 2 + (G_MLP + b))
            if not last:
                with act.Fori(0, KT // 4) as m:
                    for b in range(4):
                        w_high(s + m * 4 + 2 * FC + 4 + b, b)
            else:
                for m in range(KT):
                    if m + 4 < KT:
                        w_high(SLABS - KT + m + 4, m % 4)
                    act.wait_ge(group_out, G_MLP + CHUNKS * G_CHUNK - KT + m + 1)
                    act.wait_ge(h_added, KT + m - 1)
                    nc.scalar.activation(sq[:, m % 2, META:T], h_res[:, m, META:T], ACT.Square).then_inc(h_squared, 1)

        with act.Fori(0, CHUNKS - 1) as c:
            chunk(c, False)
        chunk(CHUNKS - 1, True)
        root(4, D_MODEL, rb)

    @block.gpsimd
    def _(pool):
        step = Steps(pool, pool_step)

        def w_low(s, slot, free=True):
            pool.wait_ge(raw_landed[slot % RAW], s * 8 + (16 - 8 * (slot % RAW)))
            pool.wait_ge(hi_ready, s + 1)
            if free:
                pool.wait_ge(slab_used, s - (RING - 1))
            nc.gpsimd.tensor_tensor(w_lo[:, slot, :, :], w_raw[:, slot % RAW, :].rearrange("p (k n) -> p k n", k=SLAB_K),
                                    w_hi[:, slot, :, :].bitcast(F32), ALU.subtract).then_inc(lo_ready, 1)

        pool.memset(eps_t[:, :], EPS).then_inc(pads_ready, 1)
        for s in range(4):
            w_low(s, s, False)

        def history(n):
            a = COL["hist"][0]
            nc.gpsimd.tensor_copy(sample(xp, S0)[:, :, 0:HIST],
                                  par[:, bass.ds(n * (DEC_B * HIST) + a, DEC_B * HIST)].rearrange(
                                      "p (b t) -> p b t", b=DEC_B)).then_inc(hist_ready, 1)

        pool.wait_ge(par_landed, 16)
        pool.wait_ge(x_squared, KT)
        pool.wait_ge(xlo_ready, KT)
        step(nc.gpsimd.memset(xp[:, 0:HIST], 0.0))
        a = COL["hist"][0]
        nc.gpsimd.tensor_copy(sample(xp, S0)[:, :, 0:HIST],
                              par[:, a:a + DEC_B * HIST].rearrange("p (b t) -> p b t", b=DEC_B)).then_inc(hist_ready, 1)

        def kept(n):
            pool.wait_ge(conv_ready, n + 1)
            nc.gpsimd.tensor_copy(conv_f[:, bass.ds(n * 9 * HIST, HIST)], xp[:, TP:TP + HIST]).then_inc(pool_step, 1)
            nc.gpsimd.tensor_copy(conv_f[:, bass.ds(n * 9 * HIST + HIST, DEC_B * HIST)].rearrange("p (b t) -> p b t", b=DEC_B),
                                  sample(xp, S0)[:, :, DEC_T:SEQ_S]).then_inc(xr_kept, 1)
            pool.wait_ge(xr_kept, n + 1)

        def add_rec(n, first):
            pool.wait_ge(rec_squared, n + 1)
            if first:
                pool.wait_ge(sums_ready, 1)
                nc.gpsimd.tensor_copy(acc[:, META:T], sq[:, 0, META:T]).then_inc(rec_added, 1)
            else:
                pool.wait_ge(rec_added, n)
                nc.gpsimd.tensor_tensor(acc[:, META:T], acc[:, META:T], sq[:, 0, META:T], ALU.add).then_inc(rec_added, 1)

        def rec_block(n, first):
            for i in (4, 5):
                w_low(n * 4 + i, i % RING)
            kept(n)
            history(n + 1)
            for i in (6, 7):
                w_low(n * 4 + i, i % RING)
            add_rec(n, first)

        rec_block(0, True)
        with pool.Fori(1, NB) as n:
            rec_block(n, False)

        with pool.Fori(SLABS_REC // 4, SLABS_REC // 4 + KV) as j:
            for i in range(4):
                w_low(j * 4 + 4 + i, i)
        pool.wait_ge(rec_ready, NB)
        pool.memset(bias_s[:, :, :, :], MASKED).then_inc(pads_ready, 1)
        with pool.Fori(SLABS_REC // 4 + KV, SLABS_IN // 4) as j:
            for i in range(4):
                w_low(j * 4 + 4 + i, i)

        pool.wait_ge(group_out, G_OUT)
        for g in range(KV):
            nc.gpsimd.tensor_copy(
                q_s[:, g, :].rearrange("p (b h t) -> p b h t", b=DEC_B, h=GQ),
                q[:, g * GQ:(g + 1) * GQ, TP:T].rearrange("p h (b t) -> p b h t", b=DEC_B)).then_inc(qs_ready, 1)
        step.loop(step.k + NB)
        pool.wait_ge(sums_ready, 2)
        for u in range(NU):
            if u < NB:
                pool.wait_ge(xhi_ready, KT + u + 1)
                nc.gpsimd.tensor_tensor(act_lo[:, 8 + u, META:T], rec[:, u, META:T], act_hi[:, 8 + u, META:T].bitcast(F32),
                                        ALU.subtract).then_inc(xlo_ready, 1)
            kind, i, g = UNITS[u]
            pool.wait_ge(o_copied, u + 1)
            if kind == "prompt":
                c0, n = META + i * P, P
            else:
                c0, n = TP + 32 * i, 32
            o = q[:, g * GQ:(g + 1) * GQ, c0:c0 + n]
            s = sq[:, 0, 0:GQ * n].rearrange("p (h n) -> p h n", h=GQ)
            step(nc.gpsimd.tensor_tensor(s, o, o, ALU.mult))
            step(nc.gpsimd.tensor_tensor(s[:, 0:2, :], s[:, 0:2, :], s[:, 2:4, :], ALU.add))
            if g == 0:
                nc.gpsimd.tensor_tensor(acc[:, c0:c0 + n], s[:, 0, :], s[:, 1, :], ALU.add).then_inc(o_added, 1)
            else:
                step(nc.gpsimd.tensor_tensor(s[:, 0, :], s[:, 0, :], s[:, 1, :], ALU.add))
                nc.gpsimd.tensor_tensor(acc[:, c0:c0 + n], acc[:, c0:c0 + n], s[:, 0, :], ALU.add).then_inc(o_added, 1)
            pool.wait_ge(o_added, u + 1)

        def low_and_add(j):
            for b in range(2):
                w_low(j * 4 + S_OUT + 4 + 2 * b, 2 * b)
                w_low(j * 4 + S_OUT + 4 + 2 * b + 1, 2 * b + 1)
                pool.wait_ge(h_squared, j * 2 + b + 1)
                if isinstance(j, int) and b == 0:
                    pool.wait_ge(sums_ready, 3)
                    nc.gpsimd.tensor_copy(acc[:, META:T], sq[:, 0, META:T]).then_inc(h_added, 1)
                else:
                    pool.wait_ge(h_added, j * 2 + b)
                    nc.gpsimd.tensor_tensor(acc[:, META:T], acc[:, META:T], sq[:, b, META:T], ALU.add).then_inc(h_added, 1)

        low_and_add(0)
        with pool.Fori(1, KT // 2) as j:
            low_and_add(j)

        with pool.Fori(S_MLP // 4, (SLABS - KT) // 4) as j:
            for i in range(4):
                w_low(j * 4 + 4 + i, i)
        for m in range(KT):
            if m + 4 < KT:
                w_low(SLABS - KT + m + 4, m % 4)
            pool.wait_ge(h_squared, KT + m + 1)
            if m == 0:
                pool.wait_ge(sums_ready, 4)
                nc.gpsimd.tensor_copy(acc[:, META:T], sq[:, 0, META:T]).then_inc(h_added, 1)
            else:
                pool.wait_ge(h_added, KT + m)
                nc.gpsimd.tensor_tensor(acc[:, META:T], acc[:, META:T], sq[:, m % 2, META:T], ALU.add).then_inc(h_added, 1)

    @block.vector
    def _(dve):
        step = Steps(dve, dve_step)
        v = nc.vector

        def rsqrt(n, dst, c0=META):
            dve.wait_ge(root_ready, n + 1)
            v.reciprocal(dst[:, c0:T], dst[:, c0:T]).then_inc(rb_ready, 1)
            dve.wait_ge(rb_ready, n + 1)

        dve.wait_ge(par_landed, 16)
        for k in range(KT):
            dve.wait_ge(xhi_ready, k + 1)
            v.scalar_tensor_tensor(act_lo[:, k, :], x_raw[:, k, :], col("g_mix", k), act_hi[:, k, :].bitcast(F32),
                                   ALU.mult, ALU.subtract).then_inc(xlo_ready, 1)
        for k in range(KT):
            dve.wait_ge(x_squared, k + 1)
            if k == 0:
                v.tensor_copy(acc[:, :], sq[:, 0, :]).then_inc(x_added, 1)
            else:
                dve.wait_ge(x_added, k)
                v.tensor_tensor(acc[:, :], acc[:, :], sq[:, k % 2, :], ALU.add).then_inc(x_added, 1)
        step(v.tensor_scalar(spt[:, 2, :], col("lam", 0, NB), -1.0, None, ALU.mult))
        v.tensor_tensor(spt[:, 0, :], col("lam", 0, NB), spt[:, 2, :], ALU.min).then_inc(sp_exp, 1)
        dve.wait_ge(sp_exp, 2)
        step(v.tensor_scalar(spt[:, 3, :], spt[:, 1, :], 2.0, None, ALU.add))
        step(v.reciprocal(spt[:, 3, :], spt[:, 3, :]))
        step(v.tensor_tensor(spt[:, 1, :], spt[:, 1, :], spt[:, 3, :], ALU.mult))
        step(v.tensor_tensor(spt[:, 3, :], spt[:, 1, :], spt[:, 1, :], ALU.mult))
        step(v.memset(spt[:, 0, :], 1.0 / 17.0))
        for d in (15, 13, 11, 9, 7, 5, 3, 1):
            step(v.tensor_tensor(spt[:, 0, :], spt[:, 0, :], spt[:, 3, :], ALU.mult))
            step(v.tensor_scalar(spt[:, 0, :], spt[:, 0, :], 1.0 / d, None, ALU.add))
        step(v.tensor_tensor(spt[:, 0, :], spt[:, 0, :], spt[:, 1, :], ALU.mult))
        step(v.tensor_scalar(spt[:, 2, :], spt[:, 2, :], 0.0, 2.0, ALU.max, ALU.mult))
        step(v.scalar_tensor_tensor(sp2[:, :], spt[:, 0, :], 4.0, spt[:, 2, :], ALU.mult, ALU.add))
        step(v.tensor_scalar(half_b[:, 0, :], col("b_a", 0, NB), 0.5, None, ALU.mult))
        v.tensor_scalar(half_b[:, 1, :], col("b_x", 0, NB), 0.5, None, ALU.mult).then_inc(sp_ready, 1)
        rsqrt(0, rb, 0)
        dve.wait_ge(gy_ps_ready, 1)
        v.tensor_tensor(gy[0:HEADS, :], ps[0:HEADS, 6, 0:GY], gym[0:HEADS, :], ALU.add).then_inc(gy_ready, 1)

        STEPS_REC = 18
        first_base = step.k

        def rec_block(n):
            step.loop(n * STEPS_REC + first_base)
            dve.wait_ge(slab_used, n * 4 + 2)
            dve.wait_ge(hist_ready, n + 1)
            v.tensor_tensor(xp[:, HIST:HIST + HALF], ps[:, 0, 0:HALF], rb[:, 0:HALF], ALU.mult).then_inc(dve_step, 1)
            v.tensor_tensor(xp[:, HIST + HALF:HIST + TP], ps[:, 1, 0:TP - HALF], rb[:, HALF:TP], ALU.mult)\
                .then_inc(dve_step, 1)
            step.k += 2
            v.tensor_tensor(sample(xp, S0)[:, :, HIST:SEQ_S],
                            ps[:, 1, TP - HALF:HALF].rearrange("p (b t) -> p b t", b=DEC_B),
                            rb[:, TP:T].rearrange("p (b t) -> p b t", b=DEC_B), ALU.mult).then_inc(group_out, 1)
            dve.wait_ge(group_out, n * 2 + 1)
            dve.wait_ge(tap0_ready, n + 1)
            for j in range(1, CONV_W):
                ins = v.scalar_tensor_tensor(xc[:, :], xp[:, j:j + LT], dcol("conv_w", n + j * NB), xc[:, :],
                                             ALU.mult, ALU.add)
                if j < CONV_W - 1:
                    step(ins)
            ins.then_inc(conv_ready, 1)
            dve.wait_ge(slab_used, n * 4 + 4)
            v.tensor_tensor(halves(gel[:, :]), acc_pair(1), live(rb), ALU.mult).then_inc(group_out, 1)
            dve.wait_ge(g_squared, n + 1)
            v.scalar_tensor_tensor(gel_t[:, :], gel_t[:, :], 1.0, gel[:, :], ALU.add, ALU.mult).then_inc(g_poly, 1)
            dve.wait_ge(g_tanh, n + 1)
            step(v.scalar_tensor_tensor(gel[:, :], gel_t[:, :], 1.0, gel[:, :], ALU.add, ALU.mult))
            dve.wait_ge(tanh_x, n + 1)
            step(v.scalar_tensor_tensor(t_x[:, :], t_x[:, :], 1.0, xc[:, :], ALU.add, ALU.mult))
            dve.wait_ge(tau_ready, n + 1)
            step(v.tensor_scalar(t_r[:, :], t_a[:, :], 1.0, None, ALU.add))
            step(v.reciprocal(t_r[:, :], t_r[:, :]))
            dve.wait_ge(sqrt_ready, n + 1)
            step(v.tensor_scalar(t_a[:, :], t_r[:, :], 2.0, -1.0, ALU.mult, ALU.add))
            step(v.tensor_tensor(t_s[:, :], t_s[:, :], t_r[:, :], ALU.mult))
            step(v.memset(t_s[:, 0:1], 0.5))
            step(v.tensor_tensor(t_s[:, :], t_s[:, :], t_x[:, :], ALU.mult))
            pads = [sample(t, TP)[:, :, 0:HIST] for t in (t_a, t_s)]
            step(v.memset(pads[0], 0.0))
            step(v.tensor_copy(pads[1], par[:, bass.ds(n * (DEC_B * HIST) + COL["h0"][0], DEC_B * HIST)].rearrange(
                "p (b t) -> p b t", b=DEC_B)))
            step(v.tensor_tensor_scan(hs[:, :], t_a[:, :], t_s[:, :], 0.0, ALU.mult, ALU.add))
            v.tensor_copy(lru_f[:, bass.ds(n * 9, 1)], hs[:, TP - 1:TP]).then_inc(dve_step, 1)
            v.tensor_copy(lru_f[:, bass.ds(n * 9 + 1, DEC_B)], sample(hs, TP)[:, :, SEQ_S - 1]).then_inc(dve_step, 1)
            v.scalar_tensor_tensor(rec_f[:, bass.ds(n * T + META, SEQ)], gel[:, 0:SEQ], 0.5, hs[:, META:TP],
                                   ALU.mult, ALU.mult).then_inc(dve_step, 1)
            v.scalar_tensor_tensor(
                rec_f[:, bass.ds(n * T + TP, TS)].rearrange("p (b t) -> p b t", b=DEC_B),
                gel[:, SEQ:TA].rearrange("p (b t) -> p b t", b=DEC_B), 0.5,
                sample(hs, TP)[:, :, HIST:SEQ_S], ALU.mult, ALU.mult).then_inc(rec_ready, 1)
            step.k += 3
            dve.wait_ge(rec_ready, n + 1)
            assert step.k == STEPS_REC, step.k

        with dve.Fori(0, NB) as n:
            rec_block(n)
        step.base, step.k = first_base + NB * STEPS_REC, 0

        with dve.Fori(0, KV) as j:
            for b in range(2):
                dve.wait_ge(slab_used, j * 4 + SLABS_REC + 2 * b + 2)
                v.tensor_tensor(halves(kv_f[:, bass.ds((j * 2 + b) * T, T)]), acc_pair(b, HALF),
                                halves(rb[:, :]), ALU.mult).then_inc(group_out, 1)
        rsqrt(1, rn)
        with dve.Fori(0, NB) as n:
            tile = live_at(rec_f, n)
            v.scalar_tensor_tensor(tile, tile, dcol("g_rec", n), rn[:, META:T], ALU.mult, ALU.mult).then_inc(rec_scaled, 1)
        with dve.Fori(0, HEADS // 2) as j:
            for b in range(2):
                dve.wait_ge(slab_used, j * 4 + SLABS_REC + 4 * KV + 2 * b + 2)
                v.tensor_tensor(halves(live_at(q_f, j * 2 + b)), acc_pair(b), live(rb), ALU.mult).then_inc(group_out, 1)

        def unit_rows(u):
            kind, i, g = UNITS[u]
            return (keys_of(i)[1], slice(0, GQ)) if kind == "prompt" else (P + TS, slice(0, 1))

        def front(u):
            kind, i, g = UNITS[u]
            nk, hs_ = unit_rows(u)
            b0 = 4 + 2 * (u % 2)
            dve.wait_ge(s_ready, u + 1)
            if u >= 2:
                dve.wait_ge(pt_ready, u - 1)
            st = stat[:, u % 2]
            if kind == "prompt":
                off = 2 * P - nk
                s_in = ps[:, b0:b0 + 2, :].rearrange("p c (h n) -> p (c h) n", h=2)[:, :, 0:nk]
                bias, sink = bias_p[:, g * GQ:(g + 1) * GQ, off:off + nk], col("sink_p", g * GQ, GQ)
                dst = probs[:, u % 2, :, 0:nk]
            else:
                s_in, bias, sink = ps[:, b0, 0:nk], bias_s[:, i, g, :], col("sink_s", g)
                dst = probs[:, u % 2, 0, 0:nk]
            step(v.scalar_tensor_tensor(dst, s_in, SCALE, bias, ALU.mult, ALU.add))
            step(v.tensor_reduce(st[:, 0, hs_], dst, AX.X, ALU.max))
            step(v.tensor_tensor(st[:, 0, hs_], st[:, 0, hs_], sink, ALU.max))
            v.tensor_scalar(st[:, 1, hs_], st[:, 0, hs_], -1.0, None, ALU.mult).then_inc(dve_step, 1)
            step.k += 1
            v.tensor_tensor(st[:, 2, hs_], sink, st[:, 0, hs_], ALU.subtract).then_inc(negmax_ready, 1)

        def norm(u):
            kind, i, g = UNITS[u]
            nk, hs_ = unit_rows(u)
            st = stat[:, u % 2]
            dve.wait_ge(exp_ready, u + 1)
            step(v.tensor_tensor(st[:, 5, hs_], st[:, 3, hs_], st[:, 4, hs_], ALU.add))
            step(v.reciprocal(st[:, 5, hs_], st[:, 5, hs_]))
            if kind == "prompt":
                p = probs[:, u % 2, :, 0:nk]
                r = st[:, 5, :].rearrange("p (h o) -> p h o", o=1).to_broadcast([P, GQ, nk])
                v.tensor_tensor(p, p, r, ALU.mult).then_inc(probs_ready, 1)
            else:
                p = probs[:, u % 2, 0, 0:nk]
                v.tensor_scalar(p, p, st[:, 5, 0:1], None, ALU.mult).then_inc(probs_ready, 1)

        def out(u):
            kind, i, g = UNITS[u]
            dve.wait_ge(o_ready, u + 1)
            if kind == "prompt":
                v.tensor_copy(q[:, g * GQ:(g + 1) * GQ, META + i * P:META + (i + 1) * P],
                              ps[:, 2 + u % 2, 0:GQ * P].rearrange("p (h n) -> p h n", h=GQ)).then_inc(o_copied, 1)
            else:
                c0 = TP + 32 * i
                v.tensor_copy(q[:, g * GQ:(g + 1) * GQ, c0:c0 + 32].rearrange("p h (b t) -> p b h t", b=4),
                              ps[:, 2 + u % 2, 0:P].rearrange("p (b h t) -> p b h t", b=4, h=GQ)).then_inc(o_copied, 1)

        dve.wait_ge(bias_landed, 16 * (1 + 4 * 2 * 2 * KV))
        for u in range(NU + 2):
            if u < NU:
                front(u)
            if 1 <= u <= NU:
                norm(u - 1)
            if u >= 2:
                if u == 2 + NU_PROMPT:
                    dve.wait_ge(qs_ready, KV)
                out(u - 2)

        rsqrt(2, rn)
        v.scalar_tensor_tensor(q[:, 0, META:T], q[:, 0, META:T], col("g_att", 0), rn[:, META:T], ALU.mult, ALU.mult).then_inc(att_scaled, 1)
        for k in range(HEADS):
            if k + 1 < HEADS:
                v.scalar_tensor_tensor(q[:, k + 1, META:T], q[:, k + 1, META:T], col("g_att", k + 1), rn[:, META:T], ALU.mult, ALU.mult)\
                    .then_inc(att_scaled, 1)
            dve.wait_ge(att_scaled, k + 1)
            dve.wait_ge(xhi_ready, KT + NB + k + 1)
            v.tensor_tensor(act_lo[:, k, META:T], q[:, k, META:T], act_hi[:, k, META:T].bitcast(F32), ALU.subtract).then_inc(xlo_ready, 1)

        for i in range(4):
            dve.wait_ge(h_landed[i], 16)
        for b in range(2):
            dve.wait_ge(slab_used, S_OUT + 3 + b)
            v.tensor_tensor(live(h_res, b), acc_pair(b), live(h_res, b), ALU.add).then_inc(group_out, 1)
        with dve.Fori(1, KT // 2) as j:
            for b in range(2):
                dve.wait_ge(slab_used, j * 4 + S_OUT + 2 * b + 2)
                tile = halves(live_at(h_f, j * 2 + b))
                v.tensor_tensor(tile, acc_pair(b), tile, ALU.add).then_inc(group_out, 1)
        for k in range(KT):
            dve.wait_ge(xhi_ready, 2 * KT + k + 1)
            v.scalar_tensor_tensor(act_lo[:, k, META:T], h_res[:, k, META:T], col("g_mlp", k), act_hi[:, k, META:T].bitcast(F32),
                                   ALU.mult, ALU.subtract).then_inc(xlo_ready, 1)
        rsqrt(3, rb)

        def chunk(c):
            with dve.Fori(0, FC // 2) as f:
                for b in range(2):
                    dve.wait_ge(slab_used, c * SLABS_CHUNK + f * 4 + (S_MLP + 2 * b + 2))
                    v.scalar_tensor_tensor(live(mlp_a), acc_pair(b), 0.0, live(rb), ALU.max, ALU.mult)\
                        .then_inc(group_out, 1)
                    dve.wait_ge(square_ready, c * FC + f * 2 + b + 1)
                    hi, lo = live_at(hid_hi_f, f * 2 + b), live_at(hid_lo_f, f * 2 + b)
                    v.tensor_copy(hi, mlp_b[:, META:T]).then_inc(hid_split, 1)
                    dve.wait_ge(hid_split, c * FC + f * 2 + b + 1)
                    v.tensor_tensor(lo, mlp_b[:, META:T], hi.bitcast(F32), ALU.subtract).then_inc(hid_ready, 1)
            with dve.Fori(0, KT // 2) as m:
                for b in range(2):
                    dve.wait_ge(slab_used, c * SLABS_CHUNK + m * 2 + (S_MLP + 2 * FC + b + 1))
                    tile = halves(live_at(h_f, m * 2 + b))
                    v.tensor_tensor(tile, acc_pair(b), tile, ALU.add).then_inc(group_out, 1)

        with dve.Fori(0, CHUNKS) as c:
            chunk(c)
        rsqrt(4, rb)
        for k in range(KT):
            v.scalar_tensor_tensor(h_res[:, k, META:T], h_res[:, k, META:T], col("g_fin", k), rb[:, META:T], ALU.mult, ALU.mult)\
                .then_inc(y_ready, 1)

    return ctx


def _rel_bucket(n):
    exact = BUCKETS // 2
    if n < exact:
        return n
    large = exact + int(np.float32(np.log(np.float32(n) / exact)) / np.float32(np.log(WINDOW / exact)) * (BUCKETS - exact))
    return min(large, BUCKETS - 1)


_IN = ["weights", "x_t", "params", "consts", "rel_bias", "onehot", "gy_mask", "w_gates", "cache_kt", "cache_v",
       "cache_k_rows", "cache_v_rows"]
_OUT = [("y_t", (KT, P, TA)), ("kv_t", (P, 2 * KV, WINDOW + TS)), ("conv_o", (P, NB, 9, HIST)), ("lru_o", (P, NB, 9)),
        ("keep_k", (DEC_B, WINDOW - DEC_T, KV * P)), ("keep_v", (DEC_B, WINDOW - DEC_T, KV * P))]


def kernel(x_prompt, x_sample, cache_k_win, cache_v_win, state_conv, state_lru, meta_tokens, norm_mix_g, w_in, conv_w,
           conv_b, w_gate_a, b_gate_a, w_gate_x, b_gate_x, lru_lambda, attn_sinks, rel_bias, attn_out_g, rec_out_g,
           w_out, norm_mlp_g, w_up, w_down, final_norm_g):
    import concourse.bacc as bacc
    from concourse.bass_utils import run_bass_kernel_spmd

    A = np.asarray
    c = np.ascontiguousarray

    def tiles(w):
        k, m = w.shape
        return w.reshape(k // P, P, m // P, P).transpose(0, 2, 1, 3)

    def slab_rows(t, ks, m):
        return t[ks, m].transpose(1, 0, 2).reshape(1, P, SLAB)

    w_i, w_o, w_u, w_d = (tiles(A(w)[0]) for w in (w_in, w_out, w_up, w_down))
    n_att = HEADS + 2 * KV
    lo8, hi8 = list(range(8)), list(range(8, 16))
    slabs = []
    order = [m for n in range(NB) for m in (n_att + n, n_att + NB + n)]
    order += list(range(HEADS, n_att)) + list(range(HEADS))
    for m in order:
        slabs += [slab_rows(w_i, lo8, m), slab_rows(w_i, hi8, m)]
    slabs += [slab_rows(w_o, hi8, 0), slab_rows(w_o, hi8, 1), slab_rows(w_o, lo8, 0), slab_rows(w_o, lo8, 1)]
    for m in range(2, KT):
        slabs += [slab_rows(w_o, hi8, m), slab_rows(w_o, lo8, m)]
    for ch in range(CHUNKS):
        for f in range(FC):
            slabs += [slab_rows(w_u, lo8, ch * FC + f), slab_rows(w_u, hi8, ch * FC + f)]
        for m in range(KT):
            slabs.append(slab_rows(w_d, list(range(ch * FC, ch * FC + FC)), m))
    weights = c(np.concatenate(slabs))
    assert weights.shape[0] == SLABS

    xs = A(x_sample).reshape(TS, D_MODEL)
    x_t = c(np.concatenate([A(meta_tokens), A(x_prompt)[0], xs]).T)

    def per_channel(a):
        a = A(a)
        a = a.reshape(-1, a.shape[-1] // P, P)
        return a.transpose(2, 0, 1).reshape(P, -1)

    h0 = np.zeros((P, NB, DEC_B, HIST), np.float32)
    h0[..., HIST - 1] = A(state_lru)[0].reshape(DEC_B, NB, P).transpose(2, 1, 0)
    hist = np.zeros((P, NB + 1, DEC_B, HIST), np.float32)
    hist[:, :NB] = A(state_conv)[0].reshape(DEC_B, HIST, NB, P).transpose(3, 2, 0, 1)
    sinks = A(attn_sinks)[0]
    sink_s = np.broadcast_to(sinks.reshape(1, KV, GQ, 1), (4, KV, GQ, DEC_T)).transpose(0, 2, 3, 1).reshape(P, KV)
    parts = {"g_mix": per_channel(norm_mix_g), "conv_w": per_channel(A(conv_w)[0]), "conv_b": per_channel(conv_b),
             "b_a": per_channel(b_gate_a), "b_x": per_channel(b_gate_x), "lam": per_channel(lru_lambda),
             "g_att": per_channel(attn_out_g), "g_rec": per_channel(rec_out_g), "g_mlp": per_channel(norm_mlp_g),
             "g_fin": per_channel(A(final_norm_g)[None]), "sink_p": np.broadcast_to(sinks, (P, HEADS)),
             "sink_s": sink_s, "h0": h0.reshape(P, -1), "hist": hist.reshape(P, -1)}
    params = c(np.concatenate([parts[n] for n, _ in _COLS], axis=1))

    onehot = np.zeros((BUCKETS, GY), np.float32)
    gy_mask = np.full((HEADS, GY), MASKED, np.float32)
    for y in range(GY):
        d = 2 * P - 1 - y
        if 0 <= d < WINDOW:
            onehot[_rel_bucket(d), y] = 1.0
            gy_mask[:, y] = 0.0
    consts = c(np.stack([np.eye(P, dtype=np.float32), np.ones((P, P), np.float32)], axis=1))
    gw = np.stack([A(w_gate_a)[0], A(w_gate_x)[0]], axis=2)
    w_gates = c(np.concatenate([gw, gw[:1]]))

    kc, vc = A(cache_k_win)[0], A(cache_v_win)[0]
    arrays = {
        "weights": weights, "x_t": x_t, "params": params, "consts": consts, "rel_bias": c(A(rel_bias)),
        "onehot": onehot, "gy_mask": gy_mask, "w_gates": w_gates,
        "cache_kt": c(kc.transpose(3, 0, 2, 1)), "cache_v": c(vc.transpose(1, 0, 2, 3)),
        "cache_k_rows": c(kc.reshape(DEC_B, WINDOW, KV * P)[:, DEC_T:]),
        "cache_v_rows": c(vc.reshape(DEC_B, WINDOW, KV * P)[:, DEC_T:]),
    }
    nc = bacc.Bacc("TRN2", target_bir_lowering=False, num_devices=1)
    args = [nc.dram_tensor(n, arrays[n].shape, F32, kind="ExternalInput").ap() for n in _IN]
    args += [nc.dram_tensor(n, s, F32, kind="ExternalOutput").ap() for n, s in _OUT]
    hymba_layer(nc, *args).close()
    r = run_bass_kernel_spmd(nc, [arrays], core_ids=[0]).results[0]

    y = r["y_t"].reshape(D_MODEL, TA).T
    y_prompt = c(y[:SEQ]).reshape(1, SEQ, D_MODEL)
    y_sample = c(y[SEQ:]).reshape(DEC_B, DEC_T, D_MODEL)
    kvw = r["kv_t"]

    def windows(t):
        return c(t[:, :, :WINDOW].transpose(2, 1, 0)).reshape(1, 1, WINDOW, KV, P),             t[:, :, WINDOW:].transpose(2, 1, 0).reshape(DEC_B, DEC_T, KV, P)

    kp, ks = windows(kvw[:, :KV])
    vp, vs = windows(kvw[:, KV:])
    new_k = np.concatenate([r["keep_k"].reshape(DEC_B, WINDOW - DEC_T, KV, P), ks], axis=1)[None]
    new_v = np.concatenate([r["keep_v"].reshape(DEC_B, WINDOW - DEC_T, KV, P), vs], axis=1)[None]
    conv = r["conv_o"].transpose(2, 3, 1, 0).reshape(9, HIST, LRU_W)
    lru = r["lru_o"].transpose(2, 1, 0).reshape(9, LRU_W)
    return (y_prompt, y_sample, kp, vp, c(conv[:1])[None], c(lru[:1])[None], c(new_k), c(new_v),
            c(conv[1:])[None], c(lru[1:])[None])
```

```python
from contextlib import ExitStack

import numpy as np

import concourse.bass as bass
from concourse import mybir

F32 = mybir.dt.float32
F32R = mybir.dt.float32r
ALU = mybir.AluOpType
ACT = mybir.ActivationFunctionType
AX = mybir.AxisListType

P = 128
D_MODEL = 2048
SEQ = 512
META = 16
DEC_B = 8
DEC_T = 8
HEADS = 8
KV = 2
GQ = HEADS // KV
WINDOW = 128
LRU_W = 1024
NB = LRU_W // P
CONV_W = 4
HIST = CONV_W - 1
D_FF = 4 * D_MODEL
BUCKETS = 32
EPS = 1e-6

TP = META + SEQ
TS = DEC_B * DEC_T
T = TP + TS
HALF = T // 2
TA = T - META
HA = TA // 2
KT = D_MODEL // P
BANK = 512

SEQ_S = HIST + DEC_T
CONV_IN = HIST + TP + DEC_B * SEQ_S
LT = CONV_IN - HIST
LH = LT // 2
S0 = TP + HIST

SLAB_K = 8
SLAB = SLAB_K * P
RING = 4
RAW = 2
SLABS_REC = 2 * NB * 2
SLABS_QKV = (HEADS + 2 * KV) * 2
SLABS_IN = SLABS_REC + SLABS_QKV
SLABS_OUT = KT * 2
FC = 8
CHUNKS = D_FF // P // FC
SLABS_CHUNK = FC * 2 + KT
S_OUT = SLABS_IN
S_MLP = SLABS_IN + SLABS_OUT
SLABS = S_MLP + CHUNKS * SLABS_CHUNK
G_OUT = 2 * NB + HEADS + 2 * KV
G_MLP = G_OUT + KT
G_CHUNK = FC + KT
X_POOL = 5
NBLK = 5

SCALE = 128 ** -0.5
MASKED = -1e30
GY = 384
GELU_C = float(np.sqrt(2.0 / np.pi))
GELU_K = 0.044715 ** 0.5

_COLS = [("g_mix", KT), ("conv_w", CONV_W * NB), ("conv_b", NB), ("b_a", NB), ("b_x", NB), ("lam", NB),
         ("g_att", HEADS), ("g_rec", NB), ("g_mlp", KT), ("g_fin", KT), ("sink_p", HEADS), ("sink_s", KV),
         ("h0", NB * DEC_B * HIST), ("hist", (NB + 1) * DEC_B * HIST)]
COL = {}
_at = 0
for _n, _w in _COLS:
    COL[_n] = (_at, _w)
    _at += _w
NPAR = _at

UNITS = [("prompt", i, g) for g in range(KV) for i in range(SEQ // P)] + [("sample", i, g) for g in range(KV) for i in range(2)]
NU = len(UNITS)
NU_PROMPT = SEQ // P * KV


def keys_of(i):
    if i == 0:
        return 0, META + P, [(0, META, 0), (1, P, META)]
    return META + (i - 1) * P, 2 * P, [(i, P, 0), (i + 1, P, P)]


class Steps:

    def __init__(self, eng, sem):
        self.eng, self.sem, self.base, self.k = eng, sem, 0, 0

    def loop(self, base):
        self.base, self.k = base, 0

    def wait(self):
        self.eng.wait_ge(self.sem, self.base + self.k)

    def __call__(self, ins):
        self.k += 1
        ins.then_inc(self.sem, 1)
        self.wait()


def hymba_layer(nc, weights, x_t, params, consts, rel_bias, onehot, gy_mask, w_gates, cache_kt, cache_v,
                cache_k_rows, cache_v_rows, y_t, kv_t, conv_o, lru_o, keep_k, keep_v):
    ctx = ExitStack()
    gy_dram = nc.dram_tensor("gy_dram", [HEADS, P, GY], F32, kind="Internal")

    base = (nc.sbuf_base + 31) // 32 * 32
    TILE = T * 4
    top = [base]

    def region(size):
        at = top[0]
        top[0] = at + (size + 31) // 32 * 32
        return at

    def sb(name, shape, dt, offset):
        return nc.alloc_sbuf_tensor_at(name, [P] + shape, dt, offset=offset)

    def small(name, shape, dt=F32):
        return sb(name, shape, dt, region(4 * int(np.prod(shape))))

    reg_a = region(2 * KT * TILE)
    reg_x = region(KT * TILE)
    reg_h = region(KT * TILE)
    act_hi = sb("act_hi", [KT, T], F32R, reg_a)
    act_lo = sb("act_lo", [KT, T], F32R, reg_a + KT * TILE)
    w_raw = small("w_raw", [RAW, SLAB])
    w_hi = small("w_hi", [RING, SLAB_K, P], F32R)
    w_lo = small("w_lo", [RING, SLAB_K, P], F32R)
    par = small("par", [NPAR])
    con = small("con", [2, P])
    gate_w = small("gate_w", [2, P])
    rb = small("rb", [T])
    acc = small("acc", [T])
    sq = small("sq", [2, T])
    conv_out = small("conv_out", [NB, 9, HIST])
    lru_out = small("lru_out", [NB, 1 + DEC_B])
    sp2 = small("sp2", [NB])
    spt = small("spt", [4, NB])
    half_b = small("half_b", [2, NB])
    mlp_a = small("mlp_a", [T])
    mlp_b = small("mlp_b", [T])
    rn = mlp_a
    diag = mlp_b
    nrm = small("nrm", [4, NBLK])
    stat = small("stat", [3, 6, GQ])
    assert top[0] <= nc.sbuf_usable_end, top[0] - nc.sbuf_usable_end
    ident, ones = con[:, 0, :], con[:, 1, :]

    x_raw = sb("x_raw", [KT, T], F32, reg_x)
    h_res = sb("h_res", [KT, T], F32, reg_x)
    xp = sb("xp", [CONV_IN], F32, reg_x)
    LB = (CONV_IN * 4 + 31) // 32 * 32
    xc = sb("xc", [LT], F32, reg_x + LB)
    t_a = sb("t_a", [LT], F32, reg_x + 2 * LB)
    t_x = sb("t_x", [LT], F32, reg_x + 3 * LB)
    t_r = sb("t_r", [LT], F32, reg_x + 4 * LB)
    t_s = sb("t_s", [LT], F32, reg_x + 5 * LB)
    gel = sb("gel", [TA], F32, reg_x + 6 * LB)
    gel_t = sb("gel_t", [TA], F32, reg_x + 7 * LB)
    hs = sb("hs", [LT], F32, reg_x + 8 * LB)
    kv = sb("kv", [2 * KV, T], F32, reg_x + (KT - 2 * KV) * TILE)
    at = reg_x
    v_tok = sb("v_tok", [6, KV, P], F32, at)
    bias_s = sb("bias_s", [2, KV, P + TS], F32, at + 6144)
    q_s = sb("q_s", [KV, 2 * P], F32, at + 6144 + 3072)
    bias_p = sb("bias_p", [HEADS, 2 * P], F32, at + 6144 + 3072 + 2048)
    assert 19456 + 8192 <= (KT - 2 * KV) * TILE and 9 * LB <= (KT - 2 * KV) * TILE
    rec = sb("rec", [NB, T], F32, reg_h)
    q = sb("q", [HEADS, T], F32, reg_h + NB * TILE)
    ck = sb("ck", [DEC_B, KV, P], F32, reg_a)
    cv = sb("cv", [DEC_B, KV, P], F32, reg_a + 8192)
    probs = [sb("probs0", [GQ, 2 * P], F32, at + 19456), sb("probs1", [GQ, 2 * P], F32, at + 19456 + 4096),
             sb("probs2", [GQ, 2 * P], F32, reg_a + KT * TILE)]
    probs_t = sb("probs_t", [2, GQ, P], F32, reg_a + KT * TILE + 4096)
    assert 16384 <= 8 * TILE
    hid_hi = sb("hid_hi", [FC, T], F32R, reg_h)
    hid_lo = sb("hid_lo", [FC, T], F32R, reg_h + FC * TILE)
    oneh = sb("oneh", [GY], F32, reg_h + NB * TILE)
    relb = sb("relb", [HEADS], F32, reg_h + NB * TILE + 4 * GY)
    gym = sb("gym", [GY], F32, reg_h + NB * TILE + 4 * GY + 32)
    gy = sb("gy", [GY], F32, reg_h + NB * TILE + 8 * GY + 32)

    ps = ctx.enter_context(nc.psum_tensor("ps", [P, 8, BANK], F32))

    def sem(name):
        return ctx.enter_context(nc.semaphore(name))

    raw_landed = [sem(f"raw_landed{i}") for i in range(RAW)]
    x_landed = [sem(f"x_landed{i}") for i in range(8)]
    h_landed = [sem(f"h_landed{i}") for i in range(4)]
    par_landed = sem("par_landed")
    con_landed = sem("con_landed")
    rel_landed = sem("rel_landed")
    gate_landed = sem("gate_landed")
    cache_landed = sem("cache_landed")
    gy_stored = sem("gy_stored")
    bias_landed = sem("bias_landed")
    hi_ready = sem("hi_ready")
    lo_ready = sem("lo_ready")
    slab_used = sem("slab_used")
    group_out = sem("group_out")
    xhi_ready = sem("xhi_ready")
    xlo_ready = sem("xlo_ready")
    x_squared = sem("x_squared")
    x_added = sem("x_added")
    sums_ready = sem("sums_ready")
    root_ready = sem("root_ready")
    var_ready = sem("var_ready")
    diag_ready = sem("diag_ready")
    spread_ready = sem("spread_ready")
    x_pool_summed = sem("x_pool_summed")
    sp_atanh = sem("sp_atanh")
    rb_ready = sem("rb_ready")
    gy_ps_ready = sem("gy_ps_ready")
    gy_ready = sem("gy_ready")
    sp_exp = sem("sp_exp")
    sp_ready = sem("sp_ready")
    hist_ready = sem("hist_ready")
    pads_ready = sem("pads_ready")
    tap0_ready = sem("tap0_ready")
    conv_ready = sem("conv_ready")
    xr_kept = sem("xr_kept")
    gates_ready = sem("gates_ready")
    g_squared = sem("g_squared")
    g_poly = sem("g_poly")
    g_tanh = sem("g_tanh")
    tanh_a = sem("tanh_a")
    tanh_x = sem("tanh_x")
    tau_ready = sem("tau_ready")
    sqrt_ready = sem("sqrt_ready")
    rec_ready = sem("rec_ready")
    rec_squared = sem("rec_squared")
    rec_added = sem("rec_added")
    rec_scaled = sem("rec_scaled")
    vt_ready = sem("vt_ready")
    v_copied = sem("v_copied")
    qs_ready = sem("qs_ready")
    s_ready = sem("s_ready")
    negmax_ready = sem("negmax_ready")
    exp_ready = sem("exp_ready")
    probs_ready = sem("probs_ready")
    pt_ready = sem("pt_ready")
    pt_copied = sem("pt_copied")
    o_ready = sem("o_ready")
    o_copied = sem("o_copied")
    o_added = sem("o_added")
    att_scaled = sem("att_scaled")
    h_squared = sem("h_squared")
    h_added = sem("h_added")
    square_ready = sem("square_ready")
    hid_split = sem("hid_split")
    hid_ready = sem("hid_ready")
    y_ready = sem("y_ready")
    stored = sem("stored")
    dve_step = sem("dve_step")
    act_step = sem("act_step")
    pool_step = sem("pool_step")

    def col(name, i=0, n=1):
        a = COL[name][0]
        return par[:, a + i:a + i + n]

    def dcol(name, i):
        return par[:, bass.ds(i + COL[name][0], 1)]

    def acc_pair(b, width=HA):
        return ps[:, 2 * b:2 * b + 2, 0:width]

    def live(buf, k=None):
        return halves(buf[:, META:T] if k is None else buf[:, k, META:T])

    def live_at(flat, k):
        return flat[:, bass.ds(k * T + META, TA)]

    def sample(buf, at):
        return buf[:, at:at + DEC_B * SEQ_S].rearrange("p (b t) -> p b t", b=DEC_B)

    rec_f = rec[:, :, :].rearrange("p k t -> p (k t)")
    kv_f = kv[:, :, :].rearrange("p k t -> p (k t)")
    q_f = q[:, :, :].rearrange("p k t -> p (k t)")
    h_f = h_res[:, :, :].rearrange("p k t -> p (k t)")
    hid_hi_f = hid_hi[:, :, :].rearrange("p k t -> p (k t)")
    hid_lo_f = hid_lo[:, :, :].rearrange("p k t -> p (k t)")
    conv_f = conv_out[:, :, :, :].rearrange("p n s t -> p (n s t)")
    lru_f = lru_out[:, :, :].rearrange("p n s -> p (n s)")

    def halves(ap):
        return ap.rearrange("p (h n) -> p h n", h=2)

    block = ctx.enter_context(nc.Block())

    @block.sync
    def _(sp):
        def raw_load(i, slot, wait):
            if wait:
                sp.wait_ge(hi_ready, i * RAW + (slot - 1))
                sp.wait_ge(lo_ready, i * RAW + (slot - 1))
            sp.dma_start(w_raw[:, slot, :], weights_v[i, slot]).then_inc(raw_landed[slot], 16)

        weights_v = weights.rearrange("(i j) p n -> i j p n", j=RAW)

        x_v = x_t.rearrange("(k p) t -> p k t", p=P)

        def x_load(i):
            sp.dma_start(x_raw[:, 2 * i:2 * i + 2, :], x_v[:, 2 * i:2 * i + 2, :]).then_inc(x_landed[i], 16)

        sp.dma_start(par[:, :], params).then_inc(par_landed, 16)
        raw_load(0, 0, False)
        x_load(0)
        raw_load(0, 1, False)
        for i in range(1, 5):
            x_load(i)
        sp.dma_start(con[:, :, :], consts).then_inc(con_landed, 16)
        raw_load(1, 0, True)
        x_load(5)
        raw_load(1, 1, True)
        x_load(6)
        x_load(7)
        sp.dma_start(oneh[0:BUCKETS, :], onehot).then_inc(rel_landed, 16)
        sp.dma_start(relb[0:BUCKETS, :], rel_bias).then_inc(rel_landed, 16)
        sp.dma_start(gym[0:HEADS, :], gy_mask).then_inc(rel_landed, 16)
        sp.dma_start(gate_w[:, :, :], w_gates[0]).then_inc(gate_landed, 16)
        with sp.Fori(2, SLABS // RAW) as i:
            for j in range(RAW):
                raw_load(i, j, True)

        for m in range(KT):
            sp.wait_ge(y_ready, m + 1)
            sp.dma_start(y_t[m], h_res[:, m, META:T]).then_inc(stored, 16)
        sp.wait_ge(stored, 16 * (2 + KT + 3))

    @block.tensor
    def _(pe):
        def products(slot, k, buf, hi, lo, kk, first, last, meta=False):
            c0, width = (0, HALF) if meta else (META, HA)
            wh, wl = w_hi[:, slot, k, :], w_lo[:, slot, k, :]
            for part, (w, act) in enumerate(((wh, hi), (wh, lo), (wl, hi))):
                for half in range(2):
                    ins = nc.tensor.matmul(ps[:, 2 * buf + half, 0:width], w,
                                           act[:, kk, c0 + half * width:c0 + (half + 1) * width],
                                           start=first and part == 0, stop=last and part == 2)
            return ins

        def slab(s, slot, buf, hi, lo, k0, first, last, ready=None, meta=False):
            pe.wait_ge(hi_ready, s + 1)
            pe.wait_ge(lo_ready, s + 1)
            for k in range(SLAB_K):
                if ready is not None:
                    ready(k)
                ins = products(slot, k, buf, hi, lo, k0 + k, first and k == 0, last and k == SLAB_K - 1, meta)
            ins.then_inc(slab_used, 1)

        def group(g, s, slot, buf, hi, lo, ready=None, wait=True, meta=False):
            if wait:
                pe.wait_ge(group_out, g - 1)
            slab(s, slot, buf, hi, lo, 0, True, False, ready, meta)
            slab(s + 1, slot + 1, buf, hi, lo, 8, False, True, None if ready is None else (lambda k: ready(8 + k)), meta)

        def token_sums(*parts, meta=False):
            c0 = 0 if meta else META
            for t in range(NBLK):
                c = c0 + t * P if t < NBLK - 1 else T - P
                for j, part in enumerate(parts):
                    ins = nc.tensor.matmul(ps[:, 7, BANK - 8 + t:BANK - 7 + t], part[:, c:c + P], ones[:, 0:1],
                                           start=j == 0, stop=j == len(parts) - 1)
            ins.then_inc(sums_ready, 1)

        def spread(n, meta=False):
            rest = T - (0 if meta else META) - BANK
            pe.wait_ge(diag_ready, n + 1)
            nc.tensor.matmul(ps[:, 5, :], ones, diag[:, 0:BANK], start=True, stop=True)
            nc.tensor.matmul(ps[:, 6, 0:rest], ones, diag[:, BANK:BANK + rest], start=True, stop=True)\
                .then_inc(spread_ready, 1)

        def xready(k):
            pe.wait_ge(xhi_ready, k + 1)
            pe.wait_ge(xlo_ready, k + 1)

        def gates(n):
            pe.wait_ge(conv_ready, n + 1)
            pe.wait_ge(gate_landed, (n + 1) * 16)
            for gi in range(2):
                for half in range(2):
                    ins = nc.tensor.matmul(ps[:, 4 + 2 * gi + half, 0:LH], gate_w[:, gi, :],
                                           xc[:, half * LH:(half + 1) * LH], start=True, stop=True)
            ins.then_inc(gates_ready, 1)

        for k in range(KT):
            xready(k)
            if k == KT - 2:
                pe.wait_ge(con_landed, 16)
                pe.wait_ge(x_added, KT - X_POOL)
                pe.wait_ge(x_pool_summed, X_POOL)
                token_sums(acc, mlp_a, meta=True)
            for b in range(2):
                s = k // SLAB_K * 2 + b
                if k % SLAB_K == 0:
                    pe.wait_ge(hi_ready, s + 1)
                    pe.wait_ge(lo_ready, s + 1)
                ins = products(s, k % SLAB_K, b, act_hi, act_lo, k, k == 0, k == KT - 1, b == 0)
                if k % SLAB_K == SLAB_K - 1:
                    ins.then_inc(slab_used, 1)
        pe.wait_ge(rel_landed, 48)
        nc.tensor.matmul(ps[0:HEADS, 4, 0:GY], relb[0:BUCKETS, :], oneh[0:BUCKETS, :],
                         start=True, stop=True).then_inc(gy_ps_ready, 1)
        spread(0, meta=True)
        pe.wait_ge(group_out, 1)
        slab(4, 0, 0, act_hi, act_lo, 0, True, False, meta=True)
        pe.wait_ge(rb_ready, 1)
        pe.wait_ge(gy_ready, 1)
        gates(0)
        slab(5, 1, 0, act_hi, act_lo, 8, False, True, meta=True)
        group(3, 6, 2, 1, act_hi, act_lo)
        gates(1)
        with pe.Fori(2, NB) as n:
            group(n * 2, n * 4, 0, 0, act_hi, act_lo, meta=True)
            group(n * 2 + 1, n * 4 + 2, 2, 1, act_hi, act_lo)
            gates(n)
        with pe.Fori(0, KV) as j:
            group(j * 2 + 2 * NB, j * 4 + SLABS_REC, 0, 0, act_hi, act_lo, meta=True)
            group(j * 2 + 2 * NB + 1, j * 4 + SLABS_REC + 2, 2, 1, act_hi, act_lo, meta=True)
        pe.wait_ge(rec_added, NB)
        token_sums(acc)
        pe.wait_ge(group_out, 2 * NB + 2 * KV)
        pe.wait_ge(tanh_x, NB)
        for b in range(SEQ // P):
            for g in range(KV):
                i = b * KV + g
                nc.tensor.transpose(ps[:, 4 + i // 4, (i % 4) * P:(i % 4 + 1) * P],
                                    kv[:, KV + g, META + b * P:META + (b + 1) * P], ident)
        for g in range(KV):
            nc.tensor.transpose(ps[0:META, 6, g * P:(g + 1) * P], kv[:, KV + g, 0:META], ident)
        pe.wait_ge(var_ready, 2)
        for g in range(KV):
            ins = nc.tensor.transpose(ps[0:TS, 7, g * P:(g + 1) * P], kv[:, KV + g, TP:T], ident)
        ins.then_inc(vt_ready, 1)
        g0, s0 = 2 * NB + 2 * KV, SLABS_REC + 4 * KV
        pe.wait_ge(group_out, g0 - 1)
        slab(s0, 0, 0, act_hi, act_lo, 0, True, False)
        pe.wait_ge(v_copied, 3)
        spread(1)
        slab(s0 + 1, 1, 0, act_hi, act_lo, 8, False, True)
        group(g0 + 1, s0 + 2, 2, 1, act_hi, act_lo)
        with pe.Fori(KV + 1, KV + HEADS // 2 - 1) as j:
            group(j * 2 + 2 * NB, j * 4 + SLABS_REC, 0, 0, act_hi, act_lo)
            group(j * 2 + 2 * NB + 1, j * 4 + SLABS_REC + 2, 2, 1, act_hi, act_lo)

        def scores(u):
            kind, i, g = UNITS[u]
            b0 = 4 + 2 * (u % 2)
            if u >= 2:
                pe.wait_ge(negmax_ready, u - 1)
            if kind == "prompt":
                k0, nk, _ = keys_of(i)
                for h in range(GQ):
                    ins = nc.tensor.matmul(ps[:, b0 + h // 2, (h % 2) * 2 * P:(h % 2) * 2 * P + nk],
                                           q[:, g * GQ + h, META + i * P:META + (i + 1) * P], kv[:, g, k0:k0 + nk],
                                           start=True, stop=True)
            else:
                nc.tensor.matmul(ps[:, b0, P:P + TS], q_s[:, g, i * P:(i + 1) * P], kv[:, g, TP:T],
                                 start=True, stop=True)
                for b in range(4):
                    ins = nc.tensor.matmul(ps[32 * b:32 * b + 32, b0, 0:P],
                                           q_s[:, g, i * P + 32 * b:i * P + 32 * b + 32],
                                           ck[:, 4 * i + b, g, :], start=True, stop=True)
            ins.then_inc(s_ready, 1)

        def turned(u):
            kind, i, g = UNITS[u]
            pe.wait_ge(probs_ready, u + 1)
            if u >= 1:
                pe.wait_ge(pt_copied, u)
            if kind == "prompt":
                for kb, (_, rows, c) in enumerate(keys_of(i)[2]):
                    for h in range(GQ):
                        ins = nc.tensor.transpose(ps[0:rows, kb, h * P:(h + 1) * P],
                                                  probs[u % 3][:, h, c:c + rows], ident)
            else:
                nc.tensor.transpose(ps[:, 0, 0:P], probs[u % 3][:, 0, 0:P], ident)
                ins = nc.tensor.transpose(ps[0:TS, 1, 0:P], probs[u % 3][:, 0, P:P + TS], ident)
            ins.then_inc(pt_ready, 1)

        def weighted(u):
            kind, i, g = UNITS[u]
            ob = 2 + u % 2
            pe.wait_ge(pt_copied, u + 1)
            if u >= 2:
                pe.wait_ge(o_copied, u - 1)
            if kind == "prompt":
                for kb, (vb, rows, _) in enumerate(keys_of(i)[2]):
                    ins = nc.tensor.matmul(ps[:, ob, 0:GQ * P], v_tok[0:rows, vb, g, :],
                                           probs_t[0:rows, kb, :, :], start=kb == 0, stop=kb == 1)
            else:
                nc.tensor.matmul(ps[:, ob, 0:P], v_tok[0:TS, 5, g, :], probs_t[0:TS, 1, 0, :],
                                 start=True, stop=False, skip_group_check=True)
                for b in range(4):
                    ins = nc.tensor.matmul(ps[:, ob, 32 * b:32 * b + 32], cv[:, 4 * i + b, g, :],
                                           probs_t[:, 0, 0, 32 * b:32 * b + 32],
                                           start=False, stop=b == 3, skip_group_check=True)
            ins.then_inc(o_ready, 1)

        group(G_OUT - 2, SLABS_IN - 4, 0, 0, act_hi, act_lo)
        pe.wait_ge(rb_ready, 2)
        scores(0)
        pe.wait_ge(group_out, G_OUT - 2)
        slab(SLABS_IN - 2, 2, 1, act_hi, act_lo, 0, True, False)
        scores(1)
        slab(SLABS_IN - 1, 3, 1, act_hi, act_lo, 8, False, True)
        scores(2)
        pe.wait_ge(group_out, G_OUT - 1)
        for u in range(NU):
            turned(u)
            if u == 0:
                pe.wait_ge(group_out, G_OUT)
            if u + 3 == NU_PROMPT:
                pe.wait_ge(qs_ready, KV)
                pe.wait_ge(cache_landed, 32)
            if u + 3 < NU:
                scores(u + 3)
            weighted(u)

        def rec_ready_k(k):
            pe.wait_ge(xhi_ready, KT + k + 1)
            pe.wait_ge(xlo_ready, KT + k + 1)

        def att_ready_k(k):
            pe.wait_ge(xhi_ready, KT + 8 + k + 1)
            pe.wait_ge(xlo_ready, KT + 8 + k + 1)

        pe.wait_ge(pt_copied, NU)
        slab(S_OUT, 0, 0, act_hi, act_lo, 8, True, False, rec_ready_k)
        pe.wait_ge(o_added, NU)
        token_sums(acc)
        pe.wait_ge(o_copied, NU)
        slab(S_OUT + 1, 1, 1, act_hi, act_lo, 8, True, False, lambda k: spread(2) if k == 4 else None)
        slab(S_OUT + 2, 2, 0, act_hi, act_lo, 0, False, True, att_ready_k)
        slab(S_OUT + 3, 3, 1, act_hi, act_lo, 0, False, True)
        with pe.Fori(1, KT // 2) as j:
            for b in range(2):
                pe.wait_ge(group_out, j * 2 + G_OUT + b - 1)
                slab(j * 4 + S_OUT + 2 * b, 2 * b, b, act_hi, act_lo, 8, True, False)
                slab(j * 4 + S_OUT + 2 * b + 1, 2 * b + 1, b, act_hi, act_lo, 0, False, True)

        def hready(k):
            pe.wait_ge(xhi_ready, 2 * KT + k + 1)
            pe.wait_ge(xlo_ready, 2 * KT + k + 1)

        def up_pair(g, s):
            group(g, s, 0, 0, act_hi, act_lo)
            group(g + 1, s + 2, 2, 1, act_hi, act_lo)

        def down_four(g, s, ready=None):
            for b in range(4):
                pe.wait_ge(group_out, g + b - 1)
                slab(s + b, b, b % 2, hid_hi, hid_lo, 0, True, True, ready if b == 0 else None)

        def chunk(c, first):
            if first:
                group(G_MLP, S_MLP, 0, 0, act_hi, act_lo, ready=hready)
                pe.wait_ge(h_added, KT)
                token_sums(acc)
                pe.wait_ge(group_out, G_MLP)
                slab(S_MLP + 2, 2, 1, act_hi, act_lo, 0, True, False)
                spread(3)
                slab(S_MLP + 3, 3, 1, act_hi, act_lo, 8, False, True)
            with pe.Fori(1 if first else 0, FC // 2) as f:
                up_pair(c * G_CHUNK + f * 2 + G_MLP, c * SLABS_CHUNK + f * 4 + S_MLP)
            g1, s1 = c * G_CHUNK + (G_MLP + FC), c * SLABS_CHUNK + (S_MLP + 2 * FC)
            down_four(g1, s1, lambda k: pe.wait_ge(hid_ready, c * FC + k + 1))
            with pe.Fori(1, KT // 4) as m:
                down_four(g1 + m * 4, s1 + m * 4)

        chunk(0, True)
        with pe.Fori(1, CHUNKS) as c:
            chunk(c, False)
        pe.wait_ge(h_added, 2 * KT)
        token_sums(acc)
        spread(4)

    @block.scalar
    def _(act):
        step = Steps(act, act_step)

        def w_high(s, slot, free=True):
            act.wait_ge(raw_landed[slot % RAW], s * 8 + (16 - 8 * (slot % RAW)))
            if free:
                act.wait_ge(slab_used, s - (RING - 1))
            nc.scalar.activation(w_hi[:, slot, :, :], w_raw[:, slot % RAW, :].rearrange("p (k n) -> p k n", k=SLAB_K),
                                 ACT.Copy).then_inc(hi_ready, 1)

        def root(n):
            act.wait_ge(var_ready, n + 1)
            nc.scalar.activation(nrm[:, 0, :], nrm[:, 1, :], ACT.Sqrt).then_inc(root_ready, 1)

        act.wait_ge(sp_exp, 1)
        nc.scalar.activation(spt[:, 1, :], spt[:, 0, :], ACT.Exp).then_inc(sp_exp, 1)
        w_high(0, 0, False)
        for k in range(KT):
            if k % 2 == 0:
                act.wait_ge(x_landed[k // 2], 16)
            nc.scalar.activation(act_hi[:, k, :], x_raw[:, k, :], ACT.Copy, scale=col("g_mix", k))\
                .then_inc(xhi_ready, 1)
            if k in (0, 6, 9):
                w_high({0: 1, 6: 2, 9: 3}[k], {0: 1, 6: 2, 9: 3}[k], False)
            if k >= X_POOL:
                j = k - X_POOL
                if j >= 2:
                    act.wait_ge(x_added, j - 1)
                nc.scalar.activation(sq[:, j % 2, :], x_raw[:, k, :], ACT.Square).then_inc(x_squared, 1)
        root(0)
        act.wait_ge(gy_ready, 1)
        act.dma_start(gy_dram.ap(), gy[0:HEADS, :].rearrange("h (o y) -> h o y", o=1).to_broadcast([HEADS, P, GY])).then_inc(gy_stored, 16)

        def tap0(n):
            act.wait_ge(group_out, n * 2 + 1)
            act.wait_ge(hist_ready, n + 1)
            nc.scalar.activation(xc[:, :], xp[:, 0:LT], ACT.Identity, bias=dcol("conv_b", n),
                                 scale=dcol("conv_w", n)).then_inc(tap0_ready, 1)

        def square_rec(n):
            act.wait_ge(rec_ready, n + 1)
            act.wait_ge(rec_added, n)
            nc.scalar.activation(sq[:, 0, META:T], live_at(rec_f, n), ACT.Square).then_inc(rec_squared, 1)

        def gelu_and_gates(n):
            act.wait_ge(group_out, n * 2 + 2)
            nc.scalar.activation(gel_t[:, :], gel[:, :], ACT.Square, scale=GELU_K).then_inc(g_squared, 1)
            act.wait_ge(g_poly, n + 1)
            nc.scalar.activation(gel_t[:, :], gel_t[:, :], ACT.Tanh, scale=GELU_C).then_inc(g_tanh, 1)

        def gates(n):
            act.wait_ge(gates_ready, n + 1)
            nc.scalar.activation(t_a[:, :].rearrange("p (h n) -> p h n", h=2), ps[:, 4:6, 0:LH], ACT.Tanh,
                                 bias=half_b[:, 0, bass.ds(n, 1)], scale=0.5).then_inc(tanh_a, 1)
            nc.scalar.activation(t_x[:, :].rearrange("p (h n) -> p h n", h=2), ps[:, 6:8, 0:LH], ACT.Tanh,
                                 bias=half_b[:, 1, bass.ds(n, 1)], scale=0.5).then_inc(tanh_x, 1)
            act.wait_ge(tanh_a, n + 1)
            nc.scalar.activation(t_a[:, :], t_a[:, :], ACT.Tanh, bias=sp2[:, bass.ds(n, 1)],
                                 scale=sp2[:, bass.ds(n, 1)]).then_inc(tau_ready, 1)
            act.wait_ge(tau_ready, n + 1)
            nc.scalar.activation(t_s[:, :], t_a[:, :], ACT.Sqrt).then_inc(sqrt_ready, 1)

        with act.Fori(0, NB) as n:
            s = n * 4
            act.wait_ge(sp_ready, 1)

            def high(i):
                w_high(s + i, i % RING)
            high(4)
            high(5)
            tap0(n)
            high(6)
            gelu_and_gates(n)
            high(7)
            gates(n)
            act.dma_start(gate_w[:, :, :], w_gates[n + 1]).then_inc(gate_landed, 16)
            square_rec(n)

        with act.Fori(SLABS_REC // 4, SLABS_REC // 4 + KV) as j:
            for i in range(4):
                w_high(j * 4 + 4 + i, i)
        root(1)
        act.wait_ge(vt_ready, 1)
        nc.scalar.activation(v_tok[:, 1:5, :, :].rearrange("p b g d -> p (b g d)").rearrange("p (c n) -> p c n", c=2),
                             ps[:, 4:6, :], ACT.Copy).then_inc(v_copied, 1)
        nc.scalar.activation(v_tok[0:META, 0, :, :], ps[0:META, 6, 0:KV * P].rearrange("p (g d) -> p g d", g=KV),
                             ACT.Copy).then_inc(v_copied, 1)
        nc.scalar.activation(v_tok[0:TS, 5, :, :], ps[0:TS, 7, 0:KV * P].rearrange("p (g d) -> p g d", g=KV),
                             ACT.Copy).then_inc(v_copied, 1)
        act.dma_start(keep_k, cache_k_rows).then_inc(stored, 16)
        act.dma_start(keep_v, cache_v_rows).then_inc(stored, 16)
        act.wait_ge(xr_kept, NB)
        act.dma_start(conv_o, conv_out[:, :, :, :]).then_inc(stored, 16)
        act.wait_ge(rec_ready, NB)
        act.dma_start(lru_o, lru_out[:, :, :]).then_inc(stored, 16)
        act.dma_start(kv_t, kv[:, :, TP - WINDOW:T]).then_inc(stored, 16)
        act.wait_ge(gy_stored, 16)
        act.dma_start(bias_p[:, :, :], bass.AP(gy_dram, P - 1, [[GY - 1, P], [P * GY, HEADS], [1, 2 * P]]))\
            .then_inc(bias_landed, 16)
        act.wait_ge(pads_ready, 1)
        for g in range(KV):
            for b in range(4):
                for i in range(2):
                    act.dma_start(bias_s[32 * b:32 * b + 32, i, g, 0:P],
                                  bass.AP(gy_dram, g * GQ * P * GY + P - 1, [[P * GY, GQ], [GY - 1, DEC_T], [1, P]]))\
                        .then_inc(bias_landed, 16)
                    act.dma_start(bias_s[32 * b:32 * b + 32, i, g, P + DEC_T * (4 * i + b):P + DEC_T * (4 * i + b + 1)],
                                  bass.AP(gy_dram, g * GQ * P * GY + 2 * P - 1, [[P * GY, GQ], [GY - 1, DEC_T], [1, DEC_T]]))\
                        .then_inc(bias_landed, 16)
        with act.Fori(SLABS_REC // 4 + KV, SLABS_IN // 4 - 1) as j:
            for i in range(4):
                w_high(j * 4 + 4 + i, i)

        def exps(u):
            kind, i, g = UNITS[u]
            act.wait_ge(negmax_ready, u + 1)
            if kind == "prompt":
                nk = keys_of(i)[1]
                nc.scalar.activation(stat[:, u % 3, 4, :], stat[:, u % 3, 2, :], ACT.Exp).then_inc(act_step, 1)
                for h in range(GQ):
                    ins = nc.scalar.activation(probs[u % 3][:, h, 0:nk], probs[u % 3][:, h, 0:nk], ACT.Exp,
                                               bias=stat[:, u % 3, 1, h:h + 1], accum_out=stat[:, u % 3, 3, h:h + 1])
                    if h < GQ - 1:
                        ins.then_inc(act_step, 1)
            else:
                nc.scalar.activation(stat[:, u % 3, 4, 0:1], stat[:, u % 3, 2, 0:1], ACT.Exp).then_inc(act_step, 1)
                ins = nc.scalar.activation(probs[u % 3][:, 0, 0:P + TS], probs[u % 3][:, 0, 0:P + TS], ACT.Exp,
                                           bias=stat[:, u % 3, 1, 0:1], accum_out=stat[:, u % 3, 3, 0:1])
            ins.then_inc(exp_ready, 1)

        def pt_copy(u):
            kind, i, g = UNITS[u]
            act.wait_ge(pt_ready, u + 1)
            if u >= 1:
                act.wait_ge(o_ready, u)
            if kind == "prompt" and i > 0:
                nc.scalar.activation(probs_t[:, :, :, :], ps[:, 0:2, :].rearrange("p c (h n) -> p c h n", h=GQ),
                                     ACT.Copy).then_inc(pt_copied, 1)
            elif kind == "prompt":
                nc.scalar.activation(probs_t[0:META, 0, :, :], ps[0:META, 0, :].rearrange("p (h n) -> p h n", h=GQ),
                                     ACT.Copy).then_inc(act_step, 1)
                nc.scalar.activation(probs_t[:, 1, :, :], ps[:, 1, :].rearrange("p (h n) -> p h n", h=GQ),
                                     ACT.Copy).then_inc(pt_copied, 1)
            else:
                nc.scalar.activation(probs_t[:, 0, 0, :], ps[:, 0, 0:P], ACT.Copy).then_inc(act_step, 1)
                nc.scalar.activation(probs_t[0:TS, 1, 0, :], ps[0:TS, 1, 0:P], ACT.Copy).then_inc(pt_copied, 1)

        w_high(SLABS_IN, 0)
        w_high(SLABS_IN + 1, 1)
        exps(0)
        w_high(SLABS_IN + 2, 2)
        exps(1)
        w_high(SLABS_IN + 3, 3)
        act.dma_start(ck[:, :, :, :], cache_kt).then_inc(cache_landed, 16)
        act.dma_start(cv[:, :, :, :], cache_v).then_inc(cache_landed, 16)
        act.wait_ge(rec_scaled, NB)
        for u in range(NU + 1):
            if 2 <= u < NU:
                exps(u)
            if u < NB:
                nc.scalar.activation(act_hi[:, 8 + u, META:T], rec[:, u, META:T], ACT.Copy).then_inc(xhi_ready, 1)
            if u >= 1:
                pt_copy(u - 1)
        act.wait_ge(s_ready, NU)
        act.wait_ge(o_ready, NU)
        act.wait_ge(negmax_ready, NU)
        act.wait_ge(stored, 16 * 5)
        x_v = x_t.rearrange("(k p) t -> p k t", p=P)
        for i in range(4):
            act.dma_start(h_res[:, 4 * i:4 * i + 4, META:T], x_v[:, 4 * i:4 * i + 4, META:T]).then_inc(h_landed[i], 16)
        root(2)
        for k in range(HEADS):
            act.wait_ge(att_scaled, k + 1)
            nc.scalar.activation(act_hi[:, k, META:T], q[:, k, META:T], ACT.Copy).then_inc(xhi_ready, 1)

        def high_and_square(j):
            for b in range(2):
                w_high(j * 4 + S_OUT + 4 + 2 * b, 2 * b)
                w_high(j * 4 + S_OUT + 4 + 2 * b + 1, 2 * b + 1)
                act.wait_ge(group_out, j * 2 + G_OUT + b + 1)
                if isinstance(j, int) and j == 0:
                    nc.scalar.activation(sq[:, b, META:T], h_res[:, b, META:T], ACT.Square).then_inc(h_squared, 1)
                else:
                    act.wait_ge(h_added, j * 2 + b - 1)
                    nc.scalar.activation(sq[:, b, META:T], live_at(h_f, j * 2 + b), ACT.Square)\
                        .then_inc(h_squared, 1)

        high_and_square(0)
        with act.Fori(1, KT // 2) as j:
            high_and_square(j)
        for k in range(KT):
            nc.scalar.activation(act_hi[:, k, META:T], h_res[:, k, META:T], ACT.Copy, scale=col("g_mlp", k)).then_inc(xhi_ready, 1)
        root(3)

        def square_hid(g):
            act.wait_ge(group_out, g + 1)
            nc.scalar.activation(mlp_b[:, META:T], mlp_a[:, META:T], ACT.Square).then_inc(square_ready, 1)

        def chunk(c, last):
            s = c * SLABS_CHUNK + S_MLP
            with act.Fori(0, FC // 2) as f:
                for b in range(2):
                    w_high(s + f * 4 + 4 + 2 * b, 2 * b)
                    w_high(s + f * 4 + 4 + 2 * b + 1, 2 * b + 1)
                    square_hid(c * G_CHUNK + f * 2 + (G_MLP + b))
            if not last:
                with act.Fori(0, KT // 4) as m:
                    for b in range(4):
                        w_high(s + m * 4 + 2 * FC + 4 + b, b)
            else:
                for m in range(KT):
                    if m + 4 < KT:
                        w_high(SLABS - KT + m + 4, m % 4)
                    act.wait_ge(group_out, G_MLP + CHUNKS * G_CHUNK - KT + m + 1)
                    act.wait_ge(h_added, KT + m - 1)
                    nc.scalar.activation(sq[:, m % 2, META:T], h_res[:, m, META:T], ACT.Square).then_inc(h_squared, 1)

        with act.Fori(0, CHUNKS - 1) as c:
            chunk(c, False)
        chunk(CHUNKS - 1, True)
        root(4)

    @block.gpsimd
    def _(pool):
        step = Steps(pool, pool_step)

        def w_low(s, slot, free=True):
            pool.wait_ge(raw_landed[slot % RAW], s * 8 + (16 - 8 * (slot % RAW)))
            pool.wait_ge(hi_ready, s + 1)
            if free:
                pool.wait_ge(slab_used, s - (RING - 1))
            nc.gpsimd.tensor_tensor(w_lo[:, slot, :, :], w_raw[:, slot % RAW, :].rearrange("p (k n) -> p k n", k=SLAB_K),
                                    w_hi[:, slot, :, :].bitcast(F32), ALU.subtract).then_inc(lo_ready, 1)

        pool.wait_ge(sp_atanh, 1)
        g = nc.gpsimd
        for d in (15, 13, 11, 9, 7, 5, 3, 1):
            step(g.tensor_tensor(spt[:, 0, :], spt[:, 0, :], spt[:, 3, :], ALU.mult))
            step(g.tensor_scalar(spt[:, 0, :], spt[:, 0, :], 1.0 / d, None, ALU.add))
        step(g.tensor_tensor(spt[:, 0, :], spt[:, 0, :], spt[:, 1, :], ALU.mult))
        step(g.tensor_scalar(spt[:, 0, :], spt[:, 0, :], 4.0, None, ALU.mult))
        g.tensor_tensor(sp2[:, :], spt[:, 0, :], spt[:, 2, :], ALU.add).then_inc(sp_ready, 1)

        def square_x(k):
            if k % 2 == 0:
                pool.wait_ge(x_landed[k // 2], 16)
            if k == 0:
                g.tensor_tensor(mlp_a[:, :], x_raw[:, k, :], x_raw[:, k, :], ALU.mult).then_inc(x_pool_summed, 1)
            else:
                pool.wait_ge(x_pool_summed, k)
                step(g.tensor_tensor(mlp_b[:, :], x_raw[:, k, :], x_raw[:, k, :], ALU.mult))
                g.tensor_tensor(mlp_a[:, :], mlp_a[:, :], mlp_b[:, :], ALU.add).then_inc(x_pool_summed, 1)

        pool.wait_ge(lo_ready, 1)
        w_low(1, 1, False)
        square_x(0)
        square_x(1)
        w_low(2, 2, False)
        w_low(3, 3, False)
        for k in range(2, X_POOL):
            square_x(k)

        def history(n):
            a = COL["hist"][0]
            nc.gpsimd.tensor_copy(sample(xp, S0)[:, :, 0:HIST],
                                  par[:, bass.ds(n * (DEC_B * HIST) + a, DEC_B * HIST)].rearrange(
                                      "p (b t) -> p b t", b=DEC_B)).then_inc(hist_ready, 1)

        pool.wait_ge(par_landed, 16)
        pool.wait_ge(x_squared, KT - X_POOL)
        pool.wait_ge(x_pool_summed, X_POOL)
        pool.wait_ge(xlo_ready, KT)
        step(nc.gpsimd.memset(xp[:, 0:HIST], 0.0))
        a = COL["hist"][0]
        nc.gpsimd.tensor_copy(sample(xp, S0)[:, :, 0:HIST],
                              par[:, a:a + DEC_B * HIST].rearrange("p (b t) -> p b t", b=DEC_B)).then_inc(hist_ready, 1)

        def kept(n):
            pool.wait_ge(conv_ready, n + 1)
            nc.gpsimd.tensor_copy(conv_f[:, bass.ds(n * 9 * HIST, HIST)], xp[:, TP:TP + HIST]).then_inc(pool_step, 1)
            nc.gpsimd.tensor_copy(conv_f[:, bass.ds(n * 9 * HIST + HIST, DEC_B * HIST)].rearrange("p (b t) -> p b t", b=DEC_B),
                                  sample(xp, S0)[:, :, DEC_T:SEQ_S]).then_inc(xr_kept, 1)
            pool.wait_ge(xr_kept, n + 1)

        def add_rec(n, first):
            pool.wait_ge(rec_squared, n + 1)
            if first:
                pool.wait_ge(sums_ready, 1)
                nc.gpsimd.tensor_copy(acc[:, META:T], sq[:, 0, META:T]).then_inc(rec_added, 1)
            else:
                pool.wait_ge(rec_added, n)
                nc.gpsimd.tensor_tensor(acc[:, META:T], acc[:, META:T], sq[:, 0, META:T], ALU.add).then_inc(rec_added, 1)

        def rec_block(n, first):
            for i in (4, 5):
                w_low(n * 4 + i, i % RING)
            kept(n)
            history(n + 1)
            for i in (6, 7):
                w_low(n * 4 + i, i % RING)
            add_rec(n, first)

        step.loop(step.k)
        pool_base = step.base
        rec_block(0, True)
        with pool.Fori(1, NB) as n:
            rec_block(n, False)

        with pool.Fori(SLABS_REC // 4, SLABS_REC // 4 + KV) as j:
            for i in range(4):
                w_low(j * 4 + 4 + i, i)
        pool.wait_ge(rec_ready, NB)
        pool.memset(bias_s[:, :, :, :], MASKED).then_inc(pads_ready, 1)
        with pool.Fori(SLABS_REC // 4 + KV, SLABS_IN // 4) as j:
            for i in range(4):
                w_low(j * 4 + 4 + i, i)

        pool.wait_ge(group_out, G_OUT)
        for g in range(KV):
            nc.gpsimd.tensor_copy(
                q_s[:, g, :].rearrange("p (b h t) -> p b h t", b=DEC_B, h=GQ),
                q[:, g * GQ:(g + 1) * GQ, TP:T].rearrange("p h (b t) -> p b h t", b=DEC_B)).then_inc(qs_ready, 1)
        step.loop(pool_base + NB)
        pool.wait_ge(sums_ready, 2)
        for u in range(NU):
            if u < NB:
                pool.wait_ge(xhi_ready, KT + u + 1)
                nc.gpsimd.tensor_tensor(act_lo[:, 8 + u, META:T], rec[:, u, META:T], act_hi[:, 8 + u, META:T].bitcast(F32),
                                        ALU.subtract).then_inc(xlo_ready, 1)
            kind, i, g = UNITS[u]
            pool.wait_ge(o_copied, u + 1)
            if kind == "prompt":
                c0, n = META + i * P, P
            else:
                c0, n = TP + 32 * i, 32
            o = q[:, g * GQ:(g + 1) * GQ, c0:c0 + n]
            s = sq[:, 0, 0:GQ * n].rearrange("p (h n) -> p h n", h=GQ)
            step(nc.gpsimd.tensor_tensor(s, o, o, ALU.mult))
            step(nc.gpsimd.tensor_tensor(s[:, 0:2, :], s[:, 0:2, :], s[:, 2:4, :], ALU.add))
            if g == 0:
                nc.gpsimd.tensor_tensor(acc[:, c0:c0 + n], s[:, 0, :], s[:, 1, :], ALU.add).then_inc(o_added, 1)
            else:
                step(nc.gpsimd.tensor_tensor(s[:, 0, :], s[:, 0, :], s[:, 1, :], ALU.add))
                nc.gpsimd.tensor_tensor(acc[:, c0:c0 + n], acc[:, c0:c0 + n], s[:, 0, :], ALU.add).then_inc(o_added, 1)
            pool.wait_ge(o_added, u + 1)

        def low_and_add(j):
            for b in range(2):
                w_low(j * 4 + S_OUT + 4 + 2 * b, 2 * b)
                w_low(j * 4 + S_OUT + 4 + 2 * b + 1, 2 * b + 1)
                pool.wait_ge(h_squared, j * 2 + b + 1)
                if isinstance(j, int) and b == 0:
                    pool.wait_ge(sums_ready, 3)
                    nc.gpsimd.tensor_copy(acc[:, META:T], sq[:, 0, META:T]).then_inc(h_added, 1)
                else:
                    pool.wait_ge(h_added, j * 2 + b)
                    nc.gpsimd.tensor_tensor(acc[:, META:T], acc[:, META:T], sq[:, b, META:T], ALU.add).then_inc(h_added, 1)

        low_and_add(0)
        with pool.Fori(1, KT // 2) as j:
            low_and_add(j)

        with pool.Fori(S_MLP // 4, (SLABS - KT) // 4) as j:
            for i in range(4):
                w_low(j * 4 + 4 + i, i)
        for m in range(KT):
            if m + 4 < KT:
                w_low(SLABS - KT + m + 4, m % 4)
            pool.wait_ge(h_squared, KT + m + 1)
            if m == 0:
                pool.wait_ge(sums_ready, 4)
                nc.gpsimd.tensor_copy(acc[:, META:T], sq[:, 0, META:T]).then_inc(h_added, 1)
            else:
                pool.wait_ge(h_added, KT + m)
                nc.gpsimd.tensor_tensor(acc[:, META:T], acc[:, META:T], sq[:, m % 2, META:T], ALU.add).then_inc(h_added, 1)

    @block.vector
    def _(dve):
        step = Steps(dve, dve_step)
        v = nc.vector

        def rsqrt(n, width, dst, meta=False):
            c0 = 0 if meta else META
            rest = T - c0 - BANK
            var, r, a = nrm[:, 1, :], nrm[:, 2, :], nrm[:, 3, :]
            dve.wait_ge(sums_ready, n + 1)
            v.tensor_scalar(var, ps[:, 7, BANK - 8:BANK - 8 + NBLK], 1.0 / width, EPS, ALU.mult, ALU.add)\
                .then_inc(var_ready, 1)
            dve.wait_ge(var_ready, n + 1)
            dve.wait_ge(root_ready, n + 1)
            step(v.reciprocal(r, nrm[:, 0, :]))
            step(v.scalar_tensor_tensor(a, var, -0.5, r, ALU.mult, ALU.mult))
            step(v.tensor_tensor(a, a, r, ALU.mult))
            step(v.scalar_tensor_tensor(r, a, 1.5, r, ALU.add, ALU.mult))
            v.tensor_tensor(diag[:, BANK:BANK + rest], ident[:, P - rest:P], r[:, NBLK - 1:NBLK].to_broadcast([P, rest]),
                            ALU.mult).then_inc(dve_step, 1)
            step.k += 1
            v.tensor_tensor(diag[:, 0:BANK].rearrange("p (b n) -> p b n", n=P),
                            ident.rearrange("p (o n) -> p o n", o=1).to_broadcast([P, NBLK - 1, P]),
                            r[:, 0:NBLK - 1].rearrange("p (b o) -> p b o", o=1).to_broadcast([P, NBLK - 1, P]),
                            ALU.mult).then_inc(diag_ready, 1)
            dve.wait_ge(spread_ready, n + 1)
            v.tensor_copy(dst[:, c0 + BANK:T], ps[:, 6, 0:rest]).then_inc(dve_step, 1)
            step.k += 1
            v.tensor_copy(dst[:, c0:c0 + BANK], ps[:, 5, :]).then_inc(rb_ready, 1)
            step.wait()
            dve.wait_ge(rb_ready, n + 1)

        dve.wait_ge(par_landed, 16)
        step(v.tensor_scalar(spt[:, 2, :], col("lam", 0, NB), -1.0, None, ALU.mult))
        v.tensor_tensor(spt[:, 0, :], col("lam", 0, NB), spt[:, 2, :], ALU.min).then_inc(sp_exp, 1)
        v.tensor_scalar(half_b[:, 0, :], col("b_a", 0, NB), 0.5, None, ALU.mult).then_inc(dve_step, 1)
        v.tensor_scalar(half_b[:, 1, :], col("b_x", 0, NB), 0.5, None, ALU.mult).then_inc(dve_step, 1)
        step.k += 2
        dve.wait_ge(sp_exp, 2)
        step(v.tensor_scalar(spt[:, 3, :], spt[:, 1, :], 2.0, None, ALU.add))
        step(v.reciprocal(spt[:, 3, :], spt[:, 3, :]))
        step(v.memset(spt[:, 0, :], 1.0 / 17.0))
        step(v.tensor_scalar(spt[:, 2, :], spt[:, 2, :], 0.0, 2.0, ALU.max, ALU.mult))
        step(v.tensor_tensor(spt[:, 1, :], spt[:, 1, :], spt[:, 3, :], ALU.mult))
        v.tensor_tensor(spt[:, 3, :], spt[:, 1, :], spt[:, 1, :], ALU.mult).then_inc(sp_atanh, 1)
        dve.wait_ge(hi_ready, 1)
        v.tensor_tensor(w_lo[:, 0, :, :], w_raw[:, 0, :].rearrange("p (k n) -> p k n", k=SLAB_K),
                        w_hi[:, 0, :, :].bitcast(F32), ALU.subtract).then_inc(lo_ready, 1)
        for k in range(KT):
            dve.wait_ge(xhi_ready, k + 1)
            v.scalar_tensor_tensor(act_lo[:, k, :], x_raw[:, k, :], col("g_mix", k), act_hi[:, k, :].bitcast(F32),
                                   ALU.mult, ALU.subtract).then_inc(xlo_ready, 1)
            j = k - X_POOL
            if j >= 0:
                dve.wait_ge(x_squared, j + 1)
            if j == 0:
                v.tensor_copy(acc[:, :], sq[:, 0, :]).then_inc(x_added, 1)
            elif j > 0:
                dve.wait_ge(x_added, j)
                v.tensor_tensor(acc[:, :], acc[:, :], sq[:, j % 2, :], ALU.add).then_inc(x_added, 1)
        rsqrt(0, D_MODEL, rb, True)
        dve.wait_ge(gy_ps_ready, 1)
        v.tensor_tensor(gy[0:HEADS, :], ps[0:HEADS, 4, 0:GY], gym[0:HEADS, :], ALU.add).then_inc(gy_ready, 1)

        STEPS_REC = 18
        first_base = step.k

        def rec_block(n):
            step.loop(n * STEPS_REC + first_base)
            dve.wait_ge(slab_used, n * 4 + 2)
            dve.wait_ge(hist_ready, n + 1)
            v.tensor_tensor(xp[:, HIST:HIST + HALF], ps[:, 0, 0:HALF], rb[:, 0:HALF], ALU.mult).then_inc(dve_step, 1)
            v.tensor_tensor(xp[:, HIST + HALF:HIST + TP], ps[:, 1, 0:TP - HALF], rb[:, HALF:TP], ALU.mult)\
                .then_inc(dve_step, 1)
            step.k += 2
            v.tensor_tensor(sample(xp, S0)[:, :, HIST:SEQ_S],
                            ps[:, 1, TP - HALF:HALF].rearrange("p (b t) -> p b t", b=DEC_B),
                            rb[:, TP:T].rearrange("p (b t) -> p b t", b=DEC_B), ALU.mult).then_inc(group_out, 1)
            dve.wait_ge(group_out, n * 2 + 1)
            dve.wait_ge(tap0_ready, n + 1)
            for j in range(1, CONV_W):
                ins = v.scalar_tensor_tensor(xc[:, :], xp[:, j:j + LT], dcol("conv_w", n + j * NB), xc[:, :],
                                             ALU.mult, ALU.add)
                if j < CONV_W - 1:
                    step(ins)
            ins.then_inc(conv_ready, 1)
            dve.wait_ge(slab_used, n * 4 + 4)
            v.tensor_tensor(halves(gel[:, :]), acc_pair(1), live(rb), ALU.mult).then_inc(group_out, 1)
            dve.wait_ge(g_squared, n + 1)
            v.scalar_tensor_tensor(gel_t[:, :], gel_t[:, :], 1.0, gel[:, :], ALU.add, ALU.mult).then_inc(g_poly, 1)
            dve.wait_ge(g_tanh, n + 1)
            step(v.scalar_tensor_tensor(gel[:, :], gel_t[:, :], 1.0, gel[:, :], ALU.add, ALU.mult))
            dve.wait_ge(tanh_x, n + 1)
            step(v.scalar_tensor_tensor(t_x[:, :], t_x[:, :], 1.0, xc[:, :], ALU.add, ALU.mult))
            dve.wait_ge(tau_ready, n + 1)
            step(v.tensor_scalar(t_r[:, :], t_a[:, :], 1.0, None, ALU.add))
            step(v.reciprocal(t_r[:, :], t_r[:, :]))
            dve.wait_ge(sqrt_ready, n + 1)
            step(v.tensor_scalar(t_a[:, :], t_r[:, :], 2.0, -1.0, ALU.mult, ALU.add))
            step(v.tensor_tensor(t_s[:, :], t_s[:, :], t_r[:, :], ALU.mult))
            step(v.memset(t_s[:, 0:1], 0.5))
            step(v.tensor_tensor(t_s[:, :], t_s[:, :], t_x[:, :], ALU.mult))
            pads = [sample(t, TP)[:, :, 0:HIST] for t in (t_a, t_s)]
            step(v.memset(pads[0], 0.0))
            step(v.tensor_copy(pads[1], par[:, bass.ds(n * (DEC_B * HIST) + COL["h0"][0], DEC_B * HIST)].rearrange(
                "p (b t) -> p b t", b=DEC_B)))
            step(v.tensor_tensor_scan(hs[:, :], t_a[:, :], t_s[:, :], 0.0, ALU.mult, ALU.add))
            v.tensor_copy(lru_f[:, bass.ds(n * 9, 1)], hs[:, TP - 1:TP]).then_inc(dve_step, 1)
            v.tensor_copy(lru_f[:, bass.ds(n * 9 + 1, DEC_B)], sample(hs, TP)[:, :, SEQ_S - 1]).then_inc(dve_step, 1)
            v.scalar_tensor_tensor(rec_f[:, bass.ds(n * T + META, SEQ)], gel[:, 0:SEQ], 0.5, hs[:, META:TP],
                                   ALU.mult, ALU.mult).then_inc(dve_step, 1)
            v.scalar_tensor_tensor(
                rec_f[:, bass.ds(n * T + TP, TS)].rearrange("p (b t) -> p b t", b=DEC_B),
                gel[:, SEQ:TA].rearrange("p (b t) -> p b t", b=DEC_B), 0.5,
                sample(hs, TP)[:, :, HIST:SEQ_S], ALU.mult, ALU.mult).then_inc(rec_ready, 1)
            step.k += 3
            dve.wait_ge(rec_ready, n + 1)
            assert step.k == STEPS_REC, step.k

        with dve.Fori(0, NB) as n:
            rec_block(n)
        step.base, step.k = first_base + NB * STEPS_REC, 0

        with dve.Fori(0, KV) as j:
            for b in range(2):
                dve.wait_ge(slab_used, j * 4 + SLABS_REC + 2 * b + 2)
                v.tensor_tensor(halves(kv_f[:, bass.ds((j * 2 + b) * T, T)]), acc_pair(b, HALF),
                                halves(rb[:, :]), ALU.mult).then_inc(group_out, 1)
        rsqrt(1, LRU_W, rn)
        with dve.Fori(0, NB) as n:
            tile = live_at(rec_f, n)
            v.scalar_tensor_tensor(tile, tile, dcol("g_rec", n), rn[:, META:T], ALU.mult, ALU.mult).then_inc(rec_scaled, 1)
        with dve.Fori(0, HEADS // 2 - 1) as j:
            for b in range(2):
                dve.wait_ge(slab_used, j * 4 + SLABS_REC + 4 * KV + 2 * b + 2)
                v.tensor_tensor(halves(live_at(q_f, j * 2 + b)), acc_pair(b), live(rb), ALU.mult).then_inc(group_out, 1)
        dve.wait_ge(slab_used, SLABS_IN - 2)
        v.tensor_tensor(live(q, HEADS - 2), acc_pair(0), live(rb), ALU.mult).then_inc(group_out, 1)

        def unit_rows(u):
            kind, i, g = UNITS[u]
            return (keys_of(i)[1], slice(0, GQ)) if kind == "prompt" else (P + TS, slice(0, 1))

        def front(u):
            kind, i, g = UNITS[u]
            nk, hs_ = unit_rows(u)
            b0 = 4 + 2 * (u % 2)
            dve.wait_ge(s_ready, u + 1)
            if u == 2:
                dve.wait_ge(slab_used, SLABS_IN)
            if u >= 3:
                dve.wait_ge(pt_ready, u - 2)
            st = stat[:, u % 3]
            if kind == "prompt":
                off = 2 * P - nk
                s_in = ps[:, b0:b0 + 2, :].rearrange("p c (h n) -> p (c h) n", h=2)[:, :, 0:nk]
                bias, sink = bias_p[:, g * GQ:(g + 1) * GQ, off:off + nk], col("sink_p", g * GQ, GQ)
                dst = probs[u % 3][:, :, 0:nk]
            else:
                s_in, bias, sink = ps[:, b0, 0:nk], bias_s[:, i, g, :], col("sink_s", g)
                dst = probs[u % 3][:, 0, 0:nk]
            step(v.scalar_tensor_tensor(dst, s_in, SCALE, bias, ALU.mult, ALU.add))
            step(v.tensor_reduce(st[:, 0, hs_], dst, AX.X, ALU.max))
            step(v.tensor_tensor(st[:, 0, hs_], st[:, 0, hs_], sink, ALU.max))
            v.tensor_scalar(st[:, 1, hs_], st[:, 0, hs_], -1.0, None, ALU.mult).then_inc(dve_step, 1)
            step.k += 1
            v.tensor_tensor(st[:, 2, hs_], sink, st[:, 0, hs_], ALU.subtract).then_inc(negmax_ready, 1)

        def norm(u):
            kind, i, g = UNITS[u]
            nk, hs_ = unit_rows(u)
            st = stat[:, u % 3]
            dve.wait_ge(exp_ready, u + 1)
            step(v.tensor_tensor(st[:, 5, hs_], st[:, 3, hs_], st[:, 4, hs_], ALU.add))
            step(v.reciprocal(st[:, 5, hs_], st[:, 5, hs_]))
            if kind == "prompt":
                p = probs[u % 3][:, :, 0:nk]
                r = st[:, 5, :].rearrange("p (h o) -> p h o", o=1).to_broadcast([P, GQ, nk])
                v.tensor_tensor(p, p, r, ALU.mult).then_inc(probs_ready, 1)
            else:
                p = probs[u % 3][:, 0, 0:nk]
                v.tensor_scalar(p, p, st[:, 5, 0:1], None, ALU.mult).then_inc(probs_ready, 1)

        def out(u):
            kind, i, g = UNITS[u]
            dve.wait_ge(o_ready, u + 1)
            if kind == "prompt":
                v.tensor_copy(q[:, g * GQ:(g + 1) * GQ, META + i * P:META + (i + 1) * P],
                              ps[:, 2 + u % 2, 0:GQ * P].rearrange("p (h n) -> p h n", h=GQ)).then_inc(o_copied, 1)
            else:
                c0 = TP + 32 * i
                v.tensor_copy(q[:, g * GQ:(g + 1) * GQ, c0:c0 + 32].rearrange("p h (b t) -> p b h t", b=4),
                              ps[:, 2 + u % 2, 0:P].rearrange("p (b h t) -> p b h t", b=4, h=GQ)).then_inc(o_copied, 1)

        dve.wait_ge(bias_landed, 16 * (1 + 4 * 2 * 2 * KV))
        for u in range(NU + 2):
            if u == 2:
                dve.wait_ge(slab_used, SLABS_IN)
                v.tensor_tensor(live(q, HEADS - 1), acc_pair(1), live(rb), ALU.mult).then_inc(group_out, 1)
            if u < NU:
                front(u)
            if 1 <= u <= NU:
                norm(u - 1)
            if u >= 2:
                if u == 2 + NU_PROMPT:
                    dve.wait_ge(qs_ready, KV)
                out(u - 2)

        rsqrt(2, LRU_W, rn)
        v.scalar_tensor_tensor(q[:, 0, META:T], q[:, 0, META:T], col("g_att", 0), rn[:, META:T], ALU.mult, ALU.mult).then_inc(att_scaled, 1)
        for k in range(HEADS):
            if k + 1 < HEADS:
                v.scalar_tensor_tensor(q[:, k + 1, META:T], q[:, k + 1, META:T], col("g_att", k + 1), rn[:, META:T], ALU.mult, ALU.mult)\
                    .then_inc(att_scaled, 1)
            dve.wait_ge(att_scaled, k + 1)
            dve.wait_ge(xhi_ready, KT + NB + k + 1)
            v.tensor_tensor(act_lo[:, k, META:T], q[:, k, META:T], act_hi[:, k, META:T].bitcast(F32), ALU.subtract).then_inc(xlo_ready, 1)

        for i in range(4):
            dve.wait_ge(h_landed[i], 16)
        for b in range(2):
            dve.wait_ge(slab_used, S_OUT + 3 + b)
            v.tensor_tensor(live(h_res, b), acc_pair(b), live(h_res, b), ALU.add).then_inc(group_out, 1)
        with dve.Fori(1, KT // 2) as j:
            for b in range(2):
                dve.wait_ge(slab_used, j * 4 + S_OUT + 2 * b + 2)
                tile = halves(live_at(h_f, j * 2 + b))
                v.tensor_tensor(tile, acc_pair(b), tile, ALU.add).then_inc(group_out, 1)
        for k in range(KT):
            dve.wait_ge(xhi_ready, 2 * KT + k + 1)
            v.scalar_tensor_tensor(act_lo[:, k, META:T], h_res[:, k, META:T], col("g_mlp", k), act_hi[:, k, META:T].bitcast(F32),
                                   ALU.mult, ALU.subtract).then_inc(xlo_ready, 1)
        rsqrt(3, D_MODEL, rb)

        def chunk(c):
            with dve.Fori(0, FC // 2) as f:
                for b in range(2):
                    dve.wait_ge(slab_used, c * SLABS_CHUNK + f * 4 + (S_MLP + 2 * b + 2))
                    v.scalar_tensor_tensor(live(mlp_a), acc_pair(b), 0.0, live(rb), ALU.max, ALU.mult)\
                        .then_inc(group_out, 1)
                    dve.wait_ge(square_ready, c * FC + f * 2 + b + 1)
                    hi, lo = live_at(hid_hi_f, f * 2 + b), live_at(hid_lo_f, f * 2 + b)
                    v.tensor_copy(hi, mlp_b[:, META:T]).then_inc(hid_split, 1)
                    dve.wait_ge(hid_split, c * FC + f * 2 + b + 1)
                    v.tensor_tensor(lo, mlp_b[:, META:T], hi.bitcast(F32), ALU.subtract).then_inc(hid_ready, 1)
            with dve.Fori(0, KT // 2) as m:
                for b in range(2):
                    dve.wait_ge(slab_used, c * SLABS_CHUNK + m * 2 + (S_MLP + 2 * FC + b + 1))
                    tile = halves(live_at(h_f, m * 2 + b))
                    v.tensor_tensor(tile, acc_pair(b), tile, ALU.add).then_inc(group_out, 1)

        with dve.Fori(0, CHUNKS) as c:
            chunk(c)
        rsqrt(4, D_MODEL, rb)
        for k in range(KT):
            v.scalar_tensor_tensor(h_res[:, k, META:T], h_res[:, k, META:T], col("g_fin", k), rb[:, META:T], ALU.mult, ALU.mult)\
                .then_inc(y_ready, 1)

    return ctx


def _rel_bucket(n):
    exact = BUCKETS // 2
    if n < exact:
        return n
    large = exact + int(np.float32(np.log(np.float32(n) / exact)) / np.float32(np.log(WINDOW / exact)) * (BUCKETS - exact))
    return min(large, BUCKETS - 1)


_IN = ["weights", "x_t", "params", "consts", "rel_bias", "onehot", "gy_mask", "w_gates", "cache_kt", "cache_v",
       "cache_k_rows", "cache_v_rows"]
_OUT = [("y_t", (KT, P, TA)), ("kv_t", (P, 2 * KV, WINDOW + TS)), ("conv_o", (P, NB, 9, HIST)), ("lru_o", (P, NB, 9)),
        ("keep_k", (DEC_B, WINDOW - DEC_T, KV * P)), ("keep_v", (DEC_B, WINDOW - DEC_T, KV * P))]


def kernel(x_prompt, x_sample, cache_k_win, cache_v_win, state_conv, state_lru, meta_tokens, norm_mix_g, w_in, conv_w,
           conv_b, w_gate_a, b_gate_a, w_gate_x, b_gate_x, lru_lambda, attn_sinks, rel_bias, attn_out_g, rec_out_g,
           w_out, norm_mlp_g, w_up, w_down, final_norm_g):
    import concourse.bacc as bacc
    from concourse.bass_utils import run_bass_kernel_spmd

    A = np.asarray
    c = np.ascontiguousarray

    def tiles(w):
        k, m = w.shape
        return w.reshape(k // P, P, m // P, P).transpose(0, 2, 1, 3)

    def slab_rows(t, ks, m):
        return t[ks, m].transpose(1, 0, 2).reshape(1, P, SLAB)

    w_i, w_o, w_u, w_d = (tiles(A(w)[0]) for w in (w_in, w_out, w_up, w_down))
    n_att = HEADS + 2 * KV
    lo8, hi8 = list(range(8)), list(range(8, 16))
    slabs = []
    order = [m for n in range(NB) for m in (n_att + n, n_att + NB + n)]
    order += list(range(HEADS, n_att)) + list(range(HEADS))
    slabs += [slab_rows(w_i, ks, m) for ks in (lo8, hi8) for m in order[:2]]
    for m in order[2:]:
        slabs += [slab_rows(w_i, lo8, m), slab_rows(w_i, hi8, m)]
    slabs += [slab_rows(w_o, hi8, 0), slab_rows(w_o, hi8, 1), slab_rows(w_o, lo8, 0), slab_rows(w_o, lo8, 1)]
    for m in range(2, KT):
        slabs += [slab_rows(w_o, hi8, m), slab_rows(w_o, lo8, m)]
    for ch in range(CHUNKS):
        for f in range(FC):
            slabs += [slab_rows(w_u, lo8, ch * FC + f), slab_rows(w_u, hi8, ch * FC + f)]
        for m in range(KT):
            slabs.append(slab_rows(w_d, list(range(ch * FC, ch * FC + FC)), m))
    weights = c(np.concatenate(slabs))
    assert weights.shape[0] == SLABS

    xs = A(x_sample).reshape(TS, D_MODEL)
    x_t = c(np.concatenate([A(meta_tokens), A(x_prompt)[0], xs]).T)

    def per_channel(a):
        a = A(a)
        a = a.reshape(-1, a.shape[-1] // P, P)
        return a.transpose(2, 0, 1).reshape(P, -1)

    h0 = np.zeros((P, NB, DEC_B, HIST), np.float32)
    h0[..., HIST - 1] = A(state_lru)[0].reshape(DEC_B, NB, P).transpose(2, 1, 0)
    hist = np.zeros((P, NB + 1, DEC_B, HIST), np.float32)
    hist[:, :NB] = A(state_conv)[0].reshape(DEC_B, HIST, NB, P).transpose(3, 2, 0, 1)
    sinks = A(attn_sinks)[0]
    sink_s = np.broadcast_to(sinks.reshape(1, KV, GQ, 1), (4, KV, GQ, DEC_T)).transpose(0, 2, 3, 1).reshape(P, KV)
    parts = {"g_mix": per_channel(norm_mix_g), "conv_w": per_channel(A(conv_w)[0]), "conv_b": per_channel(conv_b),
             "b_a": per_channel(b_gate_a), "b_x": per_channel(b_gate_x), "lam": per_channel(lru_lambda),
             "g_att": per_channel(attn_out_g), "g_rec": per_channel(rec_out_g), "g_mlp": per_channel(norm_mlp_g),
             "g_fin": per_channel(A(final_norm_g)[None]), "sink_p": np.broadcast_to(sinks, (P, HEADS)),
             "sink_s": sink_s, "h0": h0.reshape(P, -1), "hist": hist.reshape(P, -1)}
    params = c(np.concatenate([parts[n] for n, _ in _COLS], axis=1))

    onehot = np.zeros((BUCKETS, GY), np.float32)
    gy_mask = np.full((HEADS, GY), MASKED, np.float32)
    for y in range(GY):
        d = 2 * P - 1 - y
        if 0 <= d < WINDOW:
            onehot[_rel_bucket(d), y] = 1.0
            gy_mask[:, y] = 0.0
    consts = c(np.stack([np.eye(P, dtype=np.float32), np.ones((P, P), np.float32)], axis=1))
    gw = np.stack([A(w_gate_a)[0], A(w_gate_x)[0]], axis=2)
    w_gates = c(np.concatenate([gw, gw[:1]]))

    kc, vc = A(cache_k_win)[0], A(cache_v_win)[0]
    arrays = {
        "weights": weights, "x_t": x_t, "params": params, "consts": consts, "rel_bias": c(A(rel_bias)),
        "onehot": onehot, "gy_mask": gy_mask, "w_gates": w_gates,
        "cache_kt": c(kc.transpose(3, 0, 2, 1)), "cache_v": c(vc.transpose(1, 0, 2, 3)),
        "cache_k_rows": c(kc.reshape(DEC_B, WINDOW, KV * P)[:, DEC_T:]),
        "cache_v_rows": c(vc.reshape(DEC_B, WINDOW, KV * P)[:, DEC_T:]),
    }
    nc = bacc.Bacc("TRN2", target_bir_lowering=False, num_devices=1)
    args = [nc.dram_tensor(n, arrays[n].shape, F32, kind="ExternalInput").ap() for n in _IN]
    args += [nc.dram_tensor(n, s, F32, kind="ExternalOutput").ap() for n, s in _OUT]
    hymba_layer(nc, *args).close()
    r = run_bass_kernel_spmd(nc, [arrays], core_ids=[0]).results[0]

    y = r["y_t"].reshape(D_MODEL, TA).T
    y_prompt = c(y[:SEQ]).reshape(1, SEQ, D_MODEL)
    y_sample = c(y[SEQ:]).reshape(DEC_B, DEC_T, D_MODEL)
    kvw = r["kv_t"]

    def windows(t):
        return c(t[:, :, :WINDOW].transpose(2, 1, 0)).reshape(1, 1, WINDOW, KV, P),             t[:, :, WINDOW:].transpose(2, 1, 0).reshape(DEC_B, DEC_T, KV, P)

    kp, ks = windows(kvw[:, :KV])
    vp, vs = windows(kvw[:, KV:])
    new_k = np.concatenate([r["keep_k"].reshape(DEC_B, WINDOW - DEC_T, KV, P), ks], axis=1)[None]
    new_v = np.concatenate([r["keep_v"].reshape(DEC_B, WINDOW - DEC_T, KV, P), vs], axis=1)[None]
    conv = r["conv_o"].transpose(2, 3, 1, 0).reshape(9, HIST, LRU_W)
    lru = r["lru_o"].transpose(2, 1, 0).reshape(9, LRU_W)
    return (y_prompt, y_sample, kp, vp, c(conv[:1])[None], c(lru[:1])[None], c(new_k), c(new_v),
            c(conv[1:])[None], c(lru[1:])[None])
```
